# Optimizing a Trainium2 kernel written in Bass

```python
import jax, jax.numpy as jnp
from jax import lax
import numpy as np

D_MODEL = 1024
BATCH = 1
SEQ = 256
DEPTH = 2

ATT_HEADS = 8
ATT_HEAD_DIM = 64
ATT_WIDTH = ATT_HEADS * ATT_HEAD_DIM
MLSTM_HEADS = 4
MLSTM_HEAD_DIM = 128
MLSTM_WIDTH = MLSTM_HEADS * MLSTM_HEAD_DIM
CONV_WIDTH = 4
GMLP_GROUPS = 4
GMLP_GROUP_DIM = 128
GMLP_WIDTH = GMLP_GROUPS * GMLP_GROUP_DIM
CHUNK = 128
D_FF = 2816
FFN_RES = 0.5
N_BRANCH = 3
EPS = 1e-6

SPLITS = (3 * ATT_WIDTH, ATT_HEADS,
          2 * MLSTM_WIDTH, MLSTM_WIDTH, MLSTM_HEADS, MLSTM_HEADS, MLSTM_WIDTH,
          2 * GMLP_WIDTH, N_BRANCH * D_MODEL)
D_IN = 3 * ATT_WIDTH + ATT_HEADS + 3 * MLSTM_WIDTH + 2 * MLSTM_HEADS + MLSTM_WIDTH + 2 * GMLP_WIDTH + N_BRANCH * D_MODEL

kernel_name = 'hybrid_fox_mlstm_gmlp_macaron'

def rmsnorm(x, g):
    xf = x.astype(jnp.float32)
    y = xf * lax.rsqrt(jnp.mean(xf * xf, axis=-1, keepdims=True) + EPS)
    return (y * g.astype(jnp.float32)).astype(x.dtype)

def swiglu(h, w_gate, w_up, w_down):
    return (jax.nn.silu(h @ w_gate) * (h @ w_up)) @ w_down

def causal_depthwise_conv(x, w):
    return lax.conv_general_dilated(
        x, w[:, None, :].astype(x.dtype), window_strides=(1,),
        padding=[(CONV_WIDTH - 1, 0)], dimension_numbers=('NWC', 'WIO', 'NWC'),
        feature_group_count=x.shape[-1])

def forgetting_attention(q, k, v, f_pre):
    B, S, H, Dh = q.shape
    nblk = S // CHUNK
    logf = jax.nn.log_sigmoid(f_pre.astype(jnp.float32))
    c = jnp.transpose(jnp.cumsum(logf, axis=1), (0, 2, 1))
    q_blocks = q.reshape(B, nblk, CHUNK, H, Dh).transpose(1, 0, 3, 2, 4)
    c_blocks = c.reshape(B, H, nblk, CHUNK).transpose(2, 0, 1, 3)
    kpos = jnp.arange(S)
    scale = Dh ** -0.5

    def one_block(args):
        blk, qb, cb = args
        s = jnp.einsum('bhqd,bkhd->bhqk', qb, k, preferred_element_type=jnp.float32) * scale
        s = s + cb[..., :, None] - c[..., None, :]
        qpos = blk * CHUNK + jnp.arange(CHUNK)
        s = jnp.where(kpos[None, :] <= qpos[:, None], s, -jnp.inf)
        p = jax.nn.softmax(s, axis=-1)
        return jnp.einsum('bhqk,bkhd->bqhd', p.astype(v.dtype), v)

    out = lax.map(one_block, (jnp.arange(nblk), q_blocks, c_blocks))
    return out.transpose(1, 0, 2, 3, 4).reshape(B, S, H * Dh)

def mlstm_chunkwise(q, k, v, i_pre, f_pre):
    B, S, H, Dh = q.shape
    nc = S // CHUNK
    f32 = jnp.float32

    def to_chunks(a):
        a = a.astype(f32).reshape((B, nc, CHUNK, H) + a.shape[3:])
        return jnp.moveaxis(a, (1, 3), (0, 2))

    qc = to_chunks(q) * (Dh ** -0.5)
    kc = to_chunks(k)
    vc = to_chunks(v)
    lfc = to_chunks(jax.nn.log_sigmoid(f_pre.astype(f32)))
    lic = to_chunks(i_pre)
    causal = jnp.tril(jnp.ones((CHUNK, CHUNK), dtype=bool))

    def step(carry, inp):
        C, n, m = carry
        qb, kb, vb, lf, li = inp
        b = jnp.cumsum(lf, axis=-1)
        a = b + m[..., None]
        dmat = jnp.where(causal, b[..., :, None] - b[..., None, :] + li[..., None, :], -jnp.inf)
        m_t = jnp.maximum(a, jnp.max(dmat, axis=-1))
        w_intra = jnp.exp(dmat - m_t[..., None])
        w_inter = jnp.exp(a - m_t)
        qk = jnp.einsum('bhtd,bhsd->bhts', qb, kb) * w_intra
        num = jnp.einsum('bhts,bhsv->bhtv', qk, vb) + w_inter[..., None] * jnp.einsum('bhvd,bhtd->bhtv', C, qb)
        den = jnp.sum(qk, axis=-1) + w_inter * jnp.einsum('bhd,bhtd->bht', n, qb)
        h = num / jnp.maximum(jnp.abs(den), jnp.exp(-m_t))[..., None]
        bL = b[..., -1]
        g = bL[..., None] - b + li
        m_new = jnp.maximum(bL + m, jnp.max(g, axis=-1))
        w_s = jnp.exp(g - m_new[..., None])
        decay = jnp.exp(bL + m - m_new)
        C_new = decay[..., None, None] * C + jnp.einsum('bhs,bhsv,bhsd->bhvd', w_s, vb, kb)
        n_new = decay[..., None] * n + jnp.einsum('bhs,bhsd->bhd', w_s, kb)
        return (C_new, n_new, m_new), h

    init = (jnp.zeros((B, H, Dh, Dh), f32), jnp.zeros((B, H, Dh), f32), jnp.zeros((B, H), f32))
    _, hs = lax.scan(step, init, (qc, kc, vc, lfc, lic))
    return jnp.moveaxis(hs, (0, 2), (1, 3)).reshape(B, S, H, Dh)

def chunked_spatial_gating(u, v, w_s, b_s):
    B, S, _ = v.shape
    nc = S // CHUNK
    vc = v.reshape(B, nc, CHUNK, GMLP_GROUPS, GMLP_GROUP_DIM)
    w = jnp.where(jnp.tril(jnp.ones((CHUNK, CHUNK), dtype=bool)), w_s, 0.0).astype(v.dtype)
    mixed = jnp.einsum('gts,bcsgd->bctgd', w, vc) + b_s.T.astype(v.dtype)[None, None, :, :, None]
    return u * mixed.reshape(B, S, GMLP_WIDTH)

def token_mixer(h, w_in, b_f_att, b_i_ml, b_f_ml, conv_ml, norm_ml_head, norm_gmlp,
                w_spatial, b_spatial, w_br_att, w_br_ml, w_br_gmlp, w_out):
    B, S, _ = h.shape
    split_points = [int(p) for p in np.cumsum(SPLITS)[:-1]]
    proj = h @ w_in
    att_qkv, att_f, ml_qk, ml_v, ml_i, ml_f, ml_o, gm_uv, gates = jnp.split(proj, split_points, axis=-1)

    q_a, k_a, v_a = [t.reshape(B, S, ATT_HEADS, ATT_HEAD_DIM) for t in jnp.split(att_qkv, 3, axis=-1)]
    y_att = forgetting_attention(q_a, k_a, v_a, att_f + b_f_att)

    qk_m = jax.nn.silu(causal_depthwise_conv(ml_qk, conv_ml))
    q_m, k_m = [t.reshape(B, S, MLSTM_HEADS, MLSTM_HEAD_DIM) for t in jnp.split(qk_m, 2, axis=-1)]
    v_m = ml_v.reshape(B, S, MLSTM_HEADS, MLSTM_HEAD_DIM)
    h_m = mlstm_chunkwise(q_m, k_m, v_m, ml_i + b_i_ml, ml_f + b_f_ml)
    h_m = rmsnorm(h_m, norm_ml_head.reshape(MLSTM_HEADS, MLSTM_HEAD_DIM)).reshape(B, S, MLSTM_WIDTH)
    y_ml = jax.nn.sigmoid(ml_o) * h_m.astype(h.dtype)

    u_c, v_c = jnp.split(jax.nn.gelu(gm_uv), 2, axis=-1)
    y_gm = chunked_spatial_gating(u_c, rmsnorm(v_c, norm_gmlp), w_spatial, b_spatial)

    g = jax.nn.sigmoid(gates).reshape(B, S, N_BRANCH, D_MODEL)
    merged = (g[:, :, 0] * (y_att @ w_br_att)
              + g[:, :, 1] * (y_ml @ w_br_ml)
              + g[:, :, 2] * (y_gm @ w_br_gmlp))
    return merged @ w_out

def setup_inputs(seed: int = 0) -> dict:
    key = jax.random.key(seed)
    ks = jax.random.split(key, 25)
    f32 = jnp.float32

    def nrm(k, shape, scale):
        return jax.random.normal(k, shape, f32) * scale

    def gain(k, shape):
        return 1.0 + 0.02 * jax.random.normal(k, shape, f32)

    out_scale = (2 * DEPTH) ** -0.5
    return {
        'x': nrm(ks[0], (BATCH, SEQ, D_MODEL), 1.0),
        'norm_ffn1': gain(ks[1], (DEPTH, D_MODEL)),
        'ffn1_gate': nrm(ks[2], (DEPTH, D_MODEL, D_FF), D_MODEL ** -0.5),
        'ffn1_up': nrm(ks[3], (DEPTH, D_MODEL, D_FF), D_MODEL ** -0.5),
        'ffn1_down': nrm(ks[4], (DEPTH, D_FF, D_MODEL), D_FF ** -0.5 * out_scale),
        'norm_mix': gain(ks[5], (DEPTH, D_MODEL)),
        'w_in': nrm(ks[6], (DEPTH, D_MODEL, D_IN), D_MODEL ** -0.5),
        'b_f_att': jnp.linspace(1.0, 5.0, ATT_HEADS, dtype=f32)[None, :] + nrm(ks[7], (DEPTH, ATT_HEADS), 0.1),
        'b_i_ml': nrm(ks[8], (DEPTH, MLSTM_HEADS), 0.1),
        'b_f_ml': jnp.linspace(3.0, 6.0, MLSTM_HEADS, dtype=f32)[None, :] + nrm(ks[9], (DEPTH, MLSTM_HEADS), 0.1),
        'conv_ml': nrm(ks[10], (DEPTH, CONV_WIDTH, 2 * MLSTM_WIDTH), CONV_WIDTH ** -0.5),
        'norm_ml_head': gain(ks[11], (DEPTH, MLSTM_WIDTH)),
        'norm_gmlp': gain(ks[12], (DEPTH, GMLP_WIDTH)),
        'w_spatial': nrm(ks[13], (DEPTH, GMLP_GROUPS, CHUNK, CHUNK), CHUNK ** -0.5),
        'b_spatial': 1.0 + nrm(ks[14], (DEPTH, GMLP_GROUPS, CHUNK), 0.1),
        'w_br_att': nrm(ks[15], (DEPTH, ATT_WIDTH, D_MODEL), ATT_WIDTH ** -0.5),
        'w_br_ml': nrm(ks[16], (DEPTH, MLSTM_WIDTH, D_MODEL), MLSTM_WIDTH ** -0.5),
        'w_br_gmlp': nrm(ks[17], (DEPTH, GMLP_WIDTH, D_MODEL), GMLP_WIDTH ** -0.5),
        'w_out': nrm(ks[18], (DEPTH, D_MODEL, D_MODEL), D_MODEL ** -0.5 * out_scale),
        'norm_ffn2': gain(ks[19], (DEPTH, D_MODEL)),
        'ffn2_gate': nrm(ks[20], (DEPTH, D_MODEL, D_FF), D_MODEL ** -0.5),
        'ffn2_up': nrm(ks[21], (DEPTH, D_MODEL, D_FF), D_MODEL ** -0.5),
        'ffn2_down': nrm(ks[22], (DEPTH, D_FF, D_MODEL), D_FF ** -0.5 * out_scale),
        'norm_final': gain(ks[23], (D_MODEL,)),
    }

def reference(x, norm_ffn1, ffn1_gate, ffn1_up, ffn1_down, norm_mix, w_in, b_f_att, b_i_ml, b_f_ml,
              conv_ml, norm_ml_head, norm_gmlp, w_spatial, b_spatial, w_br_att, w_br_ml, w_br_gmlp,
              w_out, norm_ffn2, ffn2_gate, ffn2_up, ffn2_down, norm_final):
    for l in range(DEPTH):
        x = x + FFN_RES * swiglu(rmsnorm(x, norm_ffn1[l]), ffn1_gate[l], ffn1_up[l], ffn1_down[l])
        x = x + token_mixer(rmsnorm(x, norm_mix[l]), w_in[l], b_f_att[l], b_i_ml[l], b_f_ml[l],
                            conv_ml[l], norm_ml_head[l], norm_gmlp[l], w_spatial[l], b_spatial[l],
                            w_br_att[l], w_br_ml[l], w_br_gmlp[l], w_out[l])
        x = x + FFN_RES * swiglu(rmsnorm(x, norm_ffn2[l]), ffn2_gate[l], ffn2_up[l], ffn2_down[l])
    return rmsnorm(x, norm_final)


_drawn_inputs = setup_inputs


def setup_inputs(seed=0):
    import zlib

    import numpy as np

    out = dict(_drawn_inputs(seed))
    spreads = {}
    factors = {'norm_ffn1': 8.0,
     'norm_mix': 4.808,
     'b_i_ml': 64.0,
     'norm_ml_head': 64.0,
     'norm_gmlp': 27.357,
     'norm_ffn2': 8.0,
     'norm_final': 8.4,
     'b_spatial': 3.741}
    for name, (base, spread) in spreads.items():
        noise = np.random.default_rng([zlib.crc32(name.encode()), seed]).standard_normal(out[name].shape)
        drawn = base * np.exp(spread * noise) if base else spread * noise
        out[name] = __import__('jax').numpy.asarray(drawn.astype(out[name].dtype))
    for name, factor in factors.items():
        out[name] = (out[name] * factor).astype(out[name].dtype)
    return out
```

```python
from contextlib import ExitStack

import concourse.bass as bass
from concourse import mybir

F32 = mybir.dt.float32
F32R = mybir.dt.float32r
BF16 = mybir.dt.bfloat16
ALU = mybir.AluOpType
ACT = mybir.ActivationFunctionType
AX = mybir.AxisListType

P = 128
EPS = 1e-6
NEG = -1e30
RING = 3


class Chain:

    def __init__(self, engine, sem, layer, per_layer):
        self.engine, self.sem, self.n, self.per_layer = engine, sem, 0, per_layer
        self.base = layer * per_layer

    def __call__(self, instruction):
        instruction.then_inc(self.sem, 1)
        self.n += 1
        self.engine.wait_ge(self.sem, self.base + self.n)

    def end(self):
        assert self.n == self.per_layer, (self.n, self.per_layer)


def trunk(nc, x, norm_ffn1, ffn1_gate, ffn1_up, ffn1_down, norm_mix, w_in, b_f_att, b_i_ml, b_f_ml,
          conv_ml, norm_ml_head, norm_gmlp, w_spatial, b_spatial, w_br_att, w_br_ml, w_br_gmlp,
          w_out, norm_ffn2, ffn2_gate, ffn2_up, ffn2_down, norm_final, out):
    DEPTH, D, DFF = ffn1_gate.shape
    S = x.shape[1]
    NT = S // P
    KD = D // P
    AH = b_f_att.shape[1]
    MH = b_i_ml.shape[1]
    AW, MW = w_br_att.shape[1], w_br_ml.shape[1]
    DH = AW // AH
    NTAP = conv_ml.shape[1]
    CB = 512
    WB = 256
    NB = DFF // WB
    NGATE = 3 * D // CB
    SMALL = AH + 2 * MH
    GROUP = 3 * CB + AH
    assert NT == 2 and KD == 8 and AW == MW == CB and AH == 2 * MH and DH == 64 and GROUP == 3 * CB + 2 * MH

    FFN_UNITS = 3 * NB
    U_WI = FFN_UNITS
    U_SMALL = U_WI + 18
    U_GATE = U_SMALL + 2
    U_BR = U_GATE + 2 * NGATE
    U_OUT = U_BR + 6
    U_FFN2 = U_OUT + 4
    UNITS = U_FFN2 + FFN_UNITS
    assert UNITS % RING == 0 and FFN_UNITS % RING == 0 and U_FFN2 % RING == 0
    ATT_SCALE = DH ** -0.5
    ML_SCALE = float(P) ** -0.5
    TURN_BANKS, MERGED_BANKS = (4, 6), (2, 4)
    PROWS = 2 * MH + NTAP * KD

    with ExitStack() as ctx:
        def sb(name, shape, dt=F32):
            return ctx.enter_context(nc.sbuf_tensor(name, shape, dt))

        def sem(name):
            return ctx.enter_context(nc.semaphore(name))

        ps = ctx.enter_context(nc.psum_tensor("ps", [P, 8, 512], F32))

        xs = sb("xs", [P, NT, D])
        xT_hi = sb("xT_hi", [P, KD, S], F32R)
        xT_lo = sb("xT_lo", [P, KD, S], F32R)
        w_raw = sb("w_raw", [P, RING, 2048])
        w_hi = sb("w_hi", [P, RING, 2048], F32R)
        w_lo = sb("w_lo", [P, RING, 2048], F32R)
        featT = sb("featT", [P, 6, 4, S])
        tokv = sb("tokv", [P, 3, NT, CB])
        gates = sb("gates", [P, NGATE, NT, CB])
        yT_hi = sb("yT_hi", [P, 3, 4, S], F32R)
        yT_lo = sb("yT_lo", [P, 3, 4, S], F32R)
        gain = sb("gain", [P, D])
        scr = sb("scr", [P, 3584])
        z_rows = sb("z_rows", [P, S])
        ls_rows = sb("ls_rows", [P, S])
        negc = sb("negc", [P, S])
        b_row = sb("b_row", [P, S])
        g_row = sb("g_row", [P, S])
        negm = sb("negm", [P, S])
        r_row = sb("r_row", [P, 2 * S])
        head_sel = sb("head_sel", [P, AH, P])
        bsp = sb("bsp", [P, DEPTH * 4, P])
        wsT = sb("wsT", [P, DEPTH * 4, P])
        cols = sb("cols", [P, DEPTH * PROWS])
        lcol = sb("lcol", [P, PROWS])
        bcol = sb("bcol", [SMALL, DEPTH])
        lb = sb("lb", [SMALL, 1])
        ident = sb("ident", [P, P])
        ident16 = sb("ident16", [P, P], BF16)
        mask_q = sb("mask_q", [P, P], BF16)
        mask_k = sb("mask_k", [P, P], BF16)
        zeros16 = sb("zeros16", [P, 512], BF16)
        ones = sb("ones", [P, 1])
        tok16 = sb("tok16", [P, 4, MH])
        tiny = sb("tiny", [P, 96])

        silu = gates[:, 0, 0, :].rearrange("p (t n) -> p t n", t=NT)
        h = gates[:, 0, 1, :].rearrange("p (t n) -> p t n", t=NT)
        hT_hi, hT_lo = yT_hi[:, 0, 0:2, :], yT_lo[:, 0, 0:2, :]
        xhat = scr[:, 0:2 * D].rearrange("p (t n) -> p t n", t=NT)
        merged = xhat
        mtmp = scr[:, 2048:3072].rearrange("p (a n) -> p a n", a=2)
        qT, kT = featT[:, 0], featT[:, 1]
        ml_raw = featT[:, 2:4].rearrange("p a c t -> p (a c) t")
        so = featT[:, 4].rearrange("p c t -> p (c t)")
        gm_u = featT[:, 5].rearrange("p c t -> p (c t)")
        att_v, ml_v, gm_v = tokv[:, 0], tokv[:, 1], tokv[:, 2]
        mlqk = gates[:, 4:6].rearrange("p b t n -> p (b t n)").rearrange("p (c t) -> p c t", c=2 * MH)
        k_tok, v_w = scr[:, 0:512], scr[:, 512:1024]
        w_intra = scr[:, 1024:2048].rearrange("p (c n) -> p c n", c=2)
        c_state = scr[:, 2048:2560]
        hm = scr[:, 2560:3584].rearrange("p (c n) -> p c n", c=2)
        gm_y = scr[:, 2560:3584]
        ml_y = featT[:, 5].rearrange("p c t -> p (c t)")
        prob = featT[:, 2].rearrange("p c t -> p (c t)")
        probT = featT[:, 3].rearrange("p c t -> p (c t)")
        y_tok = tokv[:, 2]
        spat_in = scr[:, 0:DEPTH * 4 * P].rearrange("p (g s) -> p g s", g=DEPTH * 4)
        prow = scr[0:DEPTH * PROWS, 2048:2048 + P]
        ssq, rstd = tiny[:, 0:2], tiny[:, 2:4]
        mhalf, eps_col = tiny[:, 4:5], tiny[:, 5:6]
        inv_width = {D: tiny[:, 6:7], CB: tiny[:, 7:8], P: tiny[:, 8:9]}
        gssq, grstd = tiny[:, 12:14], tiny[:, 14:16]
        negmax, rsum = tiny[:, 16:24], tiny[:, 24:32]
        rinv = tiny[:, 32:40]
        n_state = tiny[:, 40:44]
        w_inter = tiny[:, 44:48]
        den, rden = tiny[:, 48:56], tiny[:, 56:64]
        hssq, hrstd = tiny[:, 64:72], tiny[:, 72:80]
        m_prev = tiny[0:MH, 80:81]
        dtmp = tiny[:, 84:88]

        x_loaded, par_loaded, gain_loaded = sem("x_loaded"), sem("par_loaded"), sem("gain_loaded")
        raw_loaded = [sem(f"raw_loaded{i}") for i in range(RING)]
        const_ready, par_turned, par_ready = sem("const_ready"), sem("par_turned"), sem("par_ready")
        hi_ready = sem("hi_ready")
        lo_ready = sem("lo_ready")
        unit_done = sem("unit_done")
        x_ready, ssq_ready, rstd_ready, xhat_ready = sem("x_ready"), sem("ssq_ready"), sem("rstd_ready"), sem("xhat_ready")
        xT_turned, xT_hi_ready, xT_lo_ready = sem("xT_turned"), sem("xT_hi_ready"), sem("xT_lo_ready")
        acc0_done = sem("acc0_done")
        gu0_done, silu_done, h_ready = sem("gu0_done"), sem("silu_done"), sem("h_ready")
        hT_turned, hT_hi_ready, hT_lo_ready = sem("hT_turned"), sem("hT_hi_ready"), sem("hT_lo_ready")
        proj_evac = sem("proj_evac")
        gate0_done, gate_evac = sem("gate0_done"), sem("gate_evac")
        br_done, br_evac, merged_ready = sem("br_done"), sem("br_evac"), sem("merged_ready")
        dve_chain, act_chain, pool_chain = sem("dve_chain"), sem("act_chain"), sem("pool_chain")
        gelu_v_done, gelu_u_done, gssq_ready, grstd_ready, vhat_ready = (
            sem("gelu_v_done"), sem("gelu_u_done"), sem("gssq_ready"), sem("grstd_ready"), sem("vhat_ready"))
        z_ready, expz_ready, exp1_ready, lnz_ready, ls_ready = (
            sem("z_ready"), sem("expz_ready"), sem("exp1_ready"), sem("lnz_ready"), sem("ls_ready"))
        lfli_done, spatial_done, gm_gained, gm_y_ready, gm_hi_ready, gm_lo_ready = (
            sem("lfli_done"), sem("spatial_done"), sem("gm_gained"), sem("gm_y_ready"), sem("gm_hi_ready"), sem("gm_lo_ready"))
        rows_ready, rexp_ready, conv_ready, mlqk_ready = sem("rows_ready"), sem("rexp_ready"), sem("conv_ready"), sem("mlqk_ready")
        decay_done, rT_done, w_intra_ready, rT_ready = sem("decay_done"), sem("rT_done"), sem("w_intra_ready"), sem("rT_ready")
        kq_done, k_turned, k_tok_ready, qk_ready, v_w_ready = (
            sem("kq_done"), sem("k_turned"), sem("k_tok_ready"), sem("qk_ready"), sem("v_w_ready"))
        state_done, intra_done, c_state_ready, n_state_ready = sem("state_done"), sem("intra_done"), sem("c_state_ready"), sem("n_state_ready")
        inter_done, h_num_ready, hsq_ready, hssq_ready, hrstd_ready, hn_ready = (
            sem("inter_done"), sem("h_num_ready"), sem("hsq_ready"), sem("hssq_ready"), sem("hrstd_ready"), sem("hn_ready"))
        ml_turned, so_ready, ml_y_ready, ml_hi_ready, ml_lo_ready = (
            sem("ml_turned"), sem("so_ready"), sem("ml_y_ready"), sem("ml_hi_ready"), sem("ml_lo_ready"))
        score_done, max_ready, prob_ready, p_turned, probT_ready, pv_done, y_tok_ready = (
            sem("score_done"), sem("max_ready"), sem("prob_ready"), sem("p_turned"), sem("probT_ready"), sem("pv_done"), sem("y_tok_ready"))
        y_turned, att_hi_ready, att_lo_ready = sem("y_turned"), sem("att_hi_ready"), sem("att_lo_ready")
        qk_scaled, negc_ready, out_stored = sem("qk_scaled"), sem("negc_ready"), sem("out_stored")

        block = ctx.enter_context(nc.Block())

        @block.sync
        def _(sp):
            def at(ap, layer):
                return ap[bass.ds(layer, 1)]

            def load(layer, j, slot, parts, turn=0):
                sp.wait_ge(lo_ready, UNITS * layer + j + RING * turn + 1)
                for dst, src in parts:
                    sp.dma_start(dst, src).then_inc(raw_loaded[slot], 32 // len(parts))

            def gate_up(layer, j, slot, wg, wu, half, t, turn=0):
                dst = w_raw[:, slot, :].rearrange("p (k n) -> p k n", k=4)
                src = [at(w, layer).rearrange("o (k p) n -> p (o k) n", p=P)[:, 4 * half:4 * half + 4, bass.ds(t * WB, WB)]
                       for w in (wg, wu)]
                load(layer, j, slot, [(dst[:, :, 0:WB], src[0]), (dst[:, :, WB:2 * WB], src[1])], turn)

            def down(layer, j, slot, wd, t, turn=0):
                dst = w_raw[:, slot, :].rearrange("p (k n) -> p k n", k=2)
                src = at(wd, layer)[:, bass.ds(t * WB, WB), :].rearrange("o (k p) n -> p (o k) n", p=P)
                load(layer, j, slot, [(dst[:, k:k + 1, :], src[:, k:k + 1, :]) for k in range(2)], turn)

            def ffn_loads(layer, b, wg, wu, wd, before_last):
                gate_up(layer, b, b % RING, wg, wu, 0, 0)
                gate_up(layer, b + 1, (b + 1) % RING, wg, wu, 1, 0)
                with sp.Fori(1, NB, 1) as t:
                    gate_up(layer, b - 1, (b + 2) % RING, wg, wu, 0, t, t)
                    gate_up(layer, b, b % RING, wg, wu, 1, t, t)
                    down(layer, b + 1, (b + 1) % RING, wd, t - 1, t)
                before_last()
                down(layer, b + FFN_UNITS - 1, (b + FFN_UNITS - 1) % RING, wd, NB - 1)

            def load_gain(n, row):
                sp.wait_ge(xhat_ready, 2 * n)
                sp.dma_start(gain[:, :], row.partition_broadcast(P)).then_inc(gain_loaded, 16)

            def w_in_block(layer, j, slot, col, half, turn=0):
                dst = w_raw[:, slot, :].rearrange("p (k n) -> p k n", k=4)
                src = at(w_in, layer).rearrange("o (k p) n -> p (o k) n", p=P)[:, 4 * half:4 * half + 4, bass.ds(col, CB)]
                load(layer, j, slot, [(dst[:, k:k + 2, :], src[:, k:k + 2, :]) for k in (0, 2)], turn)

            def rows256(layer, j, slot, w, r):
                dst = w_raw[:, slot, :].rearrange("p (k n) -> p k n", k=2)
                src = at(w, layer)[:, r * 256:(r + 1) * 256, :].rearrange("o (k p) n -> p (o k) n", p=P)
                load(layer, j, slot, [(dst[:, k:k + 1, :], src[:, k:k + 1, :]) for k in range(2)])

            for t in range(NT):
                sp.dma_start(xs[:, t, :], x[0, t * P:(t + 1) * P, :]).then_inc(x_loaded, 16)
            with sp.Fori(0, DEPTH, 1) as l:
                sp.wait_ge(lo_ready, UNITS * l + 1)
                sp.dma_start(gain[:, :], at(norm_ffn1, l).rearrange("o n -> (o n)").partition_broadcast(P)).then_inc(gain_loaded, 16)
                ffn_loads(l, 0, ffn1_gate, ffn1_up, ffn1_down,
                          lambda: load_gain(3 * l + 1, at(norm_mix, l).rearrange("o n -> (o n)")))
                with sp.Fori(0, 3, 1) as g:
                    for c in range(6):
                        w_in_block(l, U_WI + c, (U_WI + c) % RING, g * GROUP + (c // 2) * CB, c % 2, 2 * g)
                for half in range(2):
                    j = U_SMALL + half
                    dst = w_raw[:, j % RING, 0:4 * SMALL].rearrange("p (k n) -> p k n", k=4)
                    src = at(w_in, l).rearrange("o (k p) n -> p (o k) n", p=P)[:, 4 * half:4 * half + 4, :]
                    c0, c1 = 3 * CB, GROUP + 3 * CB
                    with nc.allow_non_contiguous_dma(reason="16 gate columns"):
                        load(l, j, j % RING, [(dst[:, :, 0:AH], src[:, :, c0:c0 + AH]),
                                              (dst[:, :, AH:SMALL], src[:, :, c1:c1 + 2 * MH])])
                for b in range(2 * NGATE):
                    w_in_block(l, U_GATE + b, (U_GATE + b) % RING, 2 * GROUP + 3 * CB + (b // 2) * CB, b % 2)
                for r, w in enumerate((w_br_gmlp, w_br_ml, w_br_att)):
                    for a in range(2):
                        rows256(l, U_BR + 2 * r + a, (U_BR + 2 * r + a) % RING, w, a)
                load_gain(3 * l + 2, at(norm_ffn2, l).rearrange("o n -> (o n)"))
                for a in range(4):
                    rows256(l, U_OUT + a, (U_OUT + a) % RING, w_out, a)
                ffn_loads(l, U_FFN2, ffn2_gate, ffn2_up, ffn2_down, lambda: None)
            load_gain(3 * DEPTH, norm_final)
            for j in range(RING):
                sp.wait_ge(lo_ready, UNITS * DEPTH + j + 1)
                src = ffn1_gate[0, j * P:(j + 1) * P, 0:2048]
                for k in range(2):
                    sp.dma_start(w_raw[:, j, k * 1024:(k + 1) * 1024], src[:, k * 1024:(k + 1) * 1024]).then_inc(raw_loaded[j], 16)
            for j in range(RING):
                sp.wait_ge(raw_loaded[j], 32 * (UNITS * DEPTH // RING + 1))
            for t in range(NT):
                sp.wait_ge(xhat_ready, 2 * 3 * DEPTH + t + 1)
                sp.dma_start(out[0, t * P:(t + 1) * P, :], xhat[:, t, :]).then_inc(out_stored, 16)
            sp.wait_ge(out_stored, 16 * NT)

        @block.gpsimd
        def _(pool):
            steps = [0]

            def chain(ins):
                ins.then_inc(pool_chain, 1)
                steps[0] += 1
                pool.wait_ge(pool_chain, steps[0])

            chain(nc.gpsimd.memset(ident[:, :], 0.0))
            chain(nc.gpsimd.affine_select(out=ident[:, :], in_=ident[:, :], compare_op=ALU.not_equal, fill=1.0,
                                          base=0, pattern=[[-1, P]], channel_multiplier=1))
            chain(nc.gpsimd.tensor_copy(ident16[:, :], ident[:, :]))
            chain(nc.gpsimd.memset(head_sel[:, :, :], 0.0))
            chain(nc.gpsimd.affine_select(out=head_sel[:, :, :], in_=head_sel[:, :, :], compare_op=ALU.not_equal,
                                          fill=1.0, base=0, pattern=[[-1, AH], [0, P]], channel_multiplier=1))
            chain(nc.gpsimd.memset(mask_q[:, :], 0.0))
            chain(nc.gpsimd.affine_select(out=mask_q[:, :], in_=mask_q[:, :], compare_op=ALU.is_ge, fill=NEG,
                                          base=0, pattern=[[-1, P]], channel_multiplier=1))
            chain(nc.gpsimd.memset(mask_k[:, :], 0.0))
            chain(nc.gpsimd.affine_select(out=mask_k[:, :], in_=mask_k[:, :], compare_op=ALU.is_ge, fill=NEG,
                                          base=0, pattern=[[1, P]], channel_multiplier=-1))
            chain(nc.gpsimd.memset(mhalf, -0.5))
            chain(nc.gpsimd.memset(eps_col, EPS))
            for width, col in inv_width.items():
                chain(nc.gpsimd.memset(col, 1.0 / width))
            for rows in (z_rows, ls_rows, negc, b_row, g_row, negm):
                chain(nc.gpsimd.memset(rows[:, :], 0.0))
            nc.gpsimd.memset(zeros16[:, :], 0.0).then_inc(const_ready, 1)
            pool.wait_ge(par_ready, 2)
            nc.gpsimd.affine_select(out=wsT[:, :, :], in_=wsT[:, :, :], compare_op=ALU.is_ge, fill=0.0,
                                    base=0, pattern=[[0, DEPTH * 4], [1, P]], channel_multiplier=-1).then_inc(par_ready, 1)

            def inv_root(order, dst, src, width, ready):
                shape = [P, src.shape[1]]
                order(nc.gpsimd.tensor_tensor(src, src, inv_width[width].to_broadcast(shape), ALU.mult))
                order(nc.gpsimd.tensor_tensor(src, src, eps_col.to_broadcast(shape), ALU.add))
                nc.gpsimd.tensor_tensor(dst, src, mhalf.to_broadcast(shape), ALU.pow).then_inc(ready, 1)

            def norm(order, n):
                for t in range(NT):
                    pool.wait_ge(ssq_ready, 2 * n + t + 1)
                    inv_root(order, rstd[:, t:t + 1], ssq[:, t:t + 1], D, rstd_ready)

            base = steps[0]
            with pool.Fori(0, DEPTH, 1) as l:
                order = Chain(pool, pool_chain, l, 16)
                order.base = l * 16 + base
                norm(order, 3 * l)
                norm(order, 3 * l + 1)
                pool.wait_ge(gssq_ready, l + 1)
                inv_root(order, grstd, gssq, CB, grstd_ready)
                pool.wait_ge(hssq_ready, l + 1)
                inv_root(order, hrstd, hssq, P, hrstd_ready)
                norm(order, 3 * l + 2)
                order.end()
            order = Chain(pool, pool_chain, 0, 4)
            order.base = base + 16 * DEPTH
            norm(order, 3 * DEPTH)

        @block.scalar
        def _(act):
            def split(layer, j, turn=0):
                slot = j % RING
                act.wait_ge(raw_loaded[slot], 32 * (UNITS // RING * layer + j // RING + turn + 1))
                act.wait_ge(unit_done, UNITS * layer + j + RING * turn + 1)
                nc.scalar.copy(w_hi[:, slot, :], w_raw[:, slot, :]).then_inc(hi_ready, 1)

            def pe_has(layer, j, turn=0):
                act.wait_ge(unit_done, UNITS * layer + j + RING * turn + RING + 1)

            def turn_in(group, banks=TURN_BANKS):
                for i in range(4):
                    t, q = i // 2, i % 2
                    act.wait_ge(xT_turned, 4 * group + i + 1)
                    src = ps[:, banks[t] + q, :].rearrange("p (c n) -> p c n", c=4)
                    nc.scalar.copy(xT_hi[:, 4 * q:4 * q + 4, t * P:(t + 1) * P], src).then_inc(xT_hi_ready, 1)

            def squares(n):
                for t in range(NT):
                    act.wait_ge(x_ready, 2 * n + t + 1)
                    nc.scalar.activation(xhat[:, t, :], xs[:, t, :], ACT.Square,
                                         accum_out=ssq[:, t:t + 1]).then_inc(ssq_ready, 1)

            def silus(layer, call, b, t):
                act.wait_ge(gu0_done, NB * call + t + 1)
                nc.scalar.activation(silu[:, 0, :], ps[:, 4, 0:WB], ACT.Silu).then_inc(silu_done, 1)

            def silu1():
                nc.scalar.activation(silu[:, 1, :], ps[:, 5, 0:WB], ACT.Silu).then_inc(silu_done, 1)

            def hT(call, t):
                act.wait_ge(hT_turned, NB * call + t + 1)
                nc.scalar.copy(hT_hi, ps[:, 6, :].rearrange("p (k n) -> p k n", k=2)).then_inc(hT_hi_ready, 1)

            def ffn(l, call, b):
                split(l, b + RING)
                silus(l, call, b, 0)
                pe_has(l, b + 1)
                silu1()
                split(l, b + 1 + RING)
                with act.Fori(1, NB, 1) as t:
                    hT(call, t - 1)
                    split(l, b + 2, t)
                    silus(l, call, b, t)
                    pe_has(l, b, t)
                    silu1()
                    split(l, b + 3, t)
                    split(l, b + 4, t)
                hT(call, NB - 1)

            for i in range(DEPTH):
                r = PROWS * i
                for dst, src in (
                        (prow[r:r + MH, :], norm_ml_head[i].rearrange("(c p) -> c p", p=P)),
                        (prow[r + MH:r + 2 * MH, :], norm_gmlp[i].rearrange("(c p) -> c p", p=P)),
                        (prow[r + 2 * MH:r + PROWS, :], conv_ml[i].rearrange("j (c p) -> (j c) p", p=P))):
                    act.dma_start(dst, src).then_inc(par_loaded, 16)
            act.dma_start(spat_in, w_spatial.rearrange("l g t s -> t (l g) s")).then_inc(par_loaded, 16)
            act.dma_start(bsp[:, :, :], b_spatial.rearrange("l g t -> (l g t)").partition_broadcast(P).rearrange(
                "p (a t) -> p a t", t=P)).then_inc(par_loaded, 16)
            with nc.allow_non_contiguous_dma(reason="a bias per head"):
                for r, v in ((0, b_f_att), (AH, b_i_ml), (AH + MH, b_f_ml)):
                    act.dma_start(bcol[r:r + v.shape[1], :], v.rearrange("l h -> h l")).then_inc(par_loaded, 16)
            act.sem_inc(proj_evac, 3)
            for j in range(RING):
                split(0, j)

            with act.Fori(0, DEPTH, 1) as l:
                order = Chain(act, act_chain, l, 3)
                squares(3 * l)
                turn_in(4 * l)
                ffn(l, 2 * l, 0)
                squares(3 * l + 1)
                turn_in(4 * l + 1)
                split(l, FFN_UNITS - 1 + RING)

                with act.Fori(0, 3, 1) as g:
                    for c in range(6):
                        if c == 1 or c == 3:
                            pe_has(l, U_WI + c, 2 * g)
                            dst = featT[:, bass.ds(2 * g + c // 2, 1)].rearrange("p o c t -> p (o c t)")
                            nc.scalar.copy(dst, ps[:, c - 1:c + 1, :].rearrange("p b n -> p (b n)")).then_inc(proj_evac, 1)
                        if c == 5:
                            pe_has(l, U_WI + c, 2 * g)
                            dst = tokv[:, bass.ds(g, 1)].rearrange("p o t n -> p (o t n)")
                            nc.scalar.copy(dst, ps[:, 4:6, :].rearrange("p b n -> p (b n)")).then_inc(proj_evac, 1)
                        split(l, U_WI + c + RING, 2 * g)

                def gate_tile(b, t):
                    nc.scalar.activation(gates[:, b, t, :], ps[:, 4 + t, :], ACT.Tanh, scale=0.5).then_inc(gate_evac, 1)

                def step(s, work):
                    b = (s - U_GATE) // 2 if U_GATE <= s < U_BR and (s - U_GATE) % 2 else None
                    if b is not None:
                        act.wait_ge(gate0_done, NGATE * l + b + 1)
                        gate_tile(b, 0)
                    if b is not None:
                        pe_has(l, s)
                        gate_tile(b, 1)
                    split(l, s + RING)
                    work()

                def mix_a():
                    act.wait_ge(proj_evac, 9 * l + 12)
                    nc.scalar.activation(gm_v[:, :, :], gm_v[:, :, :], ACT.Gelu_apprx_tanh).then_inc(gelu_v_done, 1)
                    nc.scalar.activation(gm_u, gm_u, ACT.Gelu_apprx_tanh).then_inc(gelu_u_done, 1)
                    act.wait_ge(gelu_v_done, l + 1)
                    order(nc.scalar.activation(scr[:, 0:CB], gm_v[:, 0, :], ACT.Square, accum_out=gssq[:, 0:1]))
                    nc.scalar.activation(scr[:, CB:2 * CB], gm_v[:, 1, :], ACT.Square,
                                         accum_out=gssq[:, 1:2]).then_inc(gssq_ready, 1)
                    nc.scalar.mul(featT[:, 0], featT[:, 0], ATT_SCALE).then_inc(qk_scaled, 1)

                def mix_b():
                    act.wait_ge(z_ready, l + 1)
                    rows = ls_rows[0:SMALL, :]
                    order(nc.scalar.activation(rows, z_rows[0:SMALL, :], ACT.Abs))
                    nc.scalar.activation(rows, rows, ACT.Exp, scale=-1.0).then_inc(expz_ready, 1)
                    act.wait_ge(exp1_ready, l + 1)
                    nc.scalar.activation(rows, rows, ACT.Ln).then_inc(lnz_ready, 1)

                def mix_c():
                    act.wait_ge(rows_ready, l + 1)
                    nc.scalar.activation(r_row[0:MH, :], r_row[0:MH, :], ACT.Exp).then_inc(rexp_ready, 1)
                    act.wait_ge(gm_y_ready, l + 1)
                    nc.scalar.copy(yT_hi[:, 2].rearrange("p c t -> p (c t)"), gm_y).then_inc(gm_hi_ready, 1)

                def mix_d():
                    act.wait_ge(decay_done, l + 1)
                    nc.scalar.activation(w_intra, ps[:, 6:8, :], ACT.Exp).then_inc(w_intra_ready, 1)
                    act.wait_ge(conv_ready, l + 1)
                    nc.scalar.activation(mlqk[:, :, :], mlqk[:, :, :], ACT.Silu).then_inc(mlqk_ready, 1)

                def mix_e():
                    act.wait_ge(k_turned, l + 1)
                    nc.scalar.copy(k_tok, ps[:, 1, :]).then_inc(k_tok_ready, 1)
                    nc.scalar.activation(so, so, ACT.Tanh, scale=0.5).then_inc(act_chain, 1)
                    order.n += 1
                    act.wait_ge(act_chain, order.base + order.n)
                    nc.scalar.activation(so, so, ACT.Copy, scale=0.5, bias=0.5).then_inc(so_ready, 1)

                def mix_f():
                    act.wait_ge(state_done, l + 1)
                    nc.scalar.copy(c_state, ps[:, 1, :]).then_inc(c_state_ready, 1)

                def mix_h():
                    act.wait_ge(h_num_ready, l + 1)
                    nc.scalar.activation(ml_y, scr[:, 2560:3584], ACT.Square).then_inc(hsq_ready, 1)

                def mix_j():
                    act.wait_ge(ml_y_ready, l + 1)
                    nc.scalar.copy(yT_hi[:, 1].rearrange("p c t -> p (c t)"), ml_y).then_inc(ml_hi_ready, 1)

                def att_exp(p):
                    act.wait_ge(max_ready, 4 * l + p + 1)
                    for e in range(2):
                        for t in range(2):
                            src = ps[:, 2 + e, 0:256] if t else ps[:, 2 + e, 256:384]
                            dst = prob[:, 512 * e:512 * e + 256] if t else prob[:, 512 * e + 256:512 * e + 384]
                            c = 4 * (p % 2) + 2 * e + t
                            nc.scalar.activation(dst, src, ACT.Exp, bias=negmax[:, c:c + 1],
                                                 accum_out=rsum[:, c:c + 1]).then_inc(prob_ready, 1)

                def att_probT(p):
                    act.wait_ge(p_turned, 4 * l + p + 1)
                    dst = probT.rearrange("p (e n) -> p e n", e=2)[:, :, 0:384]
                    nc.scalar.copy(dst, ps[:, 2:4, 0:384]).then_inc(probT_ready, 1)

                def att_yT():
                    act.wait_ge(y_turned, l + 1)
                    nc.scalar.copy(yT_hi[:, 0].rearrange("p c t -> p (c t)"),
                                   ps[:, 2:4, :].rearrange("p b n -> p (b n)")).then_inc(att_hi_ready, 1)

                work = {0: [mix_a], 1: [mix_b], 2: [mix_c], 3: [lambda: att_exp(0), mix_d],
                        4: [lambda: att_probT(0), mix_e], 5: [mix_f], 6: [lambda: att_exp(1)],
                        7: [lambda: att_probT(1), mix_h], 8: [mix_j], 9: [lambda: att_exp(2)],
                        10: [lambda: att_probT(2)], 12: [lambda: att_exp(3)], 13: [lambda: att_probT(3)], 16: [att_yT]}
                for i in range(U_OUT - U_SMALL):
                    step(U_SMALL + i, lambda i=i: [f() for f in work.get(i, [])])
                turn_in(4 * l + 2, MERGED_BANKS)
                for a in range(3):
                    split(l, U_OUT + a + RING)
                squares(3 * l + 2)
                turn_in(4 * l + 3)
                split(l, U_FFN2 - 1 + RING)
                ffn(l, 2 * l + 1, U_FFN2)
                split(l, UNITS - 1 + RING)
                order.end()
            squares(3 * DEPTH)

        @block.vector
        def _(dve):
            dve.sem_inc(lo_ready, RING)

            def split(layer, j, turn=0):
                slot = j % RING
                dve.wait_ge(hi_ready, UNITS * layer + j + RING * turn + 1)
                nc.vector.tensor_tensor(w_lo[:, slot, :], w_raw[:, slot, :], w_hi[:, slot, :].bitcast(F32),
                                        ALU.subtract).then_inc(lo_ready, 1)

            def pe_has(layer, j, turn=0):
                dve.wait_ge(unit_done, UNITS * layer + j + RING * turn + RING + 1)

            def residual(l, n, last_unit):
                for t in range(NT):
                    if t == 0:
                        dve.wait_ge(acc0_done, n)
                    else:
                        pe_has(l, last_unit)
                    nc.vector.scalar_tensor_tensor(
                        out=xs[:, t, :], in0=ps[:, 2 * t:2 * t + 2, :].rearrange("p b n -> p (b n)"), scalar=0.5,
                        in1=xs[:, t, :], op0=ALU.mult, op1=ALU.add).then_inc(x_ready, 1)

            def norm(n):
                dve.wait_ge(gain_loaded, 16 * (n + 1))
                for t in range(NT):
                    dve.wait_ge(rstd_ready, 2 * n + t + 1)
                    nc.vector.scalar_tensor_tensor(out=xhat[:, t, :], in0=xs[:, t, :], scalar=rstd[:, t:t + 1],
                                                   in1=gain[:, :], op0=ALU.mult, op1=ALU.mult).then_inc(xhat_ready, 1)

            def turn_in(group, banks=TURN_BANKS):
                for i in range(4):
                    t, q = i // 2, i % 2
                    dve.wait_ge(xT_hi_ready, 4 * group + i + 1)
                    src = ps[:, banks[t] + q, :].rearrange("p (c n) -> p c n", c=4)
                    sl = (slice(None), slice(4 * q, 4 * q + 4), slice(t * P, (t + 1) * P))
                    nc.vector.tensor_tensor(xT_lo[sl], src, xT_hi[sl].bitcast(F32), ALU.subtract).then_inc(xT_lo_ready, 1)

            def hidden(call, t):
                for i in range(NT):
                    dve.wait_ge(silu_done, 2 * NB * call + 2 * t + i + 1)
                    nc.vector.tensor_tensor(h[:, i, :], ps[:, 4 + i, WB:2 * WB], silu[:, i, :], ALU.mult).then_inc(h_ready, 1)

            def hT(call, t):
                dve.wait_ge(hT_hi_ready, NB * call + t + 1)
                nc.vector.tensor_tensor(hT_lo, ps[:, 6, :].rearrange("p (k n) -> p k n", k=2), hT_hi.bitcast(F32),
                                        ALU.subtract).then_inc(hT_lo_ready, 1)

            def ffn(l, call, b):
                split(l, b + RING)
                hidden(call, 0)
                split(l, b + 1 + RING)
                with dve.Fori(1, NB, 1) as t:
                    hT(call, t - 1)
                    split(l, b + 2, t)
                    hidden(call, t)
                    split(l, b + 3, t)
                    split(l, b + 4, t)
                hT(call, NB - 1)

            for j in range(RING):
                split(0, j)
            nc.vector.memset(ones[:, :], 1.0).then_inc(par_ready, 1)
            dve.wait_ge(par_turned, 1)
            nc.vector.tensor_copy(wsT[:, :, :].rearrange("p g s -> p (g s)"),
                                  ps[:, 0:2, :].rearrange("p b n -> p (b n)")).then_inc(par_ready, 1)
            nc.vector.tensor_copy(cols[:, :], ps[:, 2, 0:DEPTH * PROWS]).then_inc(par_ready, 1)
            dve.wait_ge(x_loaded, 32)
            dve.wait_ge(par_ready, 4)
            dve.sem_inc(x_ready, NT)

            DVE_PER_LAYER = 39
            with dve.Fori(0, DEPTH, 1) as l:
                order = Chain(dve, dve_chain, l, DVE_PER_LAYER)
                norm(3 * l)
                turn_in(4 * l)
                order(nc.vector.tensor_copy(lcol[:, :], cols[:, bass.ds(l * PROWS, PROWS)]))
                order(nc.vector.tensor_copy(lb[:, :], bcol[:, bass.ds(l, 1)]))
                ffn(l, 2 * l, 0)
                residual(l, 3 * l + 1, FFN_UNITS - 1)
                norm(3 * l + 1)
                turn_in(4 * l + 1)
                split(l, FFN_UNITS - 1 + RING)
                with dve.Fori(0, 3, 1) as g:
                    for c in range(6):
                        split(l, U_WI + c + RING, 2 * g)

                def conv(chunks):
                    dve.wait_ge(proj_evac, 9 * l + 12)
                    taps = [lcol[:, 2 * MH + j * KD:2 * MH + (j + 1) * KD] for j in range(NTAP)]
                    for j in reversed(range(NTAP)):
                        back = NTAP - 1 - j
                        for c in chunks:
                            if back == 0:
                                ins = nc.vector.tensor_scalar(mlqk[:, c, :], ml_raw[:, c, :], taps[j][:, c:c + 1], None, ALU.mult)
                            else:
                                ins = nc.vector.scalar_tensor_tensor(
                                    out=mlqk[:, c, back:], in0=ml_raw[:, c, 0:S - back], scalar=taps[j][:, c:c + 1],
                                    in1=mlqk[:, c, back:], op0=ALU.mult, op1=ALU.add)
                            if c == chunks[-1] and (j > 0 or chunks[-1] < 2 * MH - 1):
                                order(ins)
                            elif c == chunks[-1]:
                                ins.then_inc(conv_ready, 1)

                def mix_b1():
                    dve.wait_ge(grstd_ready, l + 1)
                    for t in range(NT):
                        ins = nc.vector.tensor_scalar(gm_v[:, t, :], gm_v[:, t, :], grstd[:, t:t + 1], None, ALU.mult)
                    ins.then_inc(vhat_ready, 1)

                def mix_b2():
                    pe_has(l, U_SMALL + 1)
                    nc.vector.tensor_scalar(z_rows[0:SMALL, :], ps[0:SMALL, 0, 0:S], lb[:, 0:1], None, ALU.add).then_inc(z_ready, 1)
                    dve.wait_ge(expz_ready, l + 1)
                    nc.vector.tensor_scalar(ls_rows[0:SMALL, :], ls_rows[0:SMALL, :], 1.0, None, ALU.add).then_inc(exp1_ready, 1)
                    dve.wait_ge(lnz_ready, l + 1)
                    nc.vector.scalar_tensor_tensor(out=ls_rows[0:SMALL, :], in0=z_rows[0:SMALL, :], scalar=0.0,
                                                   in1=ls_rows[0:SMALL, :], op0=ALU.min, op1=ALU.subtract).then_inc(ls_ready, 1)

                def mix_c1():
                    lf, li = ps[0:MH, 0, 0:S], ps[0:MH, 0, S:2 * S]
                    b, g_, m = b_row[0:MH, :], g_row[0:MH, :], negm[0:MH, :]
                    dve.wait_ge(lfli_done, l + 1)
                    nc.vector.tensor_tensor_scan(b[:, 0:P], lf[:, 0:P], ls_rows[0:MH, 0:P], 0.0, ALU.add, ALU.bypass)
                    order(nc.vector.tensor_tensor_scan(b[:, P:S], lf[:, P:S], ls_rows[0:MH, P:S], 0.0, ALU.add, ALU.bypass))
                    order(nc.vector.tensor_tensor(g_, li, b, ALU.subtract))
                    order(nc.vector.tensor_tensor_scan(m[:, 0:P], g_[:, 0:P], g_[:, 0:P], 0.0, ALU.max, ALU.bypass))
                    order(nc.vector.tensor_tensor(m_prev, b[:, P - 1:P], m[:, P - 1:P], ALU.add))
                    order(nc.vector.tensor_tensor_scan(m[:, P:S], g_[:, P:S], g_[:, P:S], m_prev, ALU.max, ALU.bypass))
                    nc.vector.scalar_tensor_tensor(out=r_row[0:MH, 0:S], in0=b, scalar=-1.0, in1=m, op0=ALU.mult, op1=ALU.subtract)
                    nc.vector.tensor_scalar(r_row[0:MH, S:S + P], m[:, P:S], -1.0, m_prev, ALU.mult, ALU.add)
                    order(nc.vector.tensor_scalar(r_row[0:MH, S + P:2 * S], g_[:, 0:P], m[:, P - 1:P], None, ALU.subtract))
                    nc.vector.tensor_scalar(m, m, -1.0, None, ALU.mult).then_inc(rows_ready, 1)
                    order(nc.vector.tensor_tensor_scan(negc[0:AH, :], ls_rows[0:AH, :], ls_rows[0:AH, :], 0.0, ALU.add, ALU.bypass))
                    nc.vector.tensor_scalar(negc[0:AH, :], negc[0:AH, :], -1.0, None, ALU.mult).then_inc(negc_ready, 1)

                def mix_c2():
                    dve.wait_ge(spatial_done, l + 1)
                    for g4 in range(4):
                        src = ps[:, 6 + g4 // 2, 256 * (g4 % 2):256 * (g4 % 2) + 256].rearrange("p (c t) -> p c t", c=2)
                        bias = bsp[:, bass.ds(4 * l + g4, 1), :].to_broadcast([P, 2, P])
                        ins = nc.vector.scalar_tensor_tensor(
                            out=gm_y[:, 256 * g4:256 * g4 + 256].rearrange("p (c t) -> p c t", c=2), in0=src,
                            scalar=lcol[:, MH + g4:MH + g4 + 1], in1=bias, op0=ALU.mult, op1=ALU.add)
                    ins.then_inc(gm_gained, 1)
                    dve.wait_ge(gm_gained, l + 1)
                    dve.wait_ge(gelu_u_done, l + 1)
                    nc.vector.tensor_tensor(gm_y, gm_y, gm_u, ALU.mult).then_inc(gm_y_ready, 1)

                def mix_d1():
                    dve.wait_ge(rT_done, l + 1)
                    nc.vector.tensor_copy(tok16[:, :, :].rearrange("p k h -> p (k h)"), ps[:, 0, 0:4 * MH]).then_inc(rT_ready, 1)
                    dve.wait_ge(rT_ready, l + 1)
                    order(nc.vector.tensor_scalar(w_inter, tok16[:, 2, :], ML_SCALE, None, ALU.mult))
                    dve.wait_ge(gm_hi_ready, l + 1)
                    nc.vector.tensor_tensor(yT_lo[:, 2].rearrange("p c t -> p (c t)"), gm_y,
                                            yT_hi[:, 2].rearrange("p c t -> p (c t)").bitcast(F32), ALU.subtract).then_inc(gm_lo_ready, 1)

                def mix_e1():
                    vw = v_w.rearrange("p (h n) -> p h n", h=MH)
                    ws = tok16[:, 3, :].unsqueeze(2).to_broadcast([P, MH, P])
                    nc.vector.tensor_tensor(vw, ml_v[:, 0, :].rearrange("p (h n) -> p h n", h=MH), ws, ALU.mult).then_inc(v_w_ready, 1)
                    dve.wait_ge(kq_done, l + 1)
                    dve.wait_ge(w_intra_ready, l + 1)
                    for c, bank in ((0, 0), (1, 6)):
                        ins = nc.vector.scalar_tensor_tensor(out=w_intra[:, c, :], in0=ps[:, bank, :], scalar=ML_SCALE,
                                                             in1=w_intra[:, c, :], op0=ALU.mult, op1=ALU.mult)
                    ins.then_inc(qk_ready, 1)

                def mix_f1():
                    dve.wait_ge(state_done, l + 1)
                    nc.vector.tensor_copy(n_state, ps[:, 7, 0:MH]).then_inc(n_state_ready, 1)

                def mix_g1():
                    dve.wait_ge(inter_done, l + 1)
                    heads = lambda ap: ap.rearrange("p (h n) -> p h n", h=MH)
                    wide = lambda ap: ap.unsqueeze(2).to_broadcast([P, MH, P])
                    order(nc.vector.tensor_tensor(dtmp, ps[:, 7, 16:20], w_inter, ALU.mult))
                    nc.vector.tensor_copy(den[:, 0:MH], ps[:, 7, 8:12])
                    order(nc.vector.tensor_tensor(den[:, MH:2 * MH], ps[:, 7, 12:16], dtmp, ALU.add))
                    order(nc.vector.tensor_scalar(rden, den, -1.0, None, ALU.mult))
                    order(nc.vector.tensor_tensor(den, den, rden, ALU.max))
                    order(nc.vector.tensor_tensor(den, den, tok16[:, 0:2, :].rearrange("p k h -> p (k h)"), ALU.max))
                    nc.vector.reciprocal(rden, den).then_inc(dve_chain, 1)
                    order.n += 1
                    nc.vector.tensor_tensor(heads(hm[:, 1, :]), heads(ps[:, 1, :]), wide(w_inter), ALU.mult).then_inc(dve_chain, 1)
                    order.n += 1
                    dve.wait_ge(dve_chain, order.base + order.n)
                    order(nc.vector.tensor_tensor(hm[:, 1, :], hm[:, 1, :], ps[:, 6, :], ALU.add))
                    nc.vector.tensor_tensor(heads(hm[:, 0, :]), heads(ps[:, 0, :]), wide(rden[:, 0:MH]), ALU.mult)
                    nc.vector.tensor_tensor(heads(hm[:, 1, :]), heads(hm[:, 1, :]), wide(rden[:, MH:2 * MH]), ALU.mult).then_inc(h_num_ready, 1)

                def mix_h1():
                    dve.wait_ge(hsq_ready, l + 1)
                    nc.vector.tensor_reduce(hssq, ml_y.rearrange("p (h n) -> p h n", h=2 * MH), AX.X, ALU.add).then_inc(hssq_ready, 1)
                    dve.wait_ge(hrstd_ready, l + 1)
                    all_h = scr[:, 2560:3584].rearrange("p (h n) -> p h n", h=2 * MH)
                    nc.vector.tensor_tensor(all_h, all_h, hrstd.unsqueeze(2).to_broadcast([P, 2 * MH, P]), ALU.mult).then_inc(hn_ready, 1)

                def mix_j1():
                    dve.wait_ge(ml_turned, l + 1)
                    dve.wait_ge(so_ready, l + 1)
                    for c in range(MH):
                        sl = slice(256 * c, 256 * c + 256)
                        ins = nc.vector.scalar_tensor_tensor(out=ml_y[:, sl], in0=ps[:, c // 2, 256 * (c % 2):256 * (c % 2) + 256],
                                                             scalar=lcol[:, c:c + 1], in1=so[:, sl], op0=ALU.mult, op1=ALU.mult)
                    ins.then_inc(ml_y_ready, 1)
                    dve.wait_ge(ml_hi_ready, l + 1)
                    nc.vector.tensor_tensor(yT_lo[:, 1].rearrange("p c t -> p (c t)"), ml_y,
                                            yT_hi[:, 1].rearrange("p c t -> p (c t)").bitcast(F32), ALU.subtract).then_inc(ml_lo_ready, 1)

                def att_max(p):
                    dve.wait_ge(score_done, 4 * l + p + 1)
                    nm = negmax[:, 4 * (p % 2):4 * (p % 2) + 4].rearrange("p (e t) -> p e t", e=2)
                    nc.vector.tensor_reduce(nm[:, :, 1:2], ps[:, 2:4, 0:256], AX.X, ALU.max, negate=True)
                    nc.vector.tensor_reduce(nm[:, :, 0:1], ps[:, 2:4, 256:384], AX.X, ALU.max, negate=True).then_inc(max_ready, 1)

                def att_y(p):
                    c = 4 * (p % 2)
                    dve.wait_ge(prob_ready, 16 * l + 4 * p + 4)
                    order(nc.vector.reciprocal(rinv[:, c:c + 4], rsum[:, c:c + 4]))
                    dve.wait_ge(pv_done, 4 * l + p + 1)
                    for t in range(NT):
                        r = rinv[:, c:c + 4].rearrange("p (e t) -> p e t", e=2)[:, :, t:t + 1].to_broadcast([P, 2, DH])
                        dst = y_tok[:, t, 128 * p:128 * p + 128].rearrange("p (e d) -> p e d", e=2)
                        ins = nc.vector.tensor_tensor(dst, ps[:, 2:4, 384 + DH * t:384 + DH * t + DH], r, ALU.mult)
                    ins.then_inc(y_tok_ready, 1)

                def att_yT():
                    dve.wait_ge(att_hi_ready, l + 1)
                    nc.vector.tensor_tensor(yT_lo[:, 0].rearrange("p c t -> p (c t)"),
                                            ps[:, 2:4, :].rearrange("p b n -> p (b n)"),
                                            yT_hi[:, 0].rearrange("p c t -> p (c t)").bitcast(F32), ALU.subtract).then_inc(att_lo_ready, 1)

                def merge(r, o):
                    t, half = o // 2, o % 2
                    if o < 3:
                        dve.wait_ge(br_done, 9 * l + 3 * r + o + 1)
                    else:
                        pe_has(l, U_BR + 2 * r + 1)
                    g = gates[:, 2 * (2 - r) + half, t, :]
                    dst = merged[:, t, 512 * half:512 * half + 512]
                    first = dst if r == 0 else mtmp[:, o % 2, :]
                    nc.vector.scalar_tensor_tensor(out=first, in0=g, scalar=1.0, in1=ps[:, 4 + o, :],
                                                   op0=ALU.add, op1=ALU.mult).then_inc(br_evac, 1)
                    if r:
                        dve.wait_ge(br_evac, 12 * l + 4 * r + o + 1)
                        ins = nc.vector.tensor_tensor(dst, dst, mtmp[:, o % 2, :], ALU.add)
                        if r == 2 and half:
                            ins.then_inc(merged_ready, 1)
                        else:
                            order(ins)

                work = {0: [lambda: conv([0, 1])], 1: [mix_b1, mix_b2, lambda: conv([2, 3])],
                        2: [mix_c1, mix_c2, lambda: conv([4, 5, 6, 7])], 3: [lambda: att_max(0), mix_d1],
                        4: [mix_e1], 5: [lambda: att_y(0), mix_f1], 6: [lambda: att_max(1), mix_g1], 7: [mix_h1],
                        8: [lambda: att_y(1), mix_j1], 9: [lambda: att_max(2)], 11: [lambda: att_y(2)],
                        12: [lambda: att_max(3)], 14: [lambda: att_y(3)], 16: [att_yT],
                        15: [lambda o=o: merge(0, o) for o in range(4)],
                        17: [lambda o=o: merge(1, o) for o in range(4)],
                        19: [lambda o=o: merge(2, o) for o in range(4)]}
                for i in range(U_OUT - U_SMALL):
                    if i < 19:
                        split(l, U_SMALL + i + RING)
                    for f in work.get(i, []):
                        f()
                    if i == 19:
                        turn_in(4 * l + 2, MERGED_BANKS)
                        split(l, U_SMALL + i + RING)
                for a in range(3):
                    split(l, U_OUT + a + RING)
                residual(l, 3 * l + 2, U_FFN2 - 1)
                norm(3 * l + 2)
                turn_in(4 * l + 3)
                split(l, U_FFN2 - 1 + RING)
                ffn(l, 2 * l + 1, U_FFN2)
                residual(l, 3 * l + 3, UNITS - 1)
                split(l, UNITS - 1 + RING)
                order.end()
            norm(3 * DEPTH)

        @block.tensor
        def _(pe):
            pe.sem_inc(unit_done, RING)

            def mm3(dst, x_hi, x_lo, w_h, w_l, first, last, feature_major=False):
                for i, (a, b) in enumerate(((x_hi, w_h), (x_hi, w_l), (x_lo, w_h))):
                    if feature_major:
                        a, b = b, a
                    ins = nc.tensor.matmul(dst, a, b, start=first and i == 0, stop=last and i == 2, skip_group_check=True)
                return ins

            def begin(layer, j, turn=0):
                pe.wait_ge(lo_ready, UNITS * layer + j + RING * turn + RING + 1)

            def tok_block(layer, j, half, bank, wait_tile, tile0_done, turn=0):
                begin(layer, j, turn)
                slot = j % RING
                for t in range(NT):
                    wait_tile(t)
                    for k in range(4):
                        xk = (slice(None), 4 * half + k, slice(t * P, (t + 1) * P))
                        wk = slice(512 * k, 512 * k + 512)
                        ins = mm3(ps[:, bank + t, :], xT_hi[xk], xT_lo[xk], w_hi[:, slot, wk], w_lo[:, slot, wk],
                                  half == 0 and k == 0, half == 1 and k == 3)
                    if half == 1 and t == 0:
                        ins.then_inc(tile0_done, 1)
                ins.then_inc(unit_done, 1)

            def turn(src, t, ready, banks=TURN_BANKS):
                ready(t)
                for q in range(2):
                    for c in range(4):
                        ins = nc.tensor.transpose(ps[:, banks[t] + q, P * c:P * c + P],
                                                  src[:, t, P * (4 * q + c):P * (4 * q + c) + P], ident[:, :])
                    ins.then_inc(xT_turned, 1)

            def norm(n):
                for t in range(NT):
                    turn(xhat, t, lambda t: pe.wait_ge(xhat_ready, 2 * n + t + 1))

            def have_xT(group, i):
                pe.wait_ge(xT_lo_ready, 4 * group + i + 1)

            def ffn(l, call, b, group):
                def down(j, order_turn, last):
                    begin(l, j, order_turn)
                    slot = j % RING
                    for t in range(NT):
                        for half in range(2):
                            for k in range(2):
                                hk = (slice(None), k, slice(t * P, (t + 1) * P))
                                wk = slice(1024 * k + 512 * half, 1024 * k + 512 * half + 512)
                                ins = mm3(ps[:, 2 * t + half, :], hT_hi[hk], hT_lo[hk], w_hi[:, slot, wk], w_lo[:, slot, wk],
                                          False, last and k == 1)
                        if t == 0 and last:
                            ins.then_inc(acc0_done, 1)
                    ins.then_inc(unit_done, 1)

                def turn_h():
                    for k in range(2):
                        for t in range(NT):
                            ins = nc.tensor.transpose(ps[:, 6, 256 * k + P * t:256 * k + P * t + P],
                                                      h[:, t, P * k:P * k + P], ident[:, :])
                    ins.then_inc(hT_turned, 1)

                tok_block(l, b, 0, 4, lambda t: have_xT(group, 2 * t), gu0_done)
                tok_block(l, b + 1, 1, 4, lambda t: have_xT(group, 2 * t + 1), gu0_done)
                with pe.Fori(1, NB, 1) as i:
                    tok_block(l, b + 2, 0, 4, lambda t: pe.wait_ge(h_ready, 2 * NB * call + 2 * i + t - 1), gu0_done, i - 1)
                    turn_h()
                    tok_block(l, b + 3, 1, 4, lambda t: None, gu0_done, i - 1)
                    pe.wait_ge(hT_lo_ready, NB * call + i)
                    down(b + 4, i - 1, False)
                pe.wait_ge(h_ready, 2 * NB * call + 2 * NB)
                turn_h()
                pe.wait_ge(hT_lo_ready, NB * call + NB)
                down(b + FFN_UNITS - 1, 0, True)

            def clear_acc():
                for bank in range(4):
                    nc.tensor.matmul(ps[:, bank, :], zeros16[:, 0:P], zeros16[:, :], start=True, stop=True)

            pe.wait_ge(const_ready, 1)
            pe.wait_ge(par_loaded, 16 * (3 * DEPTH + 5))
            for g in range(DEPTH * 4):
                nc.tensor.transpose(ps[:, g // 4, P * (g % 4):P * (g % 4) + P], spat_in[:, g, :], ident[:, :])
            nc.tensor.transpose(ps[:, 2, 0:DEPTH * PROWS], prow, ident[0:DEPTH * PROWS, 0:DEPTH * PROWS]).then_inc(par_turned, 1)

            with pe.Fori(0, DEPTH, 1) as l:
                norm(3 * l)
                clear_acc()
                ffn(l, 2 * l, 0, 4 * l)
                norm(3 * l + 1)

                def feature_block(j, half, bank, turns):
                    begin(l, j, turns)
                    slot = j % RING
                    for c in range(4):
                        for k in range(4):
                            kk = 4 * half + k
                            wk = slice(512 * k + P * c, 512 * k + P * c + P)
                            ins = mm3(ps[:, bank + c // 2, 256 * (c % 2):256 * (c % 2) + 256], xT_hi[:, kk, :], xT_lo[:, kk, :],
                                      w_hi[:, slot, wk], w_lo[:, slot, wk], half == 0 and k == 0 and c % 2 == 0,
                                      half == 1 and k == 3, feature_major=True)
                    ins.then_inc(unit_done, 1)

                with pe.Fori(0, 3, 1) as g:
                    have_xT(4 * l + 1, 3)
                    for c in range(4):
                        if c % 2 == 0:
                            pe.wait_ge(proj_evac, 9 * l + 3 * g + c // 2 + 1)
                        feature_block(U_WI + c, c % 2, c - c % 2, 2 * g)
                    pe.wait_ge(proj_evac, 9 * l + 3 * g + 3)
                    tok_block(l, U_WI + 4, 0, 4, lambda t: None, gate0_done, 2 * g)
                    begin(l, U_WI + 5, 2 * g)
                    slot = (U_WI + 5) % RING
                    for t in range(NT):
                        for k in range(4):
                            xk = (slice(None), 4 + k, slice(t * P, (t + 1) * P))
                            wk = slice(512 * k, 512 * k + 512)
                            ins = mm3(ps[:, 4 + t, :], xT_hi[xk], xT_lo[xk], w_hi[:, slot, wk], w_lo[:, slot, wk], False, k == 3)
                    ins.then_inc(unit_done, 1)

                pe.wait_ge(proj_evac, 9 * l + 10)
                for half in range(2):
                    j = U_SMALL + half
                    begin(l, j)
                    for k in range(4):
                        wk = slice(SMALL * k, SMALL * k + SMALL)
                        ins = mm3(ps[0:SMALL, 0, 0:S], xT_hi[:, 4 * half + k, :], xT_lo[:, 4 * half + k, :],
                                  w_hi[:, j % RING, wk], w_lo[:, j % RING, wk], half == 0 and k == 0, half == 1 and k == 3,
                                  feature_major=True)
                    ins.then_inc(unit_done, 1)

                mm = nc.tensor.matmul

                def mix_c():
                    pe.wait_ge(ls_ready, l + 1)
                    mm(ps[0:MH, 0, 0:S], ident[:, AH + MH:SMALL], ls_rows[:, :], start=True, stop=True)
                    mm(ps[0:MH, 0, S:2 * S], ident[:, AH:AH + MH], z_rows[:, :], start=True, stop=True).then_inc(lfli_done, 1)
                    pe.wait_ge(vhat_ready, l + 1)
                    for g4 in range(4):
                        for c in range(2):
                            ins = mm(ps[:, 6 + g4 // 2, 256 * (g4 % 2) + P * c:256 * (g4 % 2) + P * c + P],
                                     gm_v[:, c, P * g4:P * g4 + P],
                                     wsT[:, bass.ds(4 * l + g4, 1), :].rearrange("p o t -> p (o t)"), start=True, stop=True)
                    ins.then_inc(spatial_done, 1)

                def mix_d():
                    pe.wait_ge(rows_ready, l + 1)
                    pe.wait_ge(gm_gained, l + 1)
                    for c in range(2):
                        bank = ps[:, 6 + c, :]
                        mm(bank, g_row[:, P * c:P * c + P], head_sel[:, 0:MH, :].rearrange("p h t -> p (h t)"),
                           start=True, stop=False, skip_group_check=True)
                        for hd in range(MH):
                            mm(ps[:, 6 + c, P * hd:P * hd + P], head_sel[:, hd, :], negm[:, P * c:P * c + P],
                               start=False, stop=False, skip_group_check=True)
                            ins = mm(ps[:, 6 + c, P * hd:P * hd + P], ident16[:, :], mask_k[:, :],
                                     start=False, stop=True, skip_group_check=True)
                    ins.then_inc(decay_done, 1)
                    pe.wait_ge(rexp_ready, l + 1)
                    for k in range(4):
                        ins = mm(ps[:, 0, MH * k:MH * k + MH], r_row[0:MH, P * k:P * k + P], ident[0:MH, 0:MH], start=True, stop=True)
                    ins.then_inc(rT_done, 1)

                def mix_e():
                    pe.wait_ge(mlqk_ready, l + 1)
                    pe.wait_ge(rT_ready, l + 1)
                    pe.wait_ge(w_intra_ready, l + 1)
                    for hd in range(MH):
                        ins = nc.tensor.transpose(ps[:, 1, P * hd:P * hd + P], mlqk[:, MH + hd, 0:P], ident[:, :])
                    ins.then_inc(k_turned, 1)
                    for c, bank in ((0, 0), (1, 6)):
                        for hd in range(MH):
                            ins = mm(ps[:, bank, P * hd:P * hd + P], mlqk[:, MH + hd, P * c:P * c + P],
                                     mlqk[:, hd, P * c:P * c + P], start=True, stop=True)
                    ins.then_inc(kq_done, 1)

                def mix_f():
                    pe.wait_ge(k_tok_ready, l + 1)
                    pe.wait_ge(v_w_ready, l + 1)
                    for hd in range(MH):
                        sl = slice(P * hd, P * hd + P)
                        mm(ps[:, 1, sl], k_tok[:, sl], v_w[:, sl], start=True, stop=True)
                        ins = mm(ps[:, 7, hd:hd + 1], k_tok[:, sl], tok16[:, 3, hd:hd + 1], start=True, stop=True)
                    ins.then_inc(state_done, 1)
                    pe.wait_ge(qk_ready, l + 1)
                    for c, bank in ((0, 0), (1, 6)):
                        for hd in range(MH):
                            sl = slice(P * hd, P * hd + P)
                            mm(ps[:, bank, sl], w_intra[:, c, sl], ml_v[:, c, sl], start=True, stop=True)

                def mix_g():
                    pe.wait_ge(c_state_ready, l + 1)
                    pe.wait_ge(n_state_ready, l + 1)
                    for c in range(2):
                        for hd in range(MH):
                            mm(ps[:, 7, 8 + 4 * c + hd:9 + 4 * c + hd], w_intra[:, c, P * hd:P * hd + P], ones[:, :],
                               start=True, stop=True)
                    for hd in range(MH):
                        mm(ps[:, 1, P * hd:P * hd + P], mlqk[:, hd, P:S], c_state[:, P * hd:P * hd + P], start=True, stop=True)
                        ins = mm(ps[:, 7, 16 + hd:17 + hd], mlqk[:, hd, P:S], n_state[:, hd:hd + 1], start=True, stop=True)
                    ins.then_inc(inter_done, 1)

                def mix_i():
                    pe.wait_ge(hn_ready, l + 1)
                    for hd in range(MH):
                        for c in range(2):
                            ins = nc.tensor.transpose(ps[:, hd // 2, 256 * (hd % 2) + P * c:256 * (hd % 2) + P * c + P],
                                                      hm[:, c, P * hd:P * hd + P], ident[:, :])
                    ins.then_inc(ml_turned, 1)

                def score(p):
                    if p == 0:
                        pe.wait_ge(qk_scaled, l + 1)
                        pe.wait_ge(negc_ready, l + 1)
                    if p:
                        pe.wait_ge(y_tok_ready, 4 * l + p)
                    for e in range(2):
                        for t in range(NT):
                            dst = ps[:, 2 + e, 0:256] if t else ps[:, 2 + e, 256:384]
                            keys = P * (t + 1)
                            hp = slice(DH * e, DH * e + DH)
                            mm(dst, qT[hp, p, P * t:P * t + P], kT[hp, p, 0:keys], start=True, stop=False, skip_group_check=True)
                            mm(dst, head_sel[:, 2 * p + e, :], negc[:, 0:keys], start=False, stop=False, skip_group_check=True)
                            ins = mm(dst[:, keys - P:keys], ident16[:, :], mask_q[:, :], start=False, stop=True, skip_group_check=True)
                    ins.then_inc(score_done, 1)

                def turn_p(p):
                    pe.wait_ge(prob_ready, 16 * l + 4 * p + 4)
                    for e in range(2):
                        for i in range(3):
                            ins = nc.tensor.transpose(ps[:, 2 + e, P * i:P * i + P], prob[:, 512 * e + P * i:512 * e + P * i + P], ident[:, :])
                    ins.then_inc(p_turned, 1)

                def pv(p):
                    pe.wait_ge(probT_ready, 4 * l + p + 1)
                    for e in range(2):
                        hd = 2 * p + e
                        v = lambda c: att_v[:, c, DH * hd:DH * hd + DH]
                        pt = lambda i: probT[:, 512 * e + P * i:512 * e + P * i + P]
                        mm(ps[:, 2 + e, 384:384 + DH], pt(2), v(0), start=True, stop=True)
                        mm(ps[:, 2 + e, 384 + DH:512], pt(0), v(0), start=True, stop=False)
                        ins = mm(ps[:, 2 + e, 384 + DH:512], pt(1), v(1), start=False, stop=True)
                    ins.then_inc(pv_done, 1)

                def turn_y():
                    pe.wait_ge(y_tok_ready, 4 * l + 4)
                    for c in range(4):
                        for t in range(NT):
                            ins = nc.tensor.transpose(ps[:, 2 + c // 2, 256 * (c % 2) + P * t:256 * (c % 2) + P * t + P],
                                                      y_tok[:, t, P * c:P * c + P], ident[:, :])
                    ins.then_inc(y_turned, 1)

                work = {2: [mix_c], 3: [mix_d, lambda: score(0)], 4: [lambda: turn_p(0), mix_e],
                        5: [lambda: pv(0), mix_f], 6: [lambda: score(1), mix_g], 7: [lambda: turn_p(1)],
                        8: [lambda: pv(1), mix_i], 9: [lambda: score(2)], 10: [lambda: turn_p(2)], 11: [lambda: pv(2)],
                        12: [lambda: score(3)], 13: [lambda: turn_p(3)], 14: [lambda: pv(3)], 16: [turn_y]}
                for b in range(NGATE):
                    for half in range(2):
                        def wait_tile(t):
                            if half == 0 and b == 0:
                                if t == 0:
                                    pe.wait_ge(proj_evac, 9 * l + 12)
                            elif half == 0:
                                pe.wait_ge(gate_evac, 12 * l + 2 * (b - 1) + t + 1)
                        tok_block(l, U_GATE + 2 * b + half, half, 4, wait_tile, gate0_done)
                        for f in work.get(2 + 2 * b + half, []):
                            f()

                for r, ready in enumerate((gm_lo_ready, ml_lo_ready, att_lo_ready)):
                    pe.wait_ge(ready, l + 1)
                    if r == 0:
                        pe.wait_ge(gate_evac, 12 * (l + 1))
                        pe.wait_ge(ml_y_ready, l + 1)
                    for a in range(2):
                        j = U_BR + 2 * r + a
                        begin(l, j)
                        for o in range(4):
                            t, half = o // 2, o % 2
                            if r and a == 0:
                                pe.wait_ge(br_evac, 12 * l + 4 * (r - 1) + o + 1)
                            for k in range(2):
                                yk = (slice(None), 2 - r, 2 * a + k, slice(t * P, (t + 1) * P))
                                wk = slice(1024 * k + 512 * half, 1024 * k + 512 * half + 512)
                                ins = mm3(ps[:, 4 + o, :], yT_hi[yk], yT_lo[yk], w_hi[:, j % RING, wk], w_lo[:, j % RING, wk],
                                          a == 0 and k == 0, a == 1 and k == 1)
                            if a == 1 and o < 3:
                                ins.then_inc(br_done, 1)
                        ins.then_inc(unit_done, 1)
                        for f in work.get(j - U_SMALL, []):
                            f()

                for t in range(NT):
                    turn(merged, t, lambda t: pe.wait_ge(merged_ready, 2 * l + t + 1), MERGED_BANKS)
                for a in range(4):
                    j = U_OUT + a
                    begin(l, j)
                    for t in range(NT):
                        have_xT(4 * l + 2, 2 * t + (a // 2))
                        for half in range(2):
                            for k in range(2):
                                xk = (slice(None), 2 * a + k, slice(t * P, (t + 1) * P))
                                wk = slice(1024 * k + 512 * half, 1024 * k + 512 * half + 512)
                                ins = mm3(ps[:, 2 * t + half, :], xT_hi[xk], xT_lo[xk], w_hi[:, j % RING, wk], w_lo[:, j % RING, wk],
                                          a == 0 and k == 0, a == 3 and k == 1)
                        if t == 0 and a == 3:
                            ins.then_inc(acc0_done, 1)
                    ins.then_inc(unit_done, 1)
                norm(3 * l + 2)
                clear_acc()
                ffn(l, 2 * l + 1, U_FFN2, 4 * l + 3)


_INS = ['x', 'norm_ffn1', 'ffn1_gate', 'ffn1_up', 'ffn1_down', 'norm_mix', 'w_in', 'b_f_att', 'b_i_ml', 'b_f_ml',
        'conv_ml', 'norm_ml_head', 'norm_gmlp', 'w_spatial', 'b_spatial', 'w_br_att', 'w_br_ml', 'w_br_gmlp',
        'w_out', 'norm_ffn2', 'ffn2_gate', 'ffn2_up', 'ffn2_down', 'norm_final']


def kernel(**inputs):
    import numpy as _np
    import concourse.bacc as _bacc
    from concourse import mybir as _mybir
    from concourse.bass_utils import run_bass_kernel_spmd as _run

    nc = _bacc.Bacc("TRN2", target_bir_lowering=False, num_devices=1, dynamic_dma_scratch_size=1024)
    arrays, args = {}, []
    for name in _INS:
        a = _np.ascontiguousarray(inputs[name])
        arrays[f"in_{name}_dram"] = a
        args.append(nc.dram_tensor(f"in_{name}_dram", a.shape, _mybir.dt.from_np(a.dtype), kind="ExternalInput").ap())
    shape = inputs["x"].shape
    args.append(nc.dram_tensor("out_0_dram", shape, _mybir.dt.float32, kind="ExternalOutput").ap())
    trunk(nc, *args)
    r = _run(nc, [arrays], core_ids=[0])
    return r.results[0]["out_0_dram"]
```

```python
from contextlib import ExitStack

import concourse.bass as bass
from concourse import mybir

F32 = mybir.dt.float32
F32R = mybir.dt.float32r
BF16 = mybir.dt.bfloat16
ALU = mybir.AluOpType
ACT = mybir.ActivationFunctionType
AX = mybir.AxisListType

P = 128
EPS = 1e-6
NEG = -1e30
RING = 3
LOAD_INC = 96


class Chain:

    def __init__(self, engine, sem, layer, per_layer):
        self.engine, self.sem, self.n, self.per_layer = engine, sem, 0, per_layer
        self.base = layer * per_layer

    def __call__(self, instruction):
        instruction.then_inc(self.sem, 1)
        self.n += 1
        self.engine.wait_ge(self.sem, self.base + self.n)

    def end(self):
        assert self.n == self.per_layer, (self.n, self.per_layer)


def trunk(nc, x, norm_ffn1, ffn1_gate, ffn1_up, ffn1_down, norm_mix, w_in, b_f_att, b_i_ml, b_f_ml,
          conv_ml, norm_ml_head, norm_gmlp, w_spatial, b_spatial, w_br_att, w_br_ml, w_br_gmlp,
          w_out, norm_ffn2, ffn2_gate, ffn2_up, ffn2_down, norm_final, out):
    DEPTH, D, DFF = ffn1_gate.shape
    S = x.shape[1]
    NT = S // P
    KD = D // P
    AH = b_f_att.shape[1]
    MH = b_i_ml.shape[1]
    AW, MW = w_br_att.shape[1], w_br_ml.shape[1]
    DH = AW // AH
    NTAP = conv_ml.shape[1]
    CB = 512
    WB = 256
    NB = DFF // WB
    NGATE = 3 * D // CB
    MF, MI, AF = 0, 32, 64
    SMALL = AF + AH
    GROUP = 3 * CB + AH
    assert NT == 2 and KD == 8 and AW == MW == CB and AH == 2 * MH and DH == 64 and GROUP == 3 * CB + 2 * MH

    FFN_UNITS = 3 * NB
    U_SMALL = FFN_UNITS
    U_WI = U_SMALL + 2
    U_GATE = U_WI + 18
    U_BR = U_GATE + 2 * NGATE
    U_OUT = U_BR + 6
    U_FFN2 = U_OUT + 4
    UNITS = U_FFN2 + FFN_UNITS
    assert UNITS % RING == 0 and FFN_UNITS % RING == 0 and U_FFN2 % RING == 0
    ATT_SCALE = DH ** -0.5
    ML_SCALE = float(P) ** -0.5
    TURN_BANKS, MERGED_BANKS = (4, 6), (2, 4)
    PROWS = 2 * MH + NTAP * KD

    with ExitStack() as ctx:
        def sb(name, shape, dt=F32):
            return ctx.enter_context(nc.sbuf_tensor(name, shape, dt))

        def sem(name):
            return ctx.enter_context(nc.semaphore(name))

        ps = ctx.enter_context(nc.psum_tensor("ps", [P, 8, 512], F32))

        xs = sb("xs", [P, NT, D])
        xT_hi = sb("xT_hi", [P, KD, S], F32R)
        xT_lo = sb("xT_lo", [P, KD, S], F32R)
        w_raw = sb("w_raw", [P, RING, 2048])
        w_hi = sb("w_hi", [P, RING, 2048], F32R)
        w_lo = sb("w_lo", [P, RING, 2048], F32R)
        featT = sb("featT", [P, 6, 4, S])
        tokv = sb("tokv", [P, 3, NT, CB])
        gates = sb("gates", [P, NGATE, NT, CB])
        yT_hi = sb("yT_hi", [P, 3, 4, S], F32R)
        yT_lo = sb("yT_lo", [P, 3, 4, S], F32R)
        gain = sb("gain", [P, D])
        scr = sb("scr", [P, 3584])
        z_rows = sb("z_rows", [P, S])
        ls_rows = sb("ls_rows", [P, S])
        negc = sb("negc", [P, S])
        b_row = sb("b_row", [P, S])
        g_row = sb("g_row", [P, S])
        negm = sb("negm", [P, S])
        r_row = sb("r_row", [P, 2 * S])
        head_sel = sb("head_sel", [P, AH, P])
        bsp = sb("bsp", [P, DEPTH * 4, P])
        wsT = sb("wsT", [P, DEPTH * 4, P])
        cols = sb("cols", [P, DEPTH * PROWS])
        lcol = sb("lcol", [P, PROWS])
        bcol = sb("bcol", [P, DEPTH])
        lb = sb("lb", [P, 1])
        ident = sb("ident", [P, P])
        ident16 = sb("ident16", [P, P], BF16)
        mask_q = sb("mask_q", [P, P], BF16)
        mask_k = sb("mask_k", [P, P], BF16)
        zeros16 = sb("zeros16", [P, 512], BF16)
        ones = sb("ones", [P, 1])
        tok16 = sb("tok16", [P, 4, MH])
        tiny = sb("tiny", [P, 96])

        silu = gates[:, 0, 0, :].rearrange("p (t n) -> p t n", t=NT)
        h = gates[:, 0, 1, :].rearrange("p (t n) -> p t n", t=NT)
        hT_hi = [yT_hi[:, 0, i:i + 2, :] for i in (0, 2)]
        hT_lo = [yT_lo[:, 0, i:i + 2, :] for i in (0, 2)]
        xhat = scr[:, 0:2 * D].rearrange("p (t n) -> p t n", t=NT)
        merged = xhat
        mtmp = scr[:, 2048:3072].rearrange("p (a n) -> p a n", a=2)
        qT, kT = featT[:, 0], featT[:, 1]
        ml_raw = featT[:, 2:4].rearrange("p a c t -> p (a c) t")
        so = featT[:, 4].rearrange("p c t -> p (c t)")
        gm_u = featT[:, 5].rearrange("p c t -> p (c t)")
        att_v, ml_v, gm_v = tokv[:, 0], tokv[:, 1], tokv[:, 2]
        mlqk = gates[:, 4:6].rearrange("p b t n -> p (b t n)").rearrange("p (c t) -> p c t", c=2 * MH)
        k_tok, v_w = scr[:, 0:512], scr[:, 512:1024]
        w_intra = scr[:, 1024:2048].rearrange("p (c n) -> p c n", c=2)
        c_state = scr[:, 2048:2560]
        hm = scr[:, 2560:3584].rearrange("p (c n) -> p c n", c=2)
        gm_y = scr[:, 0:1024]
        ml_y = gates[:, 4].rearrange("p t n -> p (t n)")
        prob = featT[:, 2].rearrange("p c t -> p (c t)")
        probT = featT[:, 3].rearrange("p c t -> p (c t)")
        y_tok = tokv[:, 1]
        spat_in = gates[:, 1].rearrange("p t n -> p (t n)").rearrange("p (g s) -> p g s", g=DEPTH * 4)
        prow = gates[0:DEPTH * PROWS, 2, 0, 0:P]
        ssq, rstd = tiny[:, 0:2], tiny[:, 2:4]
        mhalf, eps_col = tiny[:, 4:5], tiny[:, 5:6]
        inv_width = {D: tiny[:, 6:7], CB: tiny[:, 7:8], P: tiny[:, 8:9]}
        gssq, grstd = tiny[:, 12:14], tiny[:, 14:16]
        negmax, rsum = tiny[:, 16:24], tiny[:, 24:32]
        rinv = tiny[:, 32:40]
        n_state = tiny[:, 40:44]
        w_inter = tiny[:, 44:48]
        den, rden = tiny[:, 48:56], tiny[:, 56:64]
        hssq, hrstd = tiny[:, 64:72], tiny[:, 72:80]
        m_prev = tiny[0:MH, 80:81]
        li_row = r_row[:, S:2 * S]
        dtmp = tiny[:, 84:88]

        x_loaded, par_loaded, gain_loaded = sem("x_loaded"), sem("par_loaded"), sem("gain_loaded")
        raw_loaded = [sem(f"raw_loaded{i}") for i in range(RING)]
        bcol_zero = sem("bcol_zero")
        const_ready, par_turned, par_ready = sem("const_ready"), sem("par_turned"), sem("par_ready")
        hi_ready = sem("hi_ready")
        lo_ready = sem("lo_ready")
        unit_done = sem("unit_done")
        x_ready, ssq_ready, rstd_ready, xhat_ready = sem("x_ready"), sem("ssq_ready"), sem("rstd_ready"), sem("xhat_ready")
        xT_turned, xT_hi_ready, xT_lo_ready = sem("xT_turned"), sem("xT_hi_ready"), sem("xT_lo_ready")
        acc0_done = sem("acc0_done")
        gu0_done, silu_done, h_ready = sem("gu0_done"), sem("silu_done"), sem("h_ready")
        hT_turned, hT_hi_ready, hT_lo_ready = sem("hT_turned"), sem("hT_hi_ready"), sem("hT_lo_ready")
        proj_evac = sem("proj_evac")
        gate0_done, gate_evac = sem("gate0_done"), sem("gate_evac")
        br_done, br_evac, merged_ready = sem("br_done"), sem("br_evac"), sem("merged_ready")
        dve_chain, act_chain, pool_chain = sem("dve_chain"), sem("act_chain"), sem("pool_chain")
        gelu_v_done, gelu_u_done, gssq_ready, grstd_ready, vhat_ready = (
            sem("gelu_v_done"), sem("gelu_u_done"), sem("gssq_ready"), sem("grstd_ready"), sem("vhat_ready"))
        z_ready, expz_ready, exp1_ready, lnz_ready, ls_ready = (
            sem("z_ready"), sem("expz_ready"), sem("exp1_ready"), sem("lnz_ready"), sem("ls_ready"))
        spatial_done, gm_gained, gm_y_ready, gm_hi_ready, gm_lo_ready = (
            sem("spatial_done"), sem("gm_gained"), sem("gm_y_ready"), sem("gm_hi_ready"), sem("gm_lo_ready"))
        rows_ready, rexp_ready, conv_ready, mlqk_ready = sem("rows_ready"), sem("rexp_ready"), sem("conv_ready"), sem("mlqk_ready")
        decay_done, rT_done, w_intra_ready, rT_ready = sem("decay_done"), sem("rT_done"), sem("w_intra_ready"), sem("rT_ready")
        kq_done, k_turned, k_tok_ready, qk_ready, v_w_ready = (
            sem("kq_done"), sem("k_turned"), sem("k_tok_ready"), sem("qk_ready"), sem("v_w_ready"))
        state_done, intra_done, c_state_ready, n_state_ready = sem("state_done"), sem("intra_done"), sem("c_state_ready"), sem("n_state_ready")
        inter_done, h_num_ready, hsq_ready, hssq_ready, hrstd_ready, hn_ready = (
            sem("inter_done"), sem("h_num_ready"), sem("hsq_ready"), sem("hssq_ready"), sem("hrstd_ready"), sem("hn_ready"))
        ml_turned, so_ready, ml_y_ready, ml_hi_ready, ml_lo_ready = (
            sem("ml_turned"), sem("so_ready"), sem("ml_y_ready"), sem("ml_hi_ready"), sem("ml_lo_ready"))
        score_done, max_ready, prob_ready, p_turned, probT_ready, pv_done, y_tok_ready = (
            sem("score_done"), sem("max_ready"), sem("prob_ready"), sem("p_turned"), sem("probT_ready"), sem("pv_done"), sem("y_tok_ready"))
        y_turned, att_hi_ready, att_lo_ready = sem("y_turned"), sem("att_hi_ready"), sem("att_lo_ready")
        qk_scaled, negc_ready, out_stored = sem("qk_scaled"), sem("negc_ready"), sem("out_stored")

        block = ctx.enter_context(nc.Block())

        @block.sync
        def _(sp):
            def at(ap, layer):
                return ap[bass.ds(layer, 1)]

            def load(layer, j, slot, parts, turn=0):
                sp.wait_ge(lo_ready, UNITS * layer + j + RING * turn + 1)
                for dst, src in parts:
                    sp.dma_start(dst, src).then_inc(raw_loaded[slot], LOAD_INC // len(parts))

            def gate_up(layer, j, slot, wg, wu, half, t, turn=0):
                dst = w_raw[:, slot, :].rearrange("p (k n) -> p k n", k=4)
                src = [at(w, layer).rearrange("o (k p) n -> p (o k) n", p=P)[:, 4 * half:4 * half + 4, bass.ds(t * WB, WB)]
                       for w in (wg, wu)]
                load(layer, j, slot, [(dst[:, :, 0:WB], src[0]), (dst[:, :, WB:2 * WB], src[1])], turn)

            def down(layer, j, slot, wd, t, turn=0):
                dst = w_raw[:, slot, :].rearrange("p (k n) -> p k n", k=2)
                src = at(wd, layer)[:, bass.ds(t * WB, WB), :].rearrange("o (k p) n -> p (o k) n", p=P)
                load(layer, j, slot, [(dst[:, k:k + 1, :], src[:, k:k + 1, :]) for k in range(2)], turn)

            def ffn_loads(layer, b, wg, wu, wd, before_last):
                gate_up(layer, b, b % RING, wg, wu, 0, 0)
                gate_up(layer, b + 1, (b + 1) % RING, wg, wu, 1, 0)
                with sp.Fori(1, NB, 1) as t:
                    gate_up(layer, b - 1, (b + 2) % RING, wg, wu, 0, t, t)
                    gate_up(layer, b, b % RING, wg, wu, 1, t, t)
                    down(layer, b + 1, (b + 1) % RING, wd, t - 1, t)
                before_last()
                down(layer, b + FFN_UNITS - 1, (b + FFN_UNITS - 1) % RING, wd, NB - 1)

            def load_gain(n, row):
                sp.wait_ge(xhat_ready, 2 * n)
                sp.dma_start(gain[:, :], row.partition_broadcast(P)).then_inc(gain_loaded, 16)

            def w_in_block(layer, j, slot, col, half, turn=0):
                dst = w_raw[:, slot, :].rearrange("p (k n) -> p k n", k=4)
                src = at(w_in, layer).rearrange("o (k p) n -> p (o k) n", p=P)[:, 4 * half:4 * half + 4, bass.ds(col, CB)]
                load(layer, j, slot, [(dst[:, k:k + 2, :], src[:, k:k + 2, :]) for k in (0, 2)], turn)

            def rows256(layer, j, slot, w, r):
                dst = w_raw[:, slot, :].rearrange("p (k n) -> p k n", k=2)
                src = at(w, layer)[:, r * 256:(r + 1) * 256, :].rearrange("o (k p) n -> p (o k) n", p=P)
                load(layer, j, slot, [(dst[:, k:k + 1, :], src[:, k:k + 1, :]) for k in range(2)])

            for t in range(NT):
                sp.dma_start(xs[:, t, :], x[0, t * P:(t + 1) * P, :]).then_inc(x_loaded, 16)
            with sp.Fori(0, DEPTH, 1) as l:
                sp.wait_ge(lo_ready, UNITS * l + 1)
                sp.dma_start(gain[:, :], at(norm_ffn1, l).rearrange("o n -> (o n)").partition_broadcast(P)).then_inc(gain_loaded, 16)
                ffn_loads(l, 0, ffn1_gate, ffn1_up, ffn1_down,
                          lambda: load_gain(3 * l + 1, at(norm_mix, l).rearrange("o n -> (o n)")))
                for half in range(2):
                    j = U_SMALL + half
                    dst = w_raw[:, j % RING, 0:4 * SMALL].rearrange("p (k n) -> p k n", k=4)
                    src = at(w_in, l).rearrange("o (k p) n -> p (o k) n", p=P)[:, 4 * half:4 * half + 4, :]
                    ca, cm = 3 * CB, GROUP + 3 * CB
                    with nc.allow_non_contiguous_dma(reason="16 gate columns"):
                        load(l, j, j % RING, [(dst[:, :, AF:AF + AH], src[:, :, ca:ca + AH]),
                                              (dst[:, :, MF:MF + MH], src[:, :, cm + MH:cm + 2 * MH]),
                                              (dst[:, :, MI:MI + MH], src[:, :, cm:cm + MH])])
                with sp.Fori(0, 3, 1) as g:
                    for c in range(6):
                        w_in_block(l, U_WI + c, (U_WI + c) % RING, g * GROUP + (c // 2) * CB, c % 2, 2 * g)
                for b in range(2 * NGATE):
                    w_in_block(l, U_GATE + b, (U_GATE + b) % RING, 2 * GROUP + 3 * CB + (b // 2) * CB, b % 2)
                for r, w in enumerate((w_br_gmlp, w_br_ml, w_br_att)):
                    for a in range(2):
                        rows256(l, U_BR + 2 * r + a, (U_BR + 2 * r + a) % RING, w, a)
                load_gain(3 * l + 2, at(norm_ffn2, l).rearrange("o n -> (o n)"))
                for a in range(4):
                    rows256(l, U_OUT + a, (U_OUT + a) % RING, w_out, a)
                ffn_loads(l, U_FFN2, ffn2_gate, ffn2_up, ffn2_down, lambda: None)
            load_gain(3 * DEPTH, norm_final)
            for j in range(2):
                sp.wait_ge(lo_ready, UNITS * DEPTH + j + 1)
                src = ffn1_gate[0, j * P:(j + 1) * P, 0:2048]
                for k in range(2):
                    sp.dma_start(w_raw[:, j, k * 1024:(k + 1) * 1024], src[:, k * 1024:(k + 1) * 1024]).then_inc(raw_loaded[j], LOAD_INC // 2)
            for j in range(2):
                sp.wait_ge(raw_loaded[j], LOAD_INC * (UNITS * DEPTH // RING + 1))
            for t in range(NT):
                sp.wait_ge(xhat_ready, 2 * 3 * DEPTH + t + 1)
                sp.dma_start(out[0, t * P:(t + 1) * P, :], xhat[:, t, :]).then_inc(out_stored, 16)
            sp.wait_ge(out_stored, 16 * NT)

        @block.gpsimd
        def _(pool):
            steps = [0]

            def chain(ins):
                ins.then_inc(pool_chain, 1)
                steps[0] += 1
                pool.wait_ge(pool_chain, steps[0])

            nc.gpsimd.memset(bcol[:, :], 0.0).then_inc(bcol_zero, 1)
            chain(nc.gpsimd.memset(ident[:, :], 0.0))
            chain(nc.gpsimd.affine_select(out=ident[:, :], in_=ident[:, :], compare_op=ALU.not_equal, fill=1.0,
                                          base=0, pattern=[[-1, P]], channel_multiplier=1))
            nc.gpsimd.memset(zeros16[:, :], 0.0).then_inc(const_ready, 1)
            chain(nc.gpsimd.memset(mhalf, -0.5))
            chain(nc.gpsimd.memset(eps_col, EPS))
            for width, col in inv_width.items():
                chain(nc.gpsimd.memset(col, 1.0 / width))
            chain(nc.gpsimd.tensor_copy(ident16[:, :], ident[:, :]))
            chain(nc.gpsimd.memset(mask_q[:, :], 0.0))
            chain(nc.gpsimd.affine_select(out=mask_q[:, :], in_=mask_q[:, :], compare_op=ALU.is_ge, fill=NEG,
                                          base=0, pattern=[[-1, P]], channel_multiplier=1))
            chain(nc.gpsimd.memset(mask_k[:, :], 0.0))
            chain(nc.gpsimd.affine_select(out=mask_k[:, :], in_=mask_k[:, :], compare_op=ALU.is_ge, fill=NEG,
                                          base=0, pattern=[[1, P]], channel_multiplier=-1))

            def more_constants():
                chain(nc.gpsimd.memset(head_sel[:, :, :], 0.0))
                for base in (MF, AF):
                    chain(nc.gpsimd.affine_select(out=head_sel[:, :, :], in_=head_sel[:, :, :], compare_op=ALU.not_equal,
                                                  fill=1.0, base=-base, pattern=[[-1, AH], [0, P]], channel_multiplier=1))
                for rows in (z_rows, ls_rows, negc, b_row, g_row, negm):
                    chain(nc.gpsimd.memset(rows[:, :], 0.0))
            more_constants()
            pool.wait_ge(par_ready, 3)
            nc.gpsimd.affine_select(out=wsT[:, :, :], in_=wsT[:, :, :], compare_op=ALU.is_ge, fill=0.0,
                                    base=0, pattern=[[0, DEPTH * 4], [1, P]], channel_multiplier=-1).then_inc(par_ready, 1)

            def inv_root(order, dst, src, width, ready):
                shape = [P, src.shape[1]]
                order(nc.gpsimd.tensor_tensor(src, src, inv_width[width].to_broadcast(shape), ALU.mult))
                order(nc.gpsimd.tensor_tensor(src, src, eps_col.to_broadcast(shape), ALU.add))
                nc.gpsimd.tensor_tensor(dst, src, mhalf.to_broadcast(shape), ALU.pow).then_inc(ready, 1)

            def norm(order, n):
                for t in range(NT):
                    pool.wait_ge(ssq_ready, 2 * n + t + 1)
                    inv_root(order, rstd[:, t:t + 1], ssq[:, t:t + 1], D, rstd_ready)

            base = steps[0]
            with pool.Fori(0, DEPTH, 1) as l:
                order = Chain(pool, pool_chain, l, 16)
                order.base = l * 16 + base
                norm(order, 3 * l)
                norm(order, 3 * l + 1)
                pool.wait_ge(gssq_ready, l + 1)
                inv_root(order, grstd, gssq, CB, grstd_ready)
                pool.wait_ge(hssq_ready, l + 1)
                inv_root(order, hrstd, hssq, P, hrstd_ready)
                norm(order, 3 * l + 2)
                order.end()
            order = Chain(pool, pool_chain, 0, 4)
            order.base = base + 16 * DEPTH
            norm(order, 3 * DEPTH)

        @block.scalar
        def _(act):
            def split(layer, j, turn=0, width=2048):
                slot = j % RING
                act.wait_ge(raw_loaded[slot], LOAD_INC * (UNITS // RING * layer + j // RING + turn + 1))
                act.wait_ge(unit_done, UNITS * layer + j + RING * turn + 1)
                nc.scalar.copy(w_hi[:, slot, 0:width], w_raw[:, slot, 0:width]).then_inc(hi_ready, 1)

            def pe_has(layer, j, turn=0):
                act.wait_ge(unit_done, UNITS * layer + j + RING * turn + RING + 1)

            def turn_in(group, banks=TURN_BANKS):
                for i in range(4):
                    t, q = i // 2, i % 2
                    act.wait_ge(xT_turned, 4 * group + i + 1)
                    src = ps[:, banks[t] + q, :].rearrange("p (c n) -> p c n", c=4)
                    nc.scalar.copy(xT_hi[:, 4 * q:4 * q + 4, t * P:(t + 1) * P], src).then_inc(xT_hi_ready, 1)

            def squares(n):
                for t in range(NT):
                    act.wait_ge(x_ready, 2 * n + t + 1)
                    nc.scalar.activation(xhat[:, t, :], xs[:, t, :], ACT.Square,
                                         accum_out=ssq[:, t:t + 1]).then_inc(ssq_ready, 1)

            def silus(layer, call, b, t):
                act.wait_ge(gu0_done, NB * call + t + 1)
                nc.scalar.activation(silu[:, 0, :], ps[:, 4, 0:WB], ACT.Silu).then_inc(silu_done, 1)

            def silu1():
                nc.scalar.activation(silu[:, 1, :], ps[:, 5, 0:WB], ACT.Silu).then_inc(silu_done, 1)

            def hT(call, t, last=0):
                act.wait_ge(hT_turned, NB * call + t + 1)
                nc.scalar.copy(hT_hi[last], ps[:, 6 + last, :].rearrange("p (k n) -> p k n", k=2)).then_inc(hT_hi_ready, 1)

            def ffn(l, call, b, next_width=2048):
                split(l, b + RING)
                silus(l, call, b, 0)
                pe_has(l, b + 1)
                silu1()
                split(l, b + 1 + RING)

                def block(t):
                    hT(call, t - 1)
                    split(l, b + 2, t)
                    silus(l, call, b, t)
                    pe_has(l, b, t)
                    silu1()
                with act.Fori(1, NB - 1, 1) as t:
                    block(t)
                    split(l, b + 3, t)
                    split(l, b + 4, t)
                block(NB - 1)
                hT(call, NB - 1, 1)
                split(l, b + FFN_UNITS, 0, next_width)
                split(l, b + FFN_UNITS + 1, 0, next_width)

            for i in range(DEPTH):
                r = PROWS * i
                for dst, src in (
                        (prow[r:r + MH, :], norm_ml_head[i].rearrange("(c p) -> c p", p=P)),
                        (prow[r + MH:r + 2 * MH, :], norm_gmlp[i].rearrange("(c p) -> c p", p=P)),
                        (prow[r + 2 * MH:r + PROWS, :], conv_ml[i].rearrange("j (c p) -> (j c) p", p=P))):
                    act.dma_start(dst, src).then_inc(par_loaded, 16)
            act.dma_start(spat_in, w_spatial.rearrange("l g t s -> t (l g) s")).then_inc(par_loaded, 16)
            act.dma_start(bsp[:, :, :], b_spatial.rearrange("l g t -> (l g t)").partition_broadcast(P).rearrange(
                "p (a t) -> p a t", t=P)).then_inc(par_loaded, 16)
            with nc.allow_non_contiguous_dma(reason="a bias per head"):
                act.wait_ge(bcol_zero, 1)
                for r, v in ((AF, b_f_att), (MI, b_i_ml), (MF, b_f_ml)):
                    act.dma_start(bcol[r:r + v.shape[1], :], v.rearrange("l h -> h l")).then_inc(par_loaded, 16)
            act.sem_inc(proj_evac, 3)
            for j in range(2):
                split(0, j)

            with act.Fori(0, DEPTH, 1) as l:
                order = Chain(act, act_chain, l, 3)
                squares(3 * l)
                split(l, 2)
                turn_in(4 * l)
                ffn(l, 2 * l, 0, 4 * SMALL)
                squares(3 * l + 1)
                split(l, FFN_UNITS - 1 + RING)
                turn_in(4 * l + 1)

                def projection(c, g):
                    pe_has(l, U_WI + 2 * c + 1, 2 * g)
                    if c < 2:
                        dst, bank = featT[:, 2 * g + c].rearrange("p c t -> p (c t)"), 2 * c
                    else:
                        dst, bank = tokv[:, g].rearrange("p t n -> p (t n)"), 4
                    nc.scalar.copy(dst, ps[:, bank:bank + 2, :].rearrange("p b n -> p (b n)")).then_inc(proj_evac, 1)

                def gate_tile(b, t):
                    nc.scalar.activation(gates[:, b, t, :], ps[:, 4 + t, :], ACT.Tanh, scale=0.5).then_inc(gate_evac, 1)

                def step(s, work):
                    if U_GATE <= s < U_BR and (s - U_GATE) % 2:
                        b = (s - U_GATE) // 2
                        if b == 4:
                            act.wait_ge(ml_lo_ready, l + 1)
                        act.wait_ge(gate0_done, NGATE * l + b + 1)
                        gate_tile(b, 0)
                        pe_has(l, s)
                        gate_tile(b, 1)
                    if U_WI <= s < U_GATE and (s - U_WI) % 2:
                        projection((s - U_WI) // 2 % 3, (s - U_WI) // 6)
                    split(l, s + RING)
                    work()

                def gm_gelu_u():
                    act.wait_ge(proj_evac, 9 * l + 11)
                    nc.scalar.activation(gm_u, gm_u, ACT.Gelu_apprx_tanh).then_inc(gelu_u_done, 1)

                def gm_gelu_v():
                    act.wait_ge(proj_evac, 9 * l + 12)
                    nc.scalar.activation(gm_v[:, :, :], gm_v[:, :, :], ACT.Gelu_apprx_tanh).then_inc(gelu_v_done, 1)
                    act.wait_ge(gelu_v_done, l + 1)
                    order(nc.scalar.activation(hm[:, 0, :], gm_v[:, 0, :], ACT.Square, accum_out=gssq[:, 0:1]))
                    nc.scalar.activation(hm[:, 1, :], gm_v[:, 1, :], ACT.Square,
                                         accum_out=gssq[:, 1:2]).then_inc(gssq_ready, 1)

                def scale_q():
                    act.wait_ge(proj_evac, 9 * l + 4)
                    nc.scalar.mul(featT[:, 0], featT[:, 0], ATT_SCALE).then_inc(qk_scaled, 1)

                def log1p():
                    act.wait_ge(z_ready, l + 1)
                    rows = ls_rows[0:SMALL, :]
                    order(nc.scalar.activation(rows, z_rows[0:SMALL, :], ACT.Abs))
                    nc.scalar.activation(rows, rows, ACT.Exp, scale=-1.0).then_inc(expz_ready, 1)
                    act.wait_ge(exp1_ready, l + 1)
                    nc.scalar.activation(rows, rows, ACT.Ln).then_inc(lnz_ready, 1)

                def row_exp():
                    act.wait_ge(rows_ready, l + 1)
                    nc.scalar.activation(r_row[0:MH, :], r_row[0:MH, :], ACT.Exp).then_inc(rexp_ready, 1)

                def ml_silu():
                    act.wait_ge(conv_ready, l + 1)
                    nc.scalar.activation(mlqk[:, :, :], mlqk[:, :, :], ACT.Silu).then_inc(mlqk_ready, 1)

                def ml_out_gate():
                    act.wait_ge(proj_evac, 9 * l + 10)
                    order(nc.scalar.activation(so, so, ACT.Tanh, scale=0.5))
                    nc.scalar.activation(so, so, ACT.Copy, scale=0.5, bias=0.5).then_inc(so_ready, 1)

                def ml_decay():
                    act.wait_ge(decay_done, l + 1)
                    nc.scalar.activation(w_intra, ps[:, 6:8, :], ACT.Exp).then_inc(w_intra_ready, 1)

                def ml_k_tok():
                    act.wait_ge(k_turned, l + 1)
                    nc.scalar.copy(k_tok, ps[:, 1, :]).then_inc(k_tok_ready, 1)

                def ml_state():
                    act.wait_ge(state_done, l + 1)
                    nc.scalar.copy(c_state, ps[:, 1, :]).then_inc(c_state_ready, 1)

                def ml_squares():
                    act.wait_ge(h_num_ready, l + 1)
                    nc.scalar.activation(ml_y, scr[:, 2560:3584], ACT.Square).then_inc(hsq_ready, 1)

                def ml_hi():
                    act.wait_ge(ml_y_ready, l + 1)
                    nc.scalar.copy(yT_hi[:, 1].rearrange("p c t -> p (c t)"), ml_y).then_inc(ml_hi_ready, 1)

                def gm_hi():
                    act.wait_ge(gm_y_ready, l + 1)
                    nc.scalar.copy(yT_hi[:, 2].rearrange("p c t -> p (c t)"), gm_y).then_inc(gm_hi_ready, 1)

                def att_exp(p):
                    act.wait_ge(max_ready, 4 * l + p + 1)
                    for e in range(2):
                        for t in range(2):
                            src = ps[:, 2 + e, 0:256] if t else ps[:, 2 + e, 256:384]
                            dst = prob[:, 512 * e:512 * e + 256] if t else prob[:, 512 * e + 256:512 * e + 384]
                            c = 4 * (p % 2) + 2 * e + t
                            nc.scalar.activation(dst, src, ACT.Exp, bias=negmax[:, c:c + 1],
                                                 accum_out=rsum[:, c:c + 1]).then_inc(prob_ready, 1)

                def att_probT(p):
                    act.wait_ge(p_turned, 4 * l + p + 1)
                    dst = probT.rearrange("p (e n) -> p e n", e=2)[:, :, 0:384]
                    nc.scalar.copy(dst, ps[:, 2:4, 0:384]).then_inc(probT_ready, 1)

                def att_yT():
                    act.wait_ge(y_turned, l + 1)
                    nc.scalar.copy(yT_hi[:, 0].rearrange("p c t -> p (c t)"),
                                   ps[:, 2:4, :].rearrange("p b n -> p (b n)")).then_inc(att_hi_ready, 1)

                work = {1: [log1p], 2: [row_exp], 4: [scale_q], 14: [ml_silu], 16: [ml_out_gate], 18: [gm_gelu_u],
                        19: [ml_decay], 20: [lambda: att_exp(0), ml_k_tok], 21: [lambda: att_probT(0), ml_state],
                        22: [gm_gelu_v], 23: [ml_squares, lambda: att_exp(1)], 24: [lambda: att_probT(1), ml_hi],
                        25: [gm_hi], 26: [lambda: att_exp(2)], 27: [lambda: att_probT(2)],
                        29: [lambda: att_exp(3)], 30: [lambda: att_probT(3)], 33: [att_yT]}
                for i in range(U_OUT - U_SMALL):
                    step(U_SMALL + i, lambda i=i: [f() for f in work.get(i, [])])
                turn_in(4 * l + 2, MERGED_BANKS)
                for a in range(3):
                    split(l, U_OUT + a + RING)
                squares(3 * l + 2)
                split(l, U_FFN2 - 1 + RING)
                turn_in(4 * l + 3)
                ffn(l, 2 * l + 1, U_FFN2)
                order.end()
            squares(3 * DEPTH)

        @block.vector
        def _(dve):
            dve.sem_inc(lo_ready, RING)

            def split(layer, j, turn=0, width=2048):
                slot = j % RING
                dve.wait_ge(hi_ready, UNITS * layer + j + RING * turn + 1)
                nc.vector.tensor_tensor(w_lo[:, slot, 0:width], w_raw[:, slot, 0:width],
                                        w_hi[:, slot, 0:width].bitcast(F32), ALU.subtract).then_inc(lo_ready, 1)

            def pe_has(layer, j, turn=0):
                dve.wait_ge(unit_done, UNITS * layer + j + RING * turn + RING + 1)

            def residual(l, n, last_unit):
                for t in range(NT):
                    if t == 0:
                        dve.wait_ge(acc0_done, n)
                    else:
                        pe_has(l, last_unit)
                    nc.vector.scalar_tensor_tensor(
                        out=xs[:, t, :], in0=ps[:, 2 * t:2 * t + 2, :].rearrange("p b n -> p (b n)"), scalar=0.5,
                        in1=xs[:, t, :], op0=ALU.mult, op1=ALU.add).then_inc(x_ready, 1)

            def norm(n):
                dve.wait_ge(gain_loaded, 16 * (n + 1))
                for t in range(NT):
                    dve.wait_ge(rstd_ready, 2 * n + t + 1)
                    nc.vector.scalar_tensor_tensor(out=xhat[:, t, :], in0=xs[:, t, :], scalar=rstd[:, t:t + 1],
                                                   in1=gain[:, :], op0=ALU.mult, op1=ALU.mult).then_inc(xhat_ready, 1)

            def turn_in(group, banks=TURN_BANKS):
                for i in range(4):
                    t, q = i // 2, i % 2
                    dve.wait_ge(xT_hi_ready, 4 * group + i + 1)
                    src = ps[:, banks[t] + q, :].rearrange("p (c n) -> p c n", c=4)
                    sl = (slice(None), slice(4 * q, 4 * q + 4), slice(t * P, (t + 1) * P))
                    nc.vector.tensor_tensor(xT_lo[sl], src, xT_hi[sl].bitcast(F32), ALU.subtract).then_inc(xT_lo_ready, 1)

            def hidden(call, t):
                for i in range(NT):
                    dve.wait_ge(silu_done, 2 * NB * call + 2 * t + i + 1)
                    nc.vector.tensor_tensor(h[:, i, :], ps[:, 4 + i, WB:2 * WB], silu[:, i, :], ALU.mult).then_inc(h_ready, 1)

            def hT(call, t, last=0):
                dve.wait_ge(hT_hi_ready, NB * call + t + 1)
                nc.vector.tensor_tensor(hT_lo[last], ps[:, 6 + last, :].rearrange("p (k n) -> p k n", k=2),
                                        hT_hi[last].bitcast(F32), ALU.subtract).then_inc(hT_lo_ready, 1)

            def ffn(l, call, b, next_width=2048):
                split(l, b + RING)
                hidden(call, 0)
                split(l, b + 1 + RING)

                def block(t):
                    hT(call, t - 1)
                    split(l, b + 2, t)
                    hidden(call, t)
                with dve.Fori(1, NB - 1, 1) as t:
                    block(t)
                    split(l, b + 3, t)
                    split(l, b + 4, t)
                block(NB - 1)
                hT(call, NB - 1, 1)
                split(l, b + FFN_UNITS, 0, next_width)

            dve.wait_ge(x_loaded, 32)
            dve.sem_inc(x_ready, NT)
            split(0, 0)
            nc.vector.memset(ones[:, :], 1.0).then_inc(par_ready, 1)
            dve.wait_ge(par_turned, 1)
            nc.vector.tensor_copy(wsT[:, :, :].rearrange("p g s -> p (g s)"),
                                  ps[:, 0:2, :].rearrange("p b n -> p (b n)")).then_inc(par_ready, 1)
            nc.vector.tensor_copy(cols[:, :], ps[:, 2, 0:DEPTH * PROWS]).then_inc(par_ready, 1)
            dve.wait_ge(par_ready, 3)

            DVE_PER_LAYER = 44
            with dve.Fori(0, DEPTH, 1) as l:
                order = Chain(dve, dve_chain, l, DVE_PER_LAYER)
                norm(3 * l)
                turn_in(4 * l)
                order(nc.vector.tensor_copy(lcol[:, :], cols[:, bass.ds(l * PROWS, PROWS)]))
                order(nc.vector.tensor_copy(lb[:, :], bcol[:, bass.ds(l, 1)]))
                for j in (1, 2):
                    split(l, j)
                ffn(l, 2 * l, 0, 4 * SMALL)
                residual(l, 3 * l + 1, FFN_UNITS - 1)
                norm(3 * l + 1)
                split(l, FFN_UNITS + 1, 0, 4 * SMALL)
                turn_in(4 * l + 1)
                split(l, FFN_UNITS - 1 + RING)

                def conv(chunks):
                    dve.wait_ge(proj_evac, 9 * l + 3 + 4 + chunks[0] // MH)
                    taps = [lcol[:, 2 * MH + j * KD:2 * MH + (j + 1) * KD] for j in range(NTAP)]
                    for j in reversed(range(NTAP)):
                        back = NTAP - 1 - j
                        for c in chunks:
                            if back == 0:
                                ins = nc.vector.tensor_scalar(mlqk[:, c, :], ml_raw[:, c, :], taps[j][:, c:c + 1], None, ALU.mult)
                            else:
                                ins = nc.vector.scalar_tensor_tensor(
                                    out=mlqk[:, c, back:], in0=ml_raw[:, c, 0:S - back], scalar=taps[j][:, c:c + 1],
                                    in1=mlqk[:, c, back:], op0=ALU.mult, op1=ALU.add)
                            if c == chunks[-1] and (j > 0 or chunks[-1] < 2 * MH - 1):
                                order(ins)
                            elif c == chunks[-1]:
                                ins.then_inc(conv_ready, 1)

                def gm_scale_v():
                    dve.wait_ge(grstd_ready, l + 1)
                    for t in range(NT):
                        ins = nc.vector.tensor_scalar(gm_v[:, t, :], gm_v[:, t, :], grstd[:, t:t + 1], None, ALU.mult)
                    ins.then_inc(vhat_ready, 1)

                def log_sigmoid():
                    pe_has(l, U_SMALL + 1)
                    dve.wait_ge(par_ready, 4)
                    nc.vector.tensor_scalar(z_rows[0:SMALL, :], ps[0:SMALL, 7, 0:S], lb[0:SMALL, 0:1], None, ALU.add).then_inc(z_ready, 1)
                    dve.wait_ge(expz_ready, l + 1)
                    nc.vector.tensor_scalar(ls_rows[0:SMALL, :], ls_rows[0:SMALL, :], 1.0, None, ALU.add).then_inc(exp1_ready, 1)
                    dve.wait_ge(lnz_ready, l + 1)
                    nc.vector.scalar_tensor_tensor(out=ls_rows[0:SMALL, :], in0=z_rows[0:SMALL, :], scalar=0.0,
                                                   in1=ls_rows[0:SMALL, :], op0=ALU.min, op1=ALU.subtract).then_inc(ls_ready, 1)

                def row_scans():
                    lf, li = ls_rows[MF:MF + MH, :], li_row[0:MH, :]
                    b, g_, m = b_row[0:MH, :], g_row[0:MH, :], negm[0:MH, :]
                    dve.wait_ge(ls_ready, l + 1)
                    order(nc.vector.tensor_copy(li, z_rows[MI:MI + MH, :]))
                    nc.vector.tensor_tensor_scan(b[:, 0:P], lf[:, 0:P], lf[:, 0:P], 0.0, ALU.add, ALU.bypass)
                    order(nc.vector.tensor_tensor_scan(b[:, P:S], lf[:, P:S], lf[:, P:S], 0.0, ALU.add, ALU.bypass))
                    order(nc.vector.tensor_tensor(g_, li, b, ALU.subtract))
                    order(nc.vector.tensor_tensor_scan(m[:, 0:P], g_[:, 0:P], g_[:, 0:P], 0.0, ALU.max, ALU.bypass))
                    order(nc.vector.tensor_tensor(m_prev, b[:, P - 1:P], m[:, P - 1:P], ALU.add))
                    order(nc.vector.tensor_tensor_scan(m[:, P:S], g_[:, P:S], g_[:, P:S], m_prev, ALU.max, ALU.bypass))
                    nc.vector.scalar_tensor_tensor(out=r_row[0:MH, 0:S], in0=b, scalar=-1.0, in1=m, op0=ALU.mult, op1=ALU.subtract)
                    nc.vector.tensor_scalar(r_row[0:MH, S:S + P], m[:, P:S], -1.0, m_prev, ALU.mult, ALU.add)
                    order(nc.vector.tensor_scalar(r_row[0:MH, S + P:2 * S], g_[:, 0:P], m[:, P - 1:P], None, ALU.subtract))
                    nc.vector.tensor_scalar(m, m, -1.0, None, ALU.mult).then_inc(rows_ready, 1)
                    order(nc.vector.tensor_tensor_scan(negc[AF:AF + AH, :], ls_rows[AF:AF + AH, :], ls_rows[AF:AF + AH, :], 0.0, ALU.add, ALU.bypass))
                    nc.vector.tensor_scalar(negc[AF:AF + AH, :], negc[AF:AF + AH, :], -1.0, None, ALU.mult).then_inc(negc_ready, 1)

                def gm_mix():
                    dve.wait_ge(spatial_done, l + 1)
                    for g4 in range(4):
                        src = ps[:, 6 + g4 // 2, 256 * (g4 % 2):256 * (g4 % 2) + 256].rearrange("p (c t) -> p c t", c=2)
                        bias = bsp[:, bass.ds(4 * l + g4, 1), :].to_broadcast([P, 2, P])
                        ins = nc.vector.scalar_tensor_tensor(
                            out=gm_y[:, 256 * g4:256 * g4 + 256].rearrange("p (c t) -> p c t", c=2), in0=src,
                            scalar=lcol[:, MH + g4:MH + g4 + 1], in1=bias, op0=ALU.mult, op1=ALU.add)
                    ins.then_inc(gm_gained, 1)
                    dve.wait_ge(gm_gained, l + 1)
                    dve.wait_ge(gelu_u_done, l + 1)
                    nc.vector.tensor_tensor(gm_y, gm_y, gm_u, ALU.mult).then_inc(gm_y_ready, 1)

                def ml_rows_turned():
                    dve.wait_ge(rT_done, l + 1)
                    nc.vector.tensor_copy(tok16[:, :, :].rearrange("p k h -> p (k h)"), ps[:, 0, 0:4 * MH]).then_inc(rT_ready, 1)
                    dve.wait_ge(rT_ready, l + 1)
                    order(nc.vector.tensor_scalar(w_inter, tok16[:, 2, :], ML_SCALE, None, ALU.mult))

                def gm_lo():
                    dve.wait_ge(gm_hi_ready, l + 1)
                    nc.vector.tensor_tensor(yT_lo[:, 2].rearrange("p c t -> p (c t)"), gm_y,
                                            yT_hi[:, 2].rearrange("p c t -> p (c t)").bitcast(F32), ALU.subtract).then_inc(gm_lo_ready, 1)

                def ml_weights():
                    vw = v_w.rearrange("p (h n) -> p h n", h=MH)
                    ws = tok16[:, 3, :].unsqueeze(2).to_broadcast([P, MH, P])
                    nc.vector.tensor_tensor(vw, ml_v[:, 0, :].rearrange("p (h n) -> p h n", h=MH), ws, ALU.mult).then_inc(v_w_ready, 1)
                    dve.wait_ge(kq_done, l + 1)
                    dve.wait_ge(w_intra_ready, l + 1)
                    for c, bank in ((0, 0), (1, 6)):
                        ins = nc.vector.scalar_tensor_tensor(out=w_intra[:, c, :], in0=ps[:, bank, :], scalar=ML_SCALE,
                                                             in1=w_intra[:, c, :], op0=ALU.mult, op1=ALU.mult)
                    ins.then_inc(qk_ready, 1)

                def ml_n_state():
                    dve.wait_ge(state_done, l + 1)
                    nc.vector.tensor_copy(n_state, ps[:, 7, 0:MH]).then_inc(n_state_ready, 1)

                def ml_outputs():
                    dve.wait_ge(inter_done, l + 1)
                    heads = lambda ap: ap.rearrange("p (h n) -> p h n", h=MH)
                    wide = lambda ap: ap.unsqueeze(2).to_broadcast([P, MH, P])
                    order(nc.vector.tensor_tensor(dtmp, ps[:, 7, 16:20], w_inter, ALU.mult))
                    nc.vector.tensor_copy(den[:, 0:MH], ps[:, 7, 8:12])
                    order(nc.vector.tensor_tensor(den[:, MH:2 * MH], ps[:, 7, 12:16], dtmp, ALU.add))
                    order(nc.vector.tensor_scalar(rden, den, -1.0, None, ALU.mult))
                    order(nc.vector.tensor_tensor(den, den, rden, ALU.max))
                    order(nc.vector.tensor_tensor(den, den, tok16[:, 0:2, :].rearrange("p k h -> p (k h)"), ALU.max))
                    nc.vector.reciprocal(rden, den).then_inc(dve_chain, 1)
                    order.n += 1
                    nc.vector.tensor_tensor(heads(hm[:, 1, :]), heads(ps[:, 1, :]), wide(w_inter), ALU.mult).then_inc(dve_chain, 1)
                    order.n += 1
                    dve.wait_ge(dve_chain, order.base + order.n)
                    order(nc.vector.tensor_tensor(hm[:, 1, :], hm[:, 1, :], ps[:, 6, :], ALU.add))
                    nc.vector.tensor_tensor(heads(hm[:, 0, :]), heads(ps[:, 0, :]), wide(rden[:, 0:MH]), ALU.mult)
                    nc.vector.tensor_tensor(heads(hm[:, 1, :]), heads(hm[:, 1, :]), wide(rden[:, MH:2 * MH]), ALU.mult).then_inc(h_num_ready, 1)

                def ml_head_norm():
                    dve.wait_ge(hsq_ready, l + 1)
                    nc.vector.tensor_reduce(hssq, ml_y.rearrange("p (h n) -> p h n", h=2 * MH), AX.X, ALU.add).then_inc(hssq_ready, 1)
                    dve.wait_ge(hrstd_ready, l + 1)
                    all_h = scr[:, 2560:3584].rearrange("p (h n) -> p h n", h=2 * MH)
                    nc.vector.tensor_tensor(all_h, all_h, hrstd.unsqueeze(2).to_broadcast([P, 2 * MH, P]), ALU.mult).then_inc(hn_ready, 1)

                def ml_gain():
                    dve.wait_ge(ml_turned, l + 1)
                    dve.wait_ge(so_ready, l + 1)
                    for c in range(MH):
                        sl = slice(256 * c, 256 * c + 256)
                        ins = nc.vector.scalar_tensor_tensor(out=ml_y[:, sl], in0=ps[:, c // 2, 256 * (c % 2):256 * (c % 2) + 256],
                                                             scalar=lcol[:, c:c + 1], in1=so[:, sl], op0=ALU.mult, op1=ALU.mult)
                    ins.then_inc(ml_y_ready, 1)

                def ml_lo():
                    dve.wait_ge(ml_hi_ready, l + 1)
                    nc.vector.tensor_tensor(yT_lo[:, 1].rearrange("p c t -> p (c t)"), ml_y,
                                            yT_hi[:, 1].rearrange("p c t -> p (c t)").bitcast(F32), ALU.subtract).then_inc(ml_lo_ready, 1)

                def att_max(p):
                    dve.wait_ge(score_done, 4 * l + p + 1)
                    nm = negmax[:, 4 * (p % 2):4 * (p % 2) + 4].rearrange("p (e t) -> p e t", e=2)
                    nc.vector.tensor_reduce(nm[:, :, 1:2], ps[:, 2:4, 0:256], AX.X, ALU.max, negate=True)
                    nc.vector.tensor_reduce(nm[:, :, 0:1], ps[:, 2:4, 256:384], AX.X, ALU.max, negate=True).then_inc(max_ready, 1)

                def att_y(p):
                    c = 4 * (p % 2)
                    dve.wait_ge(prob_ready, 16 * l + 4 * p + 4)
                    order(nc.vector.reciprocal(rinv[:, c:c + 4], rsum[:, c:c + 4]))
                    dve.wait_ge(pv_done, 4 * l + p + 1)
                    for t in range(NT):
                        r = rinv[:, c:c + 4].rearrange("p (e t) -> p e t", e=2)[:, :, t:t + 1].to_broadcast([P, 2, DH])
                        dst = y_tok[:, t, 128 * p:128 * p + 128].rearrange("p (e d) -> p e d", e=2)
                        ins = nc.vector.tensor_tensor(dst, ps[:, 2:4, 384 + DH * t:384 + DH * t + DH], r, ALU.mult)
                    ins.then_inc(y_tok_ready, 1)

                def att_yT():
                    dve.wait_ge(att_hi_ready, l + 1)
                    nc.vector.tensor_tensor(yT_lo[:, 0].rearrange("p c t -> p (c t)"),
                                            ps[:, 2:4, :].rearrange("p b n -> p (b n)"),
                                            yT_hi[:, 0].rearrange("p c t -> p (c t)").bitcast(F32), ALU.subtract).then_inc(att_lo_ready, 1)

                def merge(r, o):
                    t, half = o // 2, o % 2
                    if o < 3:
                        dve.wait_ge(br_done, 9 * l + 3 * r + o + 1)
                    else:
                        pe_has(l, U_BR + 2 * r + 1)
                    g = gates[:, 2 * (2 - r) + half, t, :]
                    dst = merged[:, t, 512 * half:512 * half + 512]
                    first = dst if r == 0 else mtmp[:, o % 2, :]
                    nc.vector.scalar_tensor_tensor(out=first, in0=g, scalar=1.0, in1=ps[:, 4 + o, :],
                                                   op0=ALU.add, op1=ALU.mult).then_inc(br_evac, 1)
                    if r:
                        dve.wait_ge(br_evac, 12 * l + 4 * r + o + 1)
                        ins = nc.vector.tensor_tensor(dst, dst, mtmp[:, o % 2, :], ALU.add)
                        if r == 2 and half:
                            ins.then_inc(merged_ready, 1)
                        else:
                            order(ins)

                work = {1: [log_sigmoid], 2: [row_scans], 10: [lambda: conv([0, 1])], 11: [lambda: conv([2, 3])],
                        12: [lambda: conv([4, 5])], 13: [lambda: conv([6, 7])], 19: [ml_rows_turned],
                        20: [lambda: att_max(0), ml_weights], 21: [ml_n_state], 22: [lambda: att_y(0), gm_scale_v, ml_outputs],
                        23: [lambda: att_max(1), ml_head_norm], 24: [ml_gain, ml_lo], 25: [lambda: att_y(1), gm_mix, gm_lo],
                        26: [lambda: att_max(2)], 28: [lambda: att_y(2)], 29: [lambda: att_max(3)],
                        31: [lambda: att_y(3)], 33: [att_yT],
                        32: [lambda o=o: merge(0, o) for o in range(4)],
                        34: [lambda o=o: merge(1, o) for o in range(4)],
                        36: [lambda o=o: merge(2, o) for o in range(4)]}
                for i in range(U_OUT - U_SMALL - 1):
                    split(l, U_SMALL + i + RING)
                    for f in work.get(i, []):
                        f()
                turn_in(4 * l + 2, MERGED_BANKS)
                for j in range(U_OUT - 1, U_OUT + 2):
                    split(l, j + RING)
                residual(l, 3 * l + 2, U_FFN2 - 1)
                norm(3 * l + 2)
                turn_in(4 * l + 3)
                for j in range(U_OUT + 2, U_OUT + 4):
                    split(l, j + RING)
                ffn(l, 2 * l + 1, U_FFN2)
                residual(l, 3 * l + 3, UNITS - 1)
                order.end()
            norm(3 * DEPTH)

        @block.tensor
        def _(pe):
            pe.sem_inc(unit_done, RING)

            def mm3(dst, x_hi, x_lo, w_h, w_l, first, last, feature_major=False):
                for i, (a, b) in enumerate(((x_hi, w_h), (x_hi, w_l), (x_lo, w_h))):
                    if feature_major:
                        a, b = b, a
                    ins = nc.tensor.matmul(dst, a, b, start=first and i == 0, stop=last and i == 2, skip_group_check=True)
                return ins

            def begin(layer, j, turn=0):
                pe.wait_ge(lo_ready, UNITS * layer + j + RING * turn + RING + 1)

            def tok_block(layer, j, half, bank, wait_tile, tile0_done, turn=0):
                begin(layer, j, turn)
                slot = j % RING
                for t in range(NT):
                    wait_tile(t)
                    for k in range(4):
                        xk = (slice(None), 4 * half + k, slice(t * P, (t + 1) * P))
                        wk = slice(512 * k, 512 * k + 512)
                        ins = mm3(ps[:, bank + t, :], xT_hi[xk], xT_lo[xk], w_hi[:, slot, wk], w_lo[:, slot, wk],
                                  half == 0 and k == 0, half == 1 and k == 3)
                    if half == 1 and t == 0:
                        ins.then_inc(tile0_done, 1)
                ins.then_inc(unit_done, 1)

            def turn(src, t, ready, banks=TURN_BANKS):
                ready(t)
                for q in range(2):
                    for c in range(4):
                        ins = nc.tensor.transpose(ps[:, banks[t] + q, P * c:P * c + P],
                                                  src[:, t, P * (4 * q + c):P * (4 * q + c) + P], ident[:, :])
                    ins.then_inc(xT_turned, 1)

            def norm(n):
                for t in range(NT):
                    turn(xhat, t, lambda t: pe.wait_ge(xhat_ready, 2 * n + t + 1))

            def have_xT(group, i):
                pe.wait_ge(xT_lo_ready, 4 * group + i + 1)

            def ffn(l, call, b, group):
                def down_tile(j, t, last):
                    slot = j % RING
                    for half in range(2):
                        for k in range(2):
                            hk = (slice(None), k, slice(t * P, (t + 1) * P))
                            wk = slice(1024 * k + 512 * half, 1024 * k + 512 * half + 512)
                            ins = mm3(ps[:, 2 * t + half, :], hT_hi[last][hk], hT_lo[last][hk], w_hi[:, slot, wk], w_lo[:, slot, wk],
                                      False, bool(last) and k == 1)
                    return ins

                def turn_h(last=0):
                    for k in range(2):
                        for t in range(NT):
                            ins = nc.tensor.transpose(ps[:, 6 + last, 256 * k + P * t:256 * k + P * t + P],
                                                      h[:, t, P * k:P * k + P], ident[:, :])
                    ins.then_inc(hT_turned, 1)

                def block(i):
                    tok_block(l, b + 2, 0, 4, lambda t: pe.wait_ge(h_ready, 2 * NB * call + 2 * i + t - 1), gu0_done, i - 1)
                    turn_h()
                    tok_block(l, b + 3, 1, 4, lambda t: None, gu0_done, i - 1)
                    pe.wait_ge(hT_lo_ready, NB * call + i)
                    begin(l, b + 4, i - 1)
                    down_tile(b + 4, 0, 0)

                tok_block(l, b, 0, 4, lambda t: have_xT(group, 2 * t), gu0_done)
                tok_block(l, b + 1, 1, 4, lambda t: have_xT(group, 2 * t + 1), gu0_done)
                with pe.Fori(1, NB - 1, 1) as i:
                    block(i)
                    down_tile(b + 4, 1, 0).then_inc(unit_done, 1)
                block(NB - 1)
                pe.wait_ge(h_ready, 2 * NB * call + 2 * NB)
                turn_h(1)
                down_tile(b + 4, 1, 0).then_inc(unit_done, 1)
                pe.wait_ge(hT_lo_ready, NB * call + NB)
                begin(l, b + FFN_UNITS - 1)
                down_tile(b + FFN_UNITS - 1, 0, 1).then_inc(acc0_done, 1)
                down_tile(b + FFN_UNITS - 1, 1, 1).then_inc(unit_done, 1)

            def clear_acc():
                for bank in range(4):
                    nc.tensor.matmul(ps[:, bank, :], zeros16[:, 0:P], zeros16[:, :], start=True, stop=True)

            pe.wait_ge(const_ready, 1)
            pe.wait_ge(par_loaded, 16 * (3 * DEPTH + 5))
            for g in range(DEPTH * 4):
                nc.tensor.transpose(ps[:, g // 4, P * (g % 4):P * (g % 4) + P], spat_in[:, g, :], ident[:, :])
            nc.tensor.transpose(ps[:, 2, 0:DEPTH * PROWS], prow, ident[0:DEPTH * PROWS, 0:DEPTH * PROWS]).then_inc(par_turned, 1)

            with pe.Fori(0, DEPTH, 1) as l:
                norm(3 * l)
                clear_acc()
                ffn(l, 2 * l, 0, 4 * l)
                norm(3 * l + 1)

                def feature_block(j, half, bank, turns):
                    begin(l, j, turns)
                    slot = j % RING
                    for c in range(4):
                        for k in range(4):
                            kk = 4 * half + k
                            wk = slice(512 * k + P * c, 512 * k + P * c + P)
                            ins = mm3(ps[:, bank + c // 2, 256 * (c % 2):256 * (c % 2) + 256], xT_hi[:, kk, :], xT_lo[:, kk, :],
                                      w_hi[:, slot, wk], w_lo[:, slot, wk], half == 0 and k == 0 and c % 2 == 0,
                                      half == 1 and k == 3, feature_major=True)
                    ins.then_inc(unit_done, 1)

                have_xT(4 * l + 1, 3)
                for half in range(2):
                    j = U_SMALL + half
                    begin(l, j)
                    for k in range(4):
                        wk = slice(SMALL * k, SMALL * k + SMALL)
                        ins = mm3(ps[0:SMALL, 7, 0:S], xT_hi[:, 4 * half + k, :], xT_lo[:, 4 * half + k, :],
                                  w_hi[:, j % RING, wk], w_lo[:, j % RING, wk], half == 0 and k == 0, half == 1 and k == 3,
                                  feature_major=True)
                    ins.then_inc(unit_done, 1)

                with pe.Fori(0, 3, 1) as g:
                    for c in range(4):
                        if c % 2 == 0:
                            pe.wait_ge(proj_evac, 9 * l + 3 * g + c // 2 + 1)
                        feature_block(U_WI + c, c % 2, c - c % 2, 2 * g)
                    pe.wait_ge(proj_evac, 9 * l + 3 * g + 3)
                    tok_block(l, U_WI + 4, 0, 4, lambda t: None, gate0_done, 2 * g)
                    begin(l, U_WI + 5, 2 * g)
                    slot = (U_WI + 5) % RING
                    for t in range(NT):
                        for k in range(4):
                            xk = (slice(None), 4 + k, slice(t * P, (t + 1) * P))
                            wk = slice(512 * k, 512 * k + 512)
                            ins = mm3(ps[:, 4 + t, :], xT_hi[xk], xT_lo[xk], w_hi[:, slot, wk], w_lo[:, slot, wk], False, k == 3)
                    ins.then_inc(unit_done, 1)

                mm = nc.tensor.matmul

                def spatial():
                    pe.wait_ge(vhat_ready, l + 1)
                    for g4 in range(4):
                        for c in range(2):
                            ins = mm(ps[:, 6 + g4 // 2, 256 * (g4 % 2) + P * c:256 * (g4 % 2) + P * c + P],
                                     gm_v[:, c, P * g4:P * g4 + P],
                                     wsT[:, bass.ds(4 * l + g4, 1), :].rearrange("p o t -> p (o t)"), start=True, stop=True)
                    ins.then_inc(spatial_done, 1)

                def decay():
                    pe.wait_ge(rows_ready, l + 1)
                    pe.wait_ge(par_ready, 4)
                    pe.wait_ge(proj_evac, 9 * l + 11)
                    for c in range(2):
                        bank = ps[:, 6 + c, :]
                        mm(bank, g_row[:, P * c:P * c + P], head_sel[:, 0:MH, :].rearrange("p h t -> p (h t)"),
                           start=True, stop=False, skip_group_check=True)
                        for hd in range(MH):
                            mm(ps[:, 6 + c, P * hd:P * hd + P], head_sel[:, hd, :], negm[:, P * c:P * c + P],
                               start=False, stop=False, skip_group_check=True)
                            ins = mm(ps[:, 6 + c, P * hd:P * hd + P], ident16[:, :], mask_k[:, :],
                                     start=False, stop=True, skip_group_check=True)
                    ins.then_inc(decay_done, 1)
                    pe.wait_ge(rexp_ready, l + 1)
                    for k in range(4):
                        ins = mm(ps[:, 0, MH * k:MH * k + MH], r_row[0:MH, P * k:P * k + P], ident[0:MH, 0:MH], start=True, stop=True)
                    ins.then_inc(rT_done, 1)

                def key_query():
                    pe.wait_ge(mlqk_ready, l + 1)
                    pe.wait_ge(rT_ready, l + 1)
                    pe.wait_ge(w_intra_ready, l + 1)
                    for hd in range(MH):
                        ins = nc.tensor.transpose(ps[:, 1, P * hd:P * hd + P], mlqk[:, MH + hd, 0:P], ident[:, :])
                    ins.then_inc(k_turned, 1)
                    for c, bank in ((0, 0), (1, 6)):
                        for hd in range(MH):
                            ins = mm(ps[:, bank, P * hd:P * hd + P], mlqk[:, MH + hd, P * c:P * c + P],
                                     mlqk[:, hd, P * c:P * c + P], start=True, stop=True)
                    ins.then_inc(kq_done, 1)

                def state_intra():
                    pe.wait_ge(k_tok_ready, l + 1)
                    pe.wait_ge(v_w_ready, l + 1)
                    for hd in range(MH):
                        sl = slice(P * hd, P * hd + P)
                        mm(ps[:, 1, sl], k_tok[:, sl], v_w[:, sl], start=True, stop=True)
                        ins = mm(ps[:, 7, hd:hd + 1], k_tok[:, sl], tok16[:, 3, hd:hd + 1], start=True, stop=True)
                    ins.then_inc(state_done, 1)
                    pe.wait_ge(qk_ready, l + 1)
                    for c, bank in ((0, 0), (1, 6)):
                        for hd in range(MH):
                            sl = slice(P * hd, P * hd + P)
                            mm(ps[:, bank, sl], w_intra[:, c, sl], ml_v[:, c, sl], start=True, stop=True)

                def inter():
                    pe.wait_ge(c_state_ready, l + 1)
                    pe.wait_ge(n_state_ready, l + 1)
                    for c in range(2):
                        for hd in range(MH):
                            mm(ps[:, 7, 8 + 4 * c + hd:9 + 4 * c + hd], w_intra[:, c, P * hd:P * hd + P], ones[:, :],
                               start=True, stop=True)
                    for hd in range(MH):
                        mm(ps[:, 1, P * hd:P * hd + P], mlqk[:, hd, P:S], c_state[:, P * hd:P * hd + P], start=True, stop=True)
                        ins = mm(ps[:, 7, 16 + hd:17 + hd], mlqk[:, hd, P:S], n_state[:, hd:hd + 1], start=True, stop=True)
                    ins.then_inc(inter_done, 1)

                def turn_heads():
                    pe.wait_ge(hn_ready, l + 1)
                    for hd in range(MH):
                        for c in range(2):
                            ins = nc.tensor.transpose(ps[:, hd // 2, 256 * (hd % 2) + P * c:256 * (hd % 2) + P * c + P],
                                                      hm[:, c, P * hd:P * hd + P], ident[:, :])
                    ins.then_inc(ml_turned, 1)

                def score(p):
                    if p == 0:
                        pe.wait_ge(qk_scaled, l + 1)
                        pe.wait_ge(negc_ready, l + 1)
                    if p:
                        pe.wait_ge(y_tok_ready, 4 * l + p)
                    for e in range(2):
                        for t in range(NT):
                            dst = ps[:, 2 + e, 0:256] if t else ps[:, 2 + e, 256:384]
                            keys = P * (t + 1)
                            hp = slice(DH * e, DH * e + DH)
                            mm(dst, qT[hp, p, P * t:P * t + P], kT[hp, p, 0:keys], start=True, stop=False, skip_group_check=True)
                            mm(dst, head_sel[:, 2 * p + e, :], negc[:, 0:keys], start=False, stop=False, skip_group_check=True)
                            ins = mm(dst[:, keys - P:keys], ident16[:, :], mask_q[:, :], start=False, stop=True, skip_group_check=True)
                    ins.then_inc(score_done, 1)

                def turn_p(p):
                    pe.wait_ge(prob_ready, 16 * l + 4 * p + 4)
                    for e in range(2):
                        for i in range(3):
                            ins = nc.tensor.transpose(ps[:, 2 + e, P * i:P * i + P], prob[:, 512 * e + P * i:512 * e + P * i + P], ident[:, :])
                    ins.then_inc(p_turned, 1)

                def pv(p):
                    pe.wait_ge(probT_ready, 4 * l + p + 1)
                    for e in range(2):
                        hd = 2 * p + e
                        v = lambda c: att_v[:, c, DH * hd:DH * hd + DH]
                        pt = lambda i: probT[:, 512 * e + P * i:512 * e + P * i + P]
                        mm(ps[:, 2 + e, 384:384 + DH], pt(2), v(0), start=True, stop=True)
                        mm(ps[:, 2 + e, 384 + DH:512], pt(0), v(0), start=True, stop=False)
                        ins = mm(ps[:, 2 + e, 384 + DH:512], pt(1), v(1), start=False, stop=True)
                    ins.then_inc(pv_done, 1)

                def turn_y():
                    pe.wait_ge(y_tok_ready, 4 * l + 4)
                    for c in range(4):
                        for t in range(NT):
                            ins = nc.tensor.transpose(ps[:, 2 + c // 2, 256 * (c % 2) + P * t:256 * (c % 2) + P * t + P],
                                                      y_tok[:, t, P * c:P * c + P], ident[:, :])
                    ins.then_inc(y_turned, 1)

                work = {20: [lambda: score(0), key_query], 21: [lambda: turn_p(0), state_intra],
                        22: [lambda: pv(0), inter], 23: [lambda: score(1)], 24: [lambda: turn_p(1), turn_heads, spatial],
                        25: [lambda: pv(1)], 26: [lambda: score(2)], 27: [lambda: turn_p(2)], 28: [lambda: pv(2)],
                        29: [lambda: score(3)], 30: [lambda: turn_p(3)], 31: [lambda: pv(3)], 33: [turn_y]}
                decay()
                for b in range(NGATE):
                    for half in range(2):
                        def wait_tile(t):
                            if half == 0 and b == 0:
                                if t == 0:
                                    pe.wait_ge(proj_evac, 9 * l + 12)
                            elif half == 0:
                                pe.wait_ge(gate_evac, 12 * l + 2 * (b - 1) + t + 1)
                        tok_block(l, U_GATE + 2 * b + half, half, 4, wait_tile, gate0_done)
                        for f in work.get(U_GATE + 2 * b + half - U_SMALL, []):
                            f()

                for r, ready in enumerate((gm_lo_ready, ml_lo_ready, att_lo_ready)):
                    pe.wait_ge(ready, l + 1)
                    if r == 0:
                        pe.wait_ge(gate_evac, 12 * (l + 1))
                        pe.wait_ge(ml_y_ready, l + 1)
                    for a in range(2):
                        j = U_BR + 2 * r + a
                        begin(l, j)
                        for o in range(4):
                            t, half = o // 2, o % 2
                            if r and a == 0:
                                pe.wait_ge(br_evac, 12 * l + 4 * (r - 1) + o + 1)
                            for k in range(2):
                                yk = (slice(None), 2 - r, 2 * a + k, slice(t * P, (t + 1) * P))
                                wk = slice(1024 * k + 512 * half, 1024 * k + 512 * half + 512)
                                ins = mm3(ps[:, 4 + o, :], yT_hi[yk], yT_lo[yk], w_hi[:, j % RING, wk], w_lo[:, j % RING, wk],
                                          a == 0 and k == 0, a == 1 and k == 1)
                            if a == 1 and o < 3:
                                ins.then_inc(br_done, 1)
                        ins.then_inc(unit_done, 1)
                        for f in work.get(j - U_SMALL, []):
                            f()

                for t in range(NT):
                    turn(merged, t, lambda t: pe.wait_ge(merged_ready, 2 * l + t + 1), MERGED_BANKS)
                for a in range(4):
                    j = U_OUT + a
                    begin(l, j)
                    for t in range(NT):
                        have_xT(4 * l + 2, 2 * t + (a // 2))
                        for half in range(2):
                            for k in range(2):
                                xk = (slice(None), 2 * a + k, slice(t * P, (t + 1) * P))
                                wk = slice(1024 * k + 512 * half, 1024 * k + 512 * half + 512)
                                ins = mm3(ps[:, 2 * t + half, :], xT_hi[xk], xT_lo[xk], w_hi[:, j % RING, wk], w_lo[:, j % RING, wk],
                                          a == 0 and k == 0, a == 3 and k == 1)
                        if t == 0 and a == 3:
                            ins.then_inc(acc0_done, 1)
                    ins.then_inc(unit_done, 1)
                norm(3 * l + 2)
                clear_acc()
                ffn(l, 2 * l + 1, U_FFN2, 4 * l + 3)


_INS = ['x', 'norm_ffn1', 'ffn1_gate', 'ffn1_up', 'ffn1_down', 'norm_mix', 'w_in', 'b_f_att', 'b_i_ml', 'b_f_ml',
        'conv_ml', 'norm_ml_head', 'norm_gmlp', 'w_spatial', 'b_spatial', 'w_br_att', 'w_br_ml', 'w_br_gmlp',
        'w_out', 'norm_ffn2', 'ffn2_gate', 'ffn2_up', 'ffn2_down', 'norm_final']


def kernel(**inputs):
    import numpy as _np
    import concourse.bacc as _bacc
    from concourse import mybir as _mybir
    from concourse.bass_utils import run_bass_kernel_spmd as _run

    nc = _bacc.Bacc("TRN2", target_bir_lowering=False, num_devices=1, dynamic_dma_scratch_size=1024)
    arrays, args = {}, []
    for name in _INS:
        a = _np.ascontiguousarray(inputs[name])
        arrays[f"in_{name}_dram"] = a
        args.append(nc.dram_tensor(f"in_{name}_dram", a.shape, _mybir.dt.from_np(a.dtype), kind="ExternalInput").ap())
    shape = inputs["x"].shape
    args.append(nc.dram_tensor("out_0_dram", shape, _mybir.dt.float32, kind="ExternalOutput").ap())
    trunk(nc, *args)
    r = _run(nc, [arrays], core_ids=[0])
    return r.results[0]["out_0_dram"]
```

```python
from contextlib import ExitStack

import concourse.bass as bass
from concourse import mybir

F32 = mybir.dt.float32
F32R = mybir.dt.float32r
BF16 = mybir.dt.bfloat16
ALU = mybir.AluOpType
ACT = mybir.ActivationFunctionType
AX = mybir.AxisListType

P = 128
EPS = 1e-6
NEG = -1e30
RING = 3
LOAD_INC = 96


class Chain:

    def __init__(self, engine, sem, layer, per_layer):
        self.engine, self.sem, self.n, self.per_layer = engine, sem, 0, per_layer
        self.base = layer * per_layer

    def __call__(self, instruction):
        instruction.then_inc(self.sem, 1)
        self.n += 1
        self.engine.wait_ge(self.sem, self.base + self.n)

    def end(self):
        assert self.n == self.per_layer, (self.n, self.per_layer)


def trunk(nc, x, norm_ffn1, ffn1_gate, ffn1_up, ffn1_down, norm_mix, w_in, b_f_att, b_i_ml, b_f_ml,
          conv_ml, norm_ml_head, norm_gmlp, w_spatial, b_spatial, w_br_att, w_br_ml, w_br_gmlp,
          w_out, norm_ffn2, ffn2_gate, ffn2_up, ffn2_down, norm_final, out):
    DEPTH, D, DFF = ffn1_gate.shape
    S = x.shape[1]
    NT = S // P
    KD = D // P
    AH = b_f_att.shape[1]
    MH = b_i_ml.shape[1]
    AW, MW = w_br_att.shape[1], w_br_ml.shape[1]
    DH = AW // AH
    NTAP = conv_ml.shape[1]
    CB = 512
    WB = 256
    NB = DFF // WB
    NGATE = 3 * D // CB
    MF, MI, AF = 0, 32, 64
    SMALL = AF + AH
    HI, LO, AHI, ALO = 0, 32, 64, 96
    GROUP = 3 * CB + AH
    assert NT == 2 and KD == 8 and AW == MW == CB and AH == 2 * MH and DH == 64 and GROUP == 3 * CB + 2 * MH

    FFN_UNITS = 3 * NB
    U_SMALL = FFN_UNITS
    U_WI = U_SMALL + 2
    U_GATE = U_WI + 18
    U_BR = U_GATE + 2 * NGATE
    U_OUT = U_BR + 6
    U_FFN2 = U_OUT + 4
    UNITS = U_FFN2 + FFN_UNITS
    assert UNITS % RING == 0 and FFN_UNITS % RING == 0 and U_FFN2 % RING == 0
    ATT_SCALE = DH ** -0.5
    ML_SCALE = float(P) ** -0.5
    TURN_BANKS, MERGED_BANKS = (4, 6), (2, 4)
    PROWS = 2 * MH + NTAP * KD

    with ExitStack() as ctx:
        def sb(name, shape, dt=F32):
            return ctx.enter_context(nc.sbuf_tensor(name, shape, dt))

        def sem(name):
            return ctx.enter_context(nc.semaphore(name))

        ps = ctx.enter_context(nc.psum_tensor("ps", [P, 8, 512], F32))

        xs = sb("xs", [P, NT, D])
        xT_hi = sb("xT_hi", [P, KD, S], F32R)
        xT_lo = sb("xT_lo", [P, KD, S], F32R)
        w_raw = sb("w_raw", [P, RING, 2048])
        w_hi = sb("w_hi", [P, RING, 2048], F32R)
        w_lo = sb("w_lo", [P, RING, 2048], F32R)
        featT = sb("featT", [P, 6, 4, S])
        tokv = sb("tokv", [P, 3, NT, CB])
        gates = sb("gates", [P, NGATE, NT, CB])
        yT_hi = sb("yT_hi", [P, 3, 4, S], F32R)
        yT_lo = sb("yT_lo", [P, 3, 4, S], F32R)
        gain = sb("gain", [P, D])
        scr = sb("scr", [P, 3584])
        z_rows = sb("z_rows", [P, S])
        ls_rows = sb("ls_rows", [P, S])
        negc = sb("negc", [P, S])
        b_row = sb("b_row", [P, S])
        g_row = sb("g_row", [P, S])
        negm = sb("negm", [P, S])
        r_row = sb("r_row", [P, 2 * S])
        g_parts, m_parts, c_parts = sb("g_parts", [P, S], F32R), sb("m_parts", [P, S], F32R), sb("c_parts", [P, S], F32R)
        head_sel = sb("head_sel", [P, AH, P], F32R)
        bsp = sb("bsp", [P, 4, P])
        wsT = sb("wsT", [P, 4, P])
        lcol = sb("lcol", [P, PROWS])
        lb = sb("lb", [P, 1])
        ident = sb("ident", [P, P])
        ident16 = sb("ident16", [P, P], BF16)
        mask_q = sb("mask_q", [P, P], BF16)
        mask_k = sb("mask_k", [P, P], BF16)
        zeros16 = sb("zeros16", [P, 512], BF16)
        ones = sb("ones", [P, P])
        rstd_row = sb("rstd_row", [P, S])
        tok16 = sb("tok16", [P, 4, MH])
        tiny = sb("tiny", [P, 96])

        silu = gates[:, 0, 0, :].rearrange("p (t n) -> p t n", t=NT)
        h = gates[:, 0, 1, :].rearrange("p (t n) -> p t n", t=NT)
        hT_hi = [yT_hi[:, 0, i:i + 2, :] for i in (0, 2)]
        hT_lo = [yT_lo[:, 0, i:i + 2, :] for i in (0, 2)]
        xhat = scr[:, 0:2 * D].rearrange("p (t n) -> p t n", t=NT)
        merged = xhat
        mtmp = scr[:, 2048:3072].rearrange("p (a n) -> p a n", a=2)
        qT, kT = featT[:, 0], featT[:, 1]
        ml_raw = featT[:, 2:4].rearrange("p a c t -> p (a c) t")
        so = featT[:, 4].rearrange("p c t -> p (c t)")
        gm_u = featT[:, 5].rearrange("p c t -> p (c t)")
        att_v, ml_v, gm_v = tokv[:, 0], tokv[:, 1], tokv[:, 2]
        mlqk = gates[:, 4:6].rearrange("p b t n -> p (b t n)").rearrange("p (c t) -> p c t", c=2 * MH)
        k_tok, v_w = scr[:, 0:512], scr[:, 512:1024]
        w_intra = scr[:, 1024:2048].rearrange("p (c n) -> p c n", c=2)
        c_state = scr[:, 2048:2560]
        hm = scr[:, 2560:3584].rearrange("p (c n) -> p c n", c=2)
        gm_y = scr[:, 0:1024]
        ml_y = gates[:, 4].rearrange("p t n -> p (t n)")
        prob = featT[:, 2].rearrange("p c t -> p (c t)")
        probT = featT[:, 3].rearrange("p c t -> p (c t)")
        y_tok = tokv[:, 1]
        spat_in = gates[:, 1].rearrange("p t n -> p (t n)").rearrange("p (g s) -> p g s", s=P)[:, 0:4]
        prow = gates[0:PROWS, 2, 0, 0:P]
        squared = gates[:, 3:5].rearrange("p b t n -> p b (t n)")
        ssq, rstd = tiny[:, 0:2], tiny[:, 2:4]
        mhalf, eps_col = tiny[:, 4:5], tiny[:, 5:6]
        inv_width = {D: tiny[:, 6:7], CB: tiny[:, 7:8], P: tiny[:, 8:9]}
        gssq, grstd = tiny[:, 12:14], tiny[:, 14:16]
        negmax, rsum = tiny[:, 16:24], tiny[:, 24:32]
        rinv = tiny[:, 32:40]
        n_state = tiny[:, 40:44]
        w_inter = tiny[:, 44:48]
        den, rden = tiny[:, 48:56], tiny[:, 56:64]
        hssq, hrstd = tiny[:, 64:72], tiny[:, 72:80]
        m_prev = tiny[0:MH, 80:81]
        li_row = r_row[:, S:2 * S]
        dtmp, half_rstd = tiny[:, 84:88], tiny[:, 88:90]
        diag = gates[:, 5, 0, 0:S].rearrange("p (t n) -> p t n", t=NT)

        x_loaded, par_loaded, gain_loaded = sem("x_loaded"), sem("par_loaded"), sem("gain_loaded")
        raw_loaded = [sem(f"raw_loaded{i}") for i in range(RING)]
        bias_cleared = sem("bias_cleared")
        const_ready, masks_ready = sem("const_ready"), sem("masks_ready")
        par_turned, wsT_copied, wsT_ready = sem("par_turned"), sem("wsT_copied"), sem("wsT_ready")
        hi_ready = sem("hi_ready")
        lo_ready = sem("lo_ready")
        unit_done = sem("unit_done")
        y0_ready, y1_ready = sem("y0_ready"), sem("y1_ready")
        x_ready, ssq_ready, rstd_ready, xhat_ready = sem("x_ready"), sem("ssq_ready"), sem("rstd_ready"), sem("xhat_ready")
        ones_ready = sem("ones_ready")
        xT_turned, xT_hi_ready, xT_lo_ready = sem("xT_turned"), sem("xT_hi_ready"), sem("xT_lo_ready")
        acc_done = sem("acc_done")
        gu0_done, silu_done, h_ready = sem("gu0_done"), sem("silu_done"), sem("h_ready")
        hT_turned, hT_hi_ready, hT_lo_ready = sem("hT_turned"), sem("hT_hi_ready"), sem("hT_lo_ready")
        feat_evac, tok_evac = sem("feat_evac"), sem("tok_evac")
        diag_ready, rstd_row_done, rstd_row_ready = sem("diag_ready"), sem("rstd_row_done"), sem("rstd_row_ready")
        gate0_done, gate_evac = sem("gate0_done"), sem("gate_evac")
        br_done, br_evac, merged_ready = sem("br_done"), sem("br_evac"), sem("merged_ready")
        dve_chain, act_chain, pool_chain = sem("dve_chain"), sem("act_chain"), sem("pool_chain")
        gelu_v_done, gelu_u_done, gssq_ready, grstd_ready, vhat_ready = (
            sem("gelu_v_done"), sem("gelu_u_done"), sem("gssq_ready"), sem("grstd_ready"), sem("vhat_ready"))
        z_ready, expz_ready, exp1_ready, lnz_ready, ls_ready = (
            sem("z_ready"), sem("expz_ready"), sem("exp1_ready"), sem("lnz_ready"), sem("ls_ready"))
        spatial_done, gm_gained, gm_y_ready, gm_hi_ready, gm_lo_ready = (
            sem("spatial_done"), sem("gm_gained"), sem("gm_y_ready"), sem("gm_hi_ready"), sem("gm_lo_ready"))
        rows_ready, rexp_ready, conv_ready, mlqk_ready = sem("rows_ready"), sem("rexp_ready"), sem("conv_ready"), sem("mlqk_ready")
        decay_done, rT_done, w_intra_ready, rT_ready = sem("decay_done"), sem("rT_done"), sem("w_intra_ready"), sem("rT_ready")
        kq_done, k_turned, k_tok_ready, qk_ready, v_w_ready = (
            sem("kq_done"), sem("k_turned"), sem("k_tok_ready"), sem("qk_ready"), sem("v_w_ready"))
        state_done, c_state_ready, n_state_ready = sem("state_done"), sem("c_state_ready"), sem("n_state_ready")
        inter_done, h_num_ready, hsq_ready, hssq_ready, hrstd_ready, hn_ready = (
            sem("inter_done"), sem("h_num_ready"), sem("hsq_ready"), sem("hssq_ready"), sem("hrstd_ready"), sem("hn_ready"))
        ml_turned, so_ready, ml_y_ready, ml_hi_ready, ml_lo_ready = (
            sem("ml_turned"), sem("so_ready"), sem("ml_y_ready"), sem("ml_hi_ready"), sem("ml_lo_ready"))
        score_done, max_ready, prob_ready, p_turned, probT_ready, pv_done, y_tok_ready = (
            sem("score_done"), sem("max_ready"), sem("prob_ready"), sem("p_turned"), sem("probT_ready"), sem("pv_done"), sem("y_tok_ready"))
        y_turned, att_hi_ready, att_lo_ready = sem("y_turned"), sem("att_hi_ready"), sem("att_lo_ready")
        negc_ready, out_stored = sem("negc_ready"), sem("out_stored")

        block = ctx.enter_context(nc.Block())

        @block.sync
        def _(sp):
            def at(ap, layer):
                return ap[bass.ds(layer, 1)]

            def load(layer, j, slot, parts, turn=0):
                sp.wait_ge(lo_ready, UNITS * layer + j + RING * turn + 1)
                for dst, src in parts:
                    sp.dma_start(dst, src).then_inc(raw_loaded[slot], LOAD_INC // len(parts))

            def gate_up(layer, j, slot, wg, wu, half, t, turn=0):
                dst = w_raw[:, slot, :].rearrange("p (k n) -> p k n", k=4)
                src = [at(w, layer).rearrange("o (k p) n -> p (o k) n", p=P)[:, 4 * half:4 * half + 4, bass.ds(t * WB, WB)]
                       for w in (wg, wu)]
                load(layer, j, slot, [(dst[:, :, 0:WB], src[0]), (dst[:, :, WB:2 * WB], src[1])], turn)

            def down(layer, j, slot, wd, t, turn=0):
                dst = w_raw[:, slot, :].rearrange("p (k n) -> p k n", k=2)
                src = at(wd, layer)[:, bass.ds(t * WB, WB), :].rearrange("o (k p) n -> p (o k) n", p=P)
                load(layer, j, slot, [(dst[:, k:k + 1, :], src[:, k:k + 1, :]) for k in range(2)], turn)

            def ffn_loads(layer, b, wg, wu, wd, after_first, before_last):
                gate_up(layer, b, b % RING, wg, wu, 0, 0)
                gate_up(layer, b + 1, (b + 1) % RING, wg, wu, 1, 0)
                after_first()
                with sp.Fori(1, NB, 1) as t:
                    gate_up(layer, b - 1, (b + 2) % RING, wg, wu, 0, t, t)
                    gate_up(layer, b, b % RING, wg, wu, 1, t, t)
                    down(layer, b + 1, (b + 1) % RING, wd, t - 1, t)
                before_last()
                down(layer, b + FFN_UNITS - 1, (b + FFN_UNITS - 1) % RING, wd, NB - 1)

            def load_gain(n, row):
                sp.wait_ge(xhat_ready, 4 * n)
                sp.dma_start(gain[:, :], row.partition_broadcast(P)).then_inc(gain_loaded, 16)

            def w_in_block(layer, j, slot, col, half, turn=0):
                dst = w_raw[:, slot, :].rearrange("p (k n) -> p k n", k=4)
                src = at(w_in, layer).rearrange("o (k p) n -> p (o k) n", p=P)[:, 4 * half:4 * half + 4, bass.ds(col, CB)]
                load(layer, j, slot, [(dst[:, k:k + 2, :], src[:, k:k + 2, :]) for k in (0, 2)], turn)

            def rows256(layer, j, slot, w, r):
                dst = w_raw[:, slot, :].rearrange("p (k n) -> p k n", k=2)
                src = at(w, layer)[:, r * 256:(r + 1) * 256, :].rearrange("o (k p) n -> p (o k) n", p=P)
                load(layer, j, slot, [(dst[:, k:k + 1, :], src[:, k:k + 1, :]) for k in range(2)])

            for t in range(NT):
                sp.dma_start(xs[:, t, :], x[0, t * P:(t + 1) * P, :]).then_inc(x_loaded, 16)
            with sp.Fori(0, DEPTH, 1) as l:
                sp.wait_ge(lo_ready, UNITS * l + 1)
                sp.dma_start(gain[:, :], at(norm_ffn1, l).rearrange("o n -> (o n)").partition_broadcast(P)).then_inc(gain_loaded, 16)

                def parameters():
                    small = [(prow[0:MH, :], at(norm_ml_head, l).rearrange("o (c p) -> (o c) p", p=P)),
                             (prow[MH:2 * MH, :], at(norm_gmlp, l).rearrange("o (c p) -> (o c) p", p=P)),
                             (prow[2 * MH:PROWS, :], at(conv_ml, l).rearrange("o j (c p) -> (o j c) p", p=P)),
                             (spat_in, at(w_spatial, l).rearrange("o g t s -> t (o g) s")),
                             (bsp[:, :, :], at(b_spatial, l).rearrange("o g t -> (o g t)").partition_broadcast(P).rearrange(
                                 "p (a t) -> p a t", t=P))]
                    for r, v in ((AF, b_f_att), (MI, b_i_ml), (MF, b_f_ml)):
                        small.append((lb[r:r + v.shape[1], :], at(v, l).rearrange("o h -> h o")))
                    sp.wait_ge(bias_cleared, 1)
                    with nc.allow_non_contiguous_dma(reason="a bias per head"):
                        for dst, src in small:
                            sp.dma_start(dst, src).then_inc(par_loaded, 16)

                ffn_loads(l, 0, ffn1_gate, ffn1_up, ffn1_down, parameters,
                          lambda: load_gain(3 * l + 1, at(norm_mix, l).rearrange("o n -> (o n)")))
                for half in range(2):
                    j = U_SMALL + half
                    dst = w_raw[:, j % RING, 0:4 * SMALL].rearrange("p (k n) -> p k n", k=4)
                    src = at(w_in, l).rearrange("o (k p) n -> p (o k) n", p=P)[:, 4 * half:4 * half + 4, :]
                    ca, cm = 3 * CB, GROUP + 3 * CB
                    with nc.allow_non_contiguous_dma(reason="16 gate columns"):
                        load(l, j, j % RING, [(dst[:, :, AF:AF + AH], src[:, :, ca:ca + AH]),
                                              (dst[:, :, MF:MF + MH], src[:, :, cm + MH:cm + 2 * MH]),
                                              (dst[:, :, MI:MI + MH], src[:, :, cm:cm + MH])])
                with sp.Fori(0, 3, 1) as g:
                    for c in range(6):
                        w_in_block(l, U_WI + c, (U_WI + c) % RING, g * GROUP + (c // 2) * CB, c % 2, 2 * g)
                for b in range(2 * NGATE):
                    w_in_block(l, U_GATE + b, (U_GATE + b) % RING, 2 * GROUP + 3 * CB + (b // 2) * CB, b % 2)
                for r, w in enumerate((w_br_gmlp, w_br_ml, w_br_att)):
                    for a in range(2):
                        rows256(l, U_BR + 2 * r + a, (U_BR + 2 * r + a) % RING, w, a)
                load_gain(3 * l + 2, at(norm_ffn2, l).rearrange("o n -> (o n)"))
                for a in range(4):
                    rows256(l, U_OUT + a, (U_OUT + a) % RING, w_out, a)
                ffn_loads(l, U_FFN2, ffn2_gate, ffn2_up, ffn2_down, lambda: None, lambda: None)
            load_gain(3 * DEPTH, norm_final)
            for j in range(1):
                sp.wait_ge(lo_ready, UNITS * DEPTH + j + 1)
                src = ffn1_gate[0, j * P:(j + 1) * P, 0:2048]
                for k in range(2):
                    sp.dma_start(w_raw[:, j, k * 1024:(k + 1) * 1024], src[:, k * 1024:(k + 1) * 1024]).then_inc(raw_loaded[j], LOAD_INC // 2)
            for j in range(1):
                sp.wait_ge(raw_loaded[j], LOAD_INC * (UNITS * DEPTH // RING + 1))
            for t, ready in enumerate((y0_ready, y1_ready)):
                sp.wait_ge(ready, 1)
                sp.dma_start(out[0, t * P:(t + 1) * P, :], xhat[:, t, :]).then_inc(out_stored, 16)
            sp.wait_ge(out_stored, 16 * NT)

        @block.gpsimd
        def _(pool):
            steps = [0]

            def chain(ins):
                ins.then_inc(pool_chain, 1)
                steps[0] += 1
                pool.wait_ge(pool_chain, steps[0])

            nc.gpsimd.memset(lb[:, :], 0.0).then_inc(bias_cleared, 1)
            chain(nc.gpsimd.memset(ident[:, :], 0.0))
            chain(nc.gpsimd.affine_select(out=ident[:, :], in_=ident[:, :], compare_op=ALU.not_equal, fill=1.0,
                                          base=0, pattern=[[-1, P]], channel_multiplier=1))
            nc.gpsimd.memset(zeros16[:, :], 0.0).then_inc(const_ready, 1)
            chain(nc.gpsimd.memset(mhalf, -0.5))
            chain(nc.gpsimd.memset(eps_col, EPS))
            for width, col in inv_width.items():
                chain(nc.gpsimd.memset(col, 1.0 / width))
            def inv_root(order, dst, src, width, ready):
                shape = [P, src.shape[1]]
                order(nc.gpsimd.tensor_tensor(src, src, inv_width[width].to_broadcast(shape), ALU.mult))
                order(nc.gpsimd.tensor_tensor(src, src, eps_col.to_broadcast(shape), ALU.add))
                nc.gpsimd.tensor_tensor(dst, src, mhalf.to_broadcast(shape), ALU.pow).then_inc(ready, 1)

            def norm(order, n):
                for t in range(NT):
                    pool.wait_ge(ssq_ready, 2 * n + t + 1)
                    inv_root(order, rstd[:, t:t + 1], ssq[:, t:t + 1], D, rstd_ready)

            norm(chain, 0)
            chain(nc.gpsimd.tensor_copy(ident16[:, :], ident[:, :]))
            chain(nc.gpsimd.memset(mask_q[:, :], 0.0))
            chain(nc.gpsimd.affine_select(out=mask_q[:, :], in_=mask_q[:, :], compare_op=ALU.is_ge, fill=NEG,
                                          base=0, pattern=[[-1, P]], channel_multiplier=1))
            chain(nc.gpsimd.memset(mask_k[:, :], 0.0))
            chain(nc.gpsimd.affine_select(out=mask_k[:, :], in_=mask_k[:, :], compare_op=ALU.is_ge, fill=NEG,
                                          base=0, pattern=[[1, P]], channel_multiplier=-1))
            ones_at = scr[:, 2048:2048 + AH * P].rearrange("p (h t) -> p h t", h=AH)
            chain(nc.gpsimd.memset(ones_at, 0.0))
            for parts in (g_parts, m_parts, c_parts):
                chain(nc.gpsimd.tensor_copy(parts[:, :], scr[:, 2048:2048 + S]))
            for first in (HI, LO, AHI, ALO):
                chain(nc.gpsimd.affine_select(out=ones_at, in_=ones_at, compare_op=ALU.not_equal,
                                              fill=1.0, base=-first, pattern=[[-1, AH], [0, P]], channel_multiplier=1))
            chain(nc.gpsimd.tensor_copy(head_sel[:, :, :], ones_at))
            for rows in (z_rows, ls_rows):
                chain(nc.gpsimd.memset(rows[:, :], 0.0))
            pool.sem_inc(masks_ready, 1)

            base = steps[0]
            with pool.Fori(0, DEPTH, 1) as l:
                order = Chain(pool, pool_chain, l, 16)
                order.base = l * 16 + base
                norm(order, 3 * l + 1)
                pool.wait_ge(gssq_ready, l + 1)
                inv_root(order, grstd, gssq, CB, grstd_ready)
                nc.gpsimd.affine_select(out=wsT[:, :, :], in_=wsT[:, :, :], compare_op=ALU.is_ge, fill=0.0,
                                        base=0, pattern=[[0, 4], [1, P]], channel_multiplier=-1).then_inc(wsT_ready, 1)
                pool.wait_ge(hssq_ready, l + 1)
                inv_root(order, hrstd, hssq, P, hrstd_ready)
                norm(order, 3 * l + 2)
                norm(order, 3 * l + 3)
                order.end()

        @block.scalar
        def _(act):
            def split(layer, j, turn=0, width=2048):
                slot = j % RING
                act.wait_ge(raw_loaded[slot], LOAD_INC * (UNITS // RING * layer + j // RING + turn + 1))
                act.wait_ge(unit_done, UNITS * layer + j + RING * turn + 1)
                nc.scalar.copy(w_hi[:, slot, 0:width], w_raw[:, slot, 0:width]).then_inc(hi_ready, 1)

            def pe_has(layer, j, turn=0):
                act.wait_ge(unit_done, UNITS * layer + j + RING * turn + RING + 1)

            def turn_in(group, banks=TURN_BANKS, parts=range(4)):
                for i in parts:
                    t, q = i // 2, i % 2
                    act.wait_ge(xT_turned, 4 * group + i + 1)
                    src = ps[:, banks[t] + q, :].rearrange("p (c n) -> p c n", c=4)
                    nc.scalar.copy(xT_hi[:, 4 * q:4 * q + 4, t * P:(t + 1) * P], src).then_inc(xT_hi_ready, 1)

            def squares(n, tiles=(0, 1)):
                for t in tiles:
                    act.wait_ge(x_ready, 2 * n + t + 1)
                    nc.scalar.activation(squared[:, t, :], xs[:, t, :], ACT.Square,
                                         accum_out=ssq[:, t:t + 1]).then_inc(ssq_ready, 1)

            def silus(layer, call, b, t):
                act.wait_ge(gu0_done, NB * call + t + 1)
                nc.scalar.activation(silu[:, 0, :], ps[:, 4, 0:WB], ACT.Silu, scale=rstd[:, 0:1]).then_inc(silu_done, 1)

            def load_silu():
                nc.scalar.activation(tiny[:, 90:91], ident[:, 0:1], ACT.Silu)

            def silu1():
                nc.scalar.activation(silu[:, 1, :], ps[:, 5, 0:WB], ACT.Silu, scale=rstd[:, 1:2]).then_inc(silu_done, 1)

            def hT(call, t, last=0):
                act.wait_ge(hT_turned, NB * call + t + 1)
                nc.scalar.copy(hT_hi[last], ps[:, 6 + last, :].rearrange("p (k n) -> p k n", k=2)).then_inc(hT_hi_ready, 1)

            def ffn(l, call, b, n, next_width=2048):
                split(l, b + RING)
                act.wait_ge(rstd_ready, 2 * n + 2)
                silus(l, call, b, 0)
                pe_has(l, b + 1)
                silu1()
                split(l, b + 1 + RING)

                def block(t):
                    hT(call, t - 1)
                    split(l, b + 2, t)
                    silus(l, call, b, t)
                    pe_has(l, b, t)
                    silu1()
                with act.Fori(1, NB - 1, 1) as t:
                    block(t)
                    split(l, b + 3, t)
                    split(l, b + 4, t)
                block(NB - 1)
                hT(call, NB - 1, 1)
                split(l, b + FFN_UNITS, 0, next_width)

            act.sem_inc(tok_evac, 1)
            split(0, 0)

            with act.Fori(0, DEPTH, 1) as l:
                order = Chain(act, act_chain, l, 4)
                turn_in(4 * l)
                split(l, 1)
                squares(3 * l)
                load_silu()
                split(l, 2)
                ffn(l, 2 * l, 0, 3 * l, 4 * SMALL)
                split(l, FFN_UNITS + 1, 0, 4 * SMALL)
                squares(3 * l + 1, [0])
                turn_in(4 * l + 1, parts=(0,))
                squares(3 * l + 1, [1])
                turn_in(4 * l + 1, parts=(1, 2, 3))
                split(l, FFN_UNITS - 1 + RING)
                act.wait_ge(rstd_ready, 2 * (3 * l + 1) + 2)
                order(nc.scalar.mul(half_rstd, rstd, 0.5))

                def projection(g):
                    pe_has(l, U_WI + 5, 2 * g)
                    for t in range(NT):
                        ins = nc.scalar.activation(tokv[:, g, t, :], ps[:, 4 + t, :], ACT.Copy, scale=rstd[:, t:t + 1])
                    ins.then_inc(tok_evac, 1)

                def gate_tile(b, t):
                    nc.scalar.activation(gates[:, b, t, :], ps[:, 4 + t, :], ACT.Tanh, scale=half_rstd[:, t:t + 1]).then_inc(gate_evac, 1)

                def step(s, work):
                    if U_GATE <= s < U_BR and (s - U_GATE) % 2:
                        b = (s - U_GATE) // 2
                        if b == 4:
                            act.wait_ge(ml_lo_ready, l + 1)
                        act.wait_ge(gate0_done, NGATE * l + b + 1)
                        gate_tile(b, 0)
                        pe_has(l, s)
                        gate_tile(b, 1)
                    if U_WI <= s < U_GATE and (s - U_WI) % 6 == 5:
                        projection((s - U_WI) // 6)
                    split(l, s + RING)
                    work()

                def gm_gelu_u():
                    act.wait_ge(feat_evac, 6 * l + 8)
                    nc.scalar.activation(gm_u, gm_u, ACT.Gelu_apprx_tanh).then_inc(gelu_u_done, 1)

                def gm_gelu_v():
                    act.wait_ge(tok_evac, 3 * l + 4)
                    nc.scalar.activation(gm_v[:, :, :], gm_v[:, :, :], ACT.Gelu_apprx_tanh).then_inc(gelu_v_done, 1)
                    act.wait_ge(gelu_v_done, l + 1)
                    order(nc.scalar.activation(hm[:, 0, :], gm_v[:, 0, :], ACT.Square, accum_out=gssq[:, 0:1]))
                    nc.scalar.activation(hm[:, 1, :], gm_v[:, 1, :], ACT.Square,
                                         accum_out=gssq[:, 1:2]).then_inc(gssq_ready, 1)

                def rstd_rows():
                    act.wait_ge(rstd_row_done, l + 1)
                    nc.scalar.copy(rstd_row[:, :], ps[:, 5, 0:S]).then_inc(rstd_row_ready, 1)

                def log1p():
                    act.wait_ge(z_ready, l + 1)
                    rows = ls_rows[0:SMALL, :]
                    order(nc.scalar.activation(rows, z_rows[0:SMALL, :], ACT.Abs))
                    nc.scalar.activation(rows, rows, ACT.Exp, scale=-1.0).then_inc(expz_ready, 1)
                    act.wait_ge(exp1_ready, l + 1)
                    nc.scalar.activation(rows, rows, ACT.Ln).then_inc(lnz_ready, 1)

                def row_exp():
                    act.wait_ge(rows_ready, l + 1)
                    nc.scalar.activation(r_row[0:MH, :], r_row[0:MH, :], ACT.Exp).then_inc(rexp_ready, 1)

                def ml_silu():
                    act.wait_ge(conv_ready, l + 1)
                    nc.scalar.activation(mlqk[:, :, :], mlqk[:, :, :], ACT.Silu).then_inc(mlqk_ready, 1)

                def ml_out_gate():
                    act.wait_ge(feat_evac, 6 * l + 7)
                    order(nc.scalar.activation(so, so, ACT.Tanh, scale=0.5))
                    nc.scalar.activation(so, so, ACT.Copy, scale=0.5, bias=0.5).then_inc(so_ready, 1)

                def ml_decay():
                    act.wait_ge(decay_done, l + 1)
                    nc.scalar.activation(w_intra, ps[:, 6:8, :], ACT.Exp).then_inc(w_intra_ready, 1)

                def ml_k_tok():
                    act.wait_ge(k_turned, l + 1)
                    nc.scalar.copy(k_tok, ps[:, 1, :]).then_inc(k_tok_ready, 1)

                def ml_state():
                    act.wait_ge(state_done, l + 1)
                    nc.scalar.copy(c_state, ps[:, 1, :]).then_inc(c_state_ready, 1)

                def ml_squares():
                    act.wait_ge(h_num_ready, l + 1)
                    nc.scalar.activation(ml_y, scr[:, 2560:3584], ACT.Square).then_inc(hsq_ready, 1)

                def ml_hi():
                    act.wait_ge(ml_y_ready, l + 1)
                    nc.scalar.copy(yT_hi[:, 1].rearrange("p c t -> p (c t)"), ml_y).then_inc(ml_hi_ready, 1)

                def gm_hi():
                    act.wait_ge(gm_y_ready, l + 1)
                    nc.scalar.copy(yT_hi[:, 2].rearrange("p c t -> p (c t)"), gm_y).then_inc(gm_hi_ready, 1)

                def att_exp(p):
                    act.wait_ge(max_ready, 4 * l + p + 1)
                    for e in range(2):
                        for t in range(2):
                            src = ps[:, 2 + e, 0:256] if t else ps[:, 2 + e, 256:384]
                            dst = prob[:, 512 * e:512 * e + 256] if t else prob[:, 512 * e + 256:512 * e + 384]
                            c = 4 * (p % 2) + 2 * e + t
                            nc.scalar.activation(dst, src, ACT.Exp, bias=negmax[:, c:c + 1],
                                                 accum_out=rsum[:, c:c + 1]).then_inc(prob_ready, 1)

                def att_probT(p):
                    act.wait_ge(p_turned, 4 * l + p + 1)
                    dst = probT.rearrange("p (e n) -> p e n", e=2)[:, :, 0:384]
                    nc.scalar.copy(dst, ps[:, 2:4, 0:384]).then_inc(probT_ready, 1)

                def att_yT():
                    act.wait_ge(y_turned, l + 1)
                    nc.scalar.copy(yT_hi[:, 0].rearrange("p c t -> p (c t)"),
                                   ps[:, 2:4, :].rearrange("p b n -> p (b n)")).then_inc(att_hi_ready, 1)

                work = {1: [rstd_rows], 3: [log1p], 7: [row_exp], 14: [ml_silu], 16: [ml_out_gate], 18: [gm_gelu_u],
                        19: [ml_decay], 20: [lambda: att_exp(0), ml_k_tok], 21: [lambda: att_probT(0), ml_state],
                        22: [gm_gelu_v], 23: [lambda: att_exp(1)], 24: [lambda: att_probT(1), ml_squares],
                        26: [lambda: att_exp(2), ml_hi], 27: [lambda: att_probT(2)], 28: [gm_hi],
                        29: [lambda: att_exp(3)], 30: [lambda: att_probT(3)], 33: [att_yT]}
                for i in range(U_OUT - U_SMALL - 1):
                    step(U_SMALL + i, lambda i=i: [f() for f in work.get(i, [])])
                turn_in(4 * l + 2, MERGED_BANKS)
                for j in range(U_OUT - 1, U_OUT + 3):
                    split(l, j + RING)
                squares(3 * l + 2, [0])
                turn_in(4 * l + 3)
                squares(3 * l + 2, [1])
                load_silu()
                split(l, U_FFN2 - 1 + RING)
                ffn(l, 2 * l + 1, U_FFN2, 3 * l + 2)
                order.end()
            squares(3 * DEPTH)
            act.wait_ge(xhat_ready, 4 * 3 * DEPTH + 2)
            act.wait_ge(rstd_ready, 2 * 3 * DEPTH + 1)
            nc.scalar.activation(xhat[:, 0, :], xhat[:, 0, :], ACT.Copy, scale=rstd[:, 0:1]).then_inc(y0_ready, 1)

        @block.vector
        def _(dve):
            dve.sem_inc(lo_ready, RING)

            def split(layer, j, turn=0, width=2048):
                slot = j % RING
                dve.wait_ge(hi_ready, UNITS * layer + j + RING * turn + 1)
                nc.vector.tensor_tensor(w_lo[:, slot, 0:width], w_raw[:, slot, 0:width],
                                        w_hi[:, slot, 0:width].bitcast(F32), ALU.subtract).then_inc(lo_ready, 1)

            def pe_has(layer, j, turn=0):
                dve.wait_ge(unit_done, UNITS * layer + j + RING * turn + RING + 1)

            def residual(l, n, last_unit, t, q):
                if 2 * t + q < 3:
                    dve.wait_ge(acc_done, 3 * (n - 1) + 2 * t + q + 1)
                else:
                    pe_has(l, last_unit)
                sl = slice(512 * q, 512 * q + 512)
                ins = nc.vector.scalar_tensor_tensor(out=xs[:, t, sl], in0=ps[:, 2 * t + q, :], scalar=0.5, in1=xs[:, t, sl],
                                                     op0=ALU.mult, op1=ALU.add)
                if q == 1:
                    ins.then_inc(x_ready, 1)

            def have_x(n, t):
                dve.wait_ge(x_ready, 2 * n + t + 1)

            def gained(t, q):
                sl = slice(512 * q, 512 * q + 512)
                nc.vector.tensor_tensor(xhat[:, t, sl], xs[:, t, sl], gain[:, sl], ALU.mult).then_inc(xhat_ready, 1)

            def have_gain(n):
                dve.wait_ge(gain_loaded, 16 * (n + 1))

            def next_x(l, n, last_unit):
                for t in range(NT):
                    for q in range(2):
                        residual(l, n, last_unit, t, q)
                    if t == 0:
                        have_gain(n)
                    have_x(n, t)
                    for q in range(2):
                        gained(t, q)

            def lo_in(group, i, banks=TURN_BANKS):
                t, q = i // 2, i % 2
                dve.wait_ge(xT_hi_ready, 4 * group + i + 1)
                src = ps[:, banks[t] + q, :].rearrange("p (c n) -> p c n", c=4)
                sl = (slice(None), slice(4 * q, 4 * q + 4), slice(t * P, (t + 1) * P))
                nc.vector.tensor_tensor(xT_lo[sl], src, xT_hi[sl].bitcast(F32), ALU.subtract).then_inc(xT_lo_ready, 1)

            def hidden(call, t):
                for i in range(NT):
                    dve.wait_ge(silu_done, 2 * NB * call + 2 * t + i + 1)
                    nc.vector.scalar_tensor_tensor(out=h[:, i, :], in0=ps[:, 4 + i, WB:2 * WB], scalar=rstd[:, i:i + 1],
                                                   in1=silu[:, i, :], op0=ALU.mult, op1=ALU.mult).then_inc(h_ready, 1)

            def hT(call, t, last=0):
                dve.wait_ge(hT_hi_ready, NB * call + t + 1)
                nc.vector.tensor_tensor(hT_lo[last], ps[:, 6 + last, :].rearrange("p (k n) -> p k n", k=2),
                                        hT_hi[last].bitcast(F32), ALU.subtract).then_inc(hT_lo_ready, 1)

            def ffn(l, call, b, next_width=2048):
                hidden(call, 0)
                split(l, b + RING)
                split(l, b + 1 + RING)

                def block(t):
                    hT(call, t - 1)
                    split(l, b + 2, t)
                    hidden(call, t)
                with dve.Fori(1, NB - 1, 1) as t:
                    block(t)
                    split(l, b + 3, t)
                    split(l, b + 4, t)
                block(NB - 1)
                hT(call, NB - 1, 1)
                split(l, b + FFN_UNITS, 0, next_width)

            dve.wait_ge(x_loaded, 32)
            dve.sem_inc(x_ready, NT)
            dve.sem_inc(feat_evac, 2)
            nc.vector.memset(ones[:, :], 1.0).then_inc(ones_ready, 1)
            have_gain(0)
            for t in range(NT):
                for q in range(2):
                    gained(t, q)
            split(0, 0)

            DVE_PER_LAYER = 46
            with dve.Fori(0, DEPTH, 1) as l:
                order = Chain(dve, dve_chain, l, DVE_PER_LAYER)
                for i in range(4):
                    lo_in(4 * l, i)
                for j in (1, 2):
                    split(l, j)
                ffn(l, 2 * l, 0, 4 * SMALL)
                split(l, FFN_UNITS + 1, 0, 4 * SMALL)
                n = 3 * l + 1
                next_x(l, n, FFN_UNITS - 1)
                for i in range(4):
                    lo_in(4 * l + 1, i)
                dve.wait_ge(rstd_ready, 2 * n + 2)
                for t in range(NT):
                    ins = nc.vector.tensor_scalar(diag[:, t, :], ident[:, :], rstd[:, t:t + 1], None, ALU.mult)
                ins.then_inc(diag_ready, 1)
                split(l, FFN_UNITS - 1 + RING)

                def projection(c, g):
                    pe_has(l, U_WI + 2 * c + 1, 2 * g)
                    if c == 0 and g == 0:
                        dve.wait_ge(rstd_row_ready, l + 1)
                    nc.vector.scalar_tensor_tensor(
                        out=featT[:, 2 * g + c], in0=ps[:, 2 * c:2 * c + 2, :].rearrange("p b (h t) -> p (b h) t", h=2),
                        scalar=ATT_SCALE if c == 0 and g == 0 else 1.0, in1=rstd_row[:, :].unsqueeze(1).to_broadcast([P, 4, S]),
                        op0=ALU.mult, op1=ALU.mult).then_inc(feat_evac, 1)

                def conv(chunks):
                    dve.wait_ge(feat_evac, 6 * l + 2 + 3 + chunks[0] // MH)
                    taps = [lcol[:, 2 * MH + j * KD:2 * MH + (j + 1) * KD] for j in range(NTAP)]
                    for j in reversed(range(NTAP)):
                        back = NTAP - 1 - j
                        for c in chunks:
                            if back == 0:
                                ins = nc.vector.tensor_scalar(mlqk[:, c, :], ml_raw[:, c, :], taps[j][:, c:c + 1], None, ALU.mult)
                            else:
                                ins = nc.vector.scalar_tensor_tensor(
                                    out=mlqk[:, c, back:], in0=ml_raw[:, c, 0:S - back], scalar=taps[j][:, c:c + 1],
                                    in1=mlqk[:, c, back:], op0=ALU.mult, op1=ALU.add)
                            if c == chunks[-1] and (j > 0 or chunks[-1] < 2 * MH - 1):
                                order(ins)
                            elif c == chunks[-1]:
                                ins.then_inc(conv_ready, 1)

                def gm_scale_v():
                    dve.wait_ge(grstd_ready, l + 1)
                    for t in range(NT):
                        ins = nc.vector.tensor_scalar(gm_v[:, t, :], gm_v[:, t, :], grstd[:, t:t + 1], None, ALU.mult)
                    ins.then_inc(vhat_ready, 1)

                def parameters():
                    dve.wait_ge(par_turned, l + 1)
                    nc.vector.tensor_copy(lcol[:, :], ps[:, 7, 0:PROWS])
                    nc.vector.tensor_copy(wsT[:, :, :].rearrange("p g s -> p (g s)"), ps[:, 6, :]).then_inc(wsT_copied, 1)

                def log_sigmoid():
                    pe_has(l, U_SMALL + 1)
                    dve.wait_ge(par_loaded, 16 * 8 * (l + 1))
                    dve.wait_ge(masks_ready, 1)
                    dve.wait_ge(rstd_row_ready, l + 1)
                    order(nc.vector.tensor_tensor(z_rows[0:SMALL, :], ps[0:SMALL, 4, 0:S], rstd_row[0:SMALL, :], ALU.mult))
                    nc.vector.tensor_scalar(z_rows[0:SMALL, :], z_rows[0:SMALL, :], lb[0:SMALL, 0:1], None, ALU.add).then_inc(z_ready, 1)
                    dve.wait_ge(expz_ready, l + 1)
                    nc.vector.tensor_scalar(ls_rows[0:SMALL, :], ls_rows[0:SMALL, :], 1.0, None, ALU.add).then_inc(exp1_ready, 1)
                    dve.wait_ge(lnz_ready, l + 1)
                    nc.vector.scalar_tensor_tensor(out=ls_rows[0:SMALL, :], in0=z_rows[0:SMALL, :], scalar=0.0,
                                                   in1=ls_rows[0:SMALL, :], op0=ALU.min, op1=ALU.subtract).then_inc(ls_ready, 1)

                def parts(dst, src, hi, lo):
                    n = src.shape[0]
                    order(nc.vector.tensor_copy(dst[hi:hi + n, :], src))
                    return nc.vector.tensor_tensor(dst[lo:lo + n, :], src, dst[hi:hi + n, :].bitcast(F32), ALU.subtract)

                def row_scans():
                    lf, li = ls_rows[MF:MF + MH, :], li_row[0:MH, :]
                    b, g_, m = b_row[0:MH, :], g_row[0:MH, :], negm[0:MH, :]
                    dve.wait_ge(ls_ready, l + 1)
                    order(nc.vector.tensor_copy(li, z_rows[MI:MI + MH, :]))
                    nc.vector.tensor_tensor_scan(b[:, 0:P], lf[:, 0:P], lf[:, 0:P], 0.0, ALU.add, ALU.bypass)
                    order(nc.vector.tensor_tensor_scan(b[:, P:S], lf[:, P:S], lf[:, P:S], 0.0, ALU.add, ALU.bypass))
                    order(nc.vector.tensor_tensor(g_, li, b, ALU.subtract))
                    order(nc.vector.tensor_tensor_scan(m[:, 0:P], g_[:, 0:P], g_[:, 0:P], 0.0, ALU.max, ALU.bypass))
                    order(nc.vector.tensor_tensor(m_prev, b[:, P - 1:P], m[:, P - 1:P], ALU.add))
                    order(nc.vector.tensor_tensor_scan(m[:, P:S], g_[:, P:S], g_[:, P:S], m_prev, ALU.max, ALU.bypass))
                    nc.vector.scalar_tensor_tensor(out=r_row[0:MH, 0:S], in0=b, scalar=-1.0, in1=m, op0=ALU.mult, op1=ALU.subtract)
                    nc.vector.tensor_scalar(r_row[0:MH, S:S + P], m[:, P:S], -1.0, m_prev, ALU.mult, ALU.add)
                    order(nc.vector.tensor_scalar(r_row[0:MH, S + P:2 * S], g_[:, 0:P], m[:, P - 1:P], None, ALU.subtract))
                    order(nc.vector.tensor_scalar(m, m, -1.0, None, ALU.mult))
                    parts(g_parts, g_, HI, LO)
                    parts(m_parts, m, HI, LO).then_inc(rows_ready, 1)
                    order(nc.vector.tensor_tensor_scan(negc[AF:AF + AH, :], ls_rows[AF:AF + AH, :], ls_rows[AF:AF + AH, :], 0.0, ALU.add, ALU.bypass))
                    order(nc.vector.tensor_scalar(negc[AF:AF + AH, :], negc[AF:AF + AH, :], -1.0, None, ALU.mult))
                    parts(c_parts, negc[AF:AF + AH, :], AHI, ALO).then_inc(negc_ready, 1)

                def gm_mix():
                    dve.wait_ge(spatial_done, l + 1)
                    for g4 in range(4):
                        src = ps[:, 6 + g4 // 2, 256 * (g4 % 2):256 * (g4 % 2) + 256].rearrange("p (c t) -> p c t", c=2)
                        bias = bsp[:, g4:g4 + 1, :].to_broadcast([P, 2, P])
                        ins = nc.vector.scalar_tensor_tensor(
                            out=gm_y[:, 256 * g4:256 * g4 + 256].rearrange("p (c t) -> p c t", c=2), in0=src,
                            scalar=lcol[:, MH + g4:MH + g4 + 1], in1=bias, op0=ALU.mult, op1=ALU.add)
                    ins.then_inc(gm_gained, 1)
                    dve.wait_ge(gm_gained, l + 1)
                    dve.wait_ge(gelu_u_done, l + 1)
                    nc.vector.tensor_tensor(gm_y, gm_y, gm_u, ALU.mult).then_inc(gm_y_ready, 1)

                def ml_rows_turned():
                    dve.wait_ge(rT_done, l + 1)
                    nc.vector.tensor_copy(tok16[:, :, :].rearrange("p k h -> p (k h)"), ps[:, 0, 0:4 * MH]).then_inc(rT_ready, 1)
                    dve.wait_ge(rT_ready, l + 1)
                    order(nc.vector.tensor_scalar(w_inter, tok16[:, 2, :], ML_SCALE, None, ALU.mult))

                def gm_lo():
                    dve.wait_ge(gm_hi_ready, l + 1)
                    nc.vector.tensor_tensor(yT_lo[:, 2].rearrange("p c t -> p (c t)"), gm_y,
                                            yT_hi[:, 2].rearrange("p c t -> p (c t)").bitcast(F32), ALU.subtract).then_inc(gm_lo_ready, 1)

                def ml_weights():
                    vw = v_w.rearrange("p (h n) -> p h n", h=MH)
                    ws = tok16[:, 3, :].unsqueeze(2).to_broadcast([P, MH, P])
                    nc.vector.tensor_tensor(vw, ml_v[:, 0, :].rearrange("p (h n) -> p h n", h=MH), ws, ALU.mult).then_inc(v_w_ready, 1)
                    dve.wait_ge(kq_done, l + 1)
                    dve.wait_ge(w_intra_ready, l + 1)
                    for c, bank in ((0, 0), (1, 6)):
                        ins = nc.vector.scalar_tensor_tensor(out=w_intra[:, c, :], in0=ps[:, bank, :], scalar=ML_SCALE,
                                                             in1=w_intra[:, c, :], op0=ALU.mult, op1=ALU.mult)
                    ins.then_inc(qk_ready, 1)

                def ml_n_state():
                    dve.wait_ge(state_done, l + 1)
                    nc.vector.tensor_copy(n_state, ps[:, 7, 0:MH]).then_inc(n_state_ready, 1)

                def ml_outputs():
                    dve.wait_ge(inter_done, l + 1)
                    heads = lambda ap: ap.rearrange("p (h n) -> p h n", h=MH)
                    wide = lambda ap: ap.unsqueeze(2).to_broadcast([P, MH, P])
                    order(nc.vector.tensor_tensor(dtmp, ps[:, 7, 16:20], w_inter, ALU.mult))
                    nc.vector.tensor_copy(den[:, 0:MH], ps[:, 7, 8:12])
                    order(nc.vector.tensor_tensor(den[:, MH:2 * MH], ps[:, 7, 12:16], dtmp, ALU.add))
                    order(nc.vector.tensor_scalar(rden, den, -1.0, None, ALU.mult))
                    order(nc.vector.tensor_tensor(den, den, rden, ALU.max))
                    order(nc.vector.tensor_tensor(den, den, tok16[:, 0:2, :].rearrange("p k h -> p (k h)"), ALU.max))
                    nc.vector.reciprocal(rden, den).then_inc(dve_chain, 1)
                    order.n += 1
                    nc.vector.tensor_tensor(heads(hm[:, 1, :]), heads(ps[:, 1, :]), wide(w_inter), ALU.mult).then_inc(dve_chain, 1)
                    order.n += 1
                    dve.wait_ge(dve_chain, order.base + order.n)
                    order(nc.vector.tensor_tensor(hm[:, 1, :], hm[:, 1, :], ps[:, 6, :], ALU.add))
                    nc.vector.tensor_tensor(heads(hm[:, 0, :]), heads(ps[:, 0, :]), wide(rden[:, 0:MH]), ALU.mult)
                    nc.vector.tensor_tensor(heads(hm[:, 1, :]), heads(hm[:, 1, :]), wide(rden[:, MH:2 * MH]), ALU.mult).then_inc(h_num_ready, 1)

                def ml_head_norm():
                    dve.wait_ge(hsq_ready, l + 1)
                    nc.vector.tensor_reduce(hssq, ml_y.rearrange("p (h n) -> p h n", h=2 * MH), AX.X, ALU.add).then_inc(hssq_ready, 1)
                    dve.wait_ge(hrstd_ready, l + 1)
                    all_h = scr[:, 2560:3584].rearrange("p (h n) -> p h n", h=2 * MH)
                    nc.vector.tensor_tensor(all_h, all_h, hrstd.unsqueeze(2).to_broadcast([P, 2 * MH, P]), ALU.mult).then_inc(hn_ready, 1)

                def ml_gain():
                    dve.wait_ge(ml_turned, l + 1)
                    dve.wait_ge(so_ready, l + 1)
                    for c in range(MH):
                        sl = slice(256 * c, 256 * c + 256)
                        ins = nc.vector.scalar_tensor_tensor(out=ml_y[:, sl], in0=ps[:, c // 2, 256 * (c % 2):256 * (c % 2) + 256],
                                                             scalar=lcol[:, c:c + 1], in1=so[:, sl], op0=ALU.mult, op1=ALU.mult)
                    ins.then_inc(ml_y_ready, 1)

                def ml_lo():
                    dve.wait_ge(ml_hi_ready, l + 1)
                    nc.vector.tensor_tensor(yT_lo[:, 1].rearrange("p c t -> p (c t)"), ml_y,
                                            yT_hi[:, 1].rearrange("p c t -> p (c t)").bitcast(F32), ALU.subtract).then_inc(ml_lo_ready, 1)

                def att_max(p):
                    dve.wait_ge(score_done, 4 * l + p + 1)
                    nm = negmax[:, 4 * (p % 2):4 * (p % 2) + 4].rearrange("p (e t) -> p e t", e=2)
                    nc.vector.tensor_reduce(nm[:, :, 1:2], ps[:, 2:4, 0:256], AX.X, ALU.max, negate=True)
                    nc.vector.tensor_reduce(nm[:, :, 0:1], ps[:, 2:4, 256:384], AX.X, ALU.max, negate=True).then_inc(max_ready, 1)

                def att_y(p):
                    c = 4 * (p % 2)
                    dve.wait_ge(prob_ready, 16 * l + 4 * p + 4)
                    order(nc.vector.reciprocal(rinv[:, c:c + 4], rsum[:, c:c + 4]))
                    dve.wait_ge(pv_done, 4 * l + p + 1)
                    for t in range(NT):
                        r = rinv[:, c:c + 4].rearrange("p (e t) -> p e t", e=2)[:, :, t:t + 1].to_broadcast([P, 2, DH])
                        dst = y_tok[:, t, 128 * p:128 * p + 128].rearrange("p (e d) -> p e d", e=2)
                        ins = nc.vector.tensor_tensor(dst, ps[:, 2:4, 384 + DH * t:384 + DH * t + DH], r, ALU.mult)
                    ins.then_inc(y_tok_ready, 1)

                def att_yT():
                    dve.wait_ge(att_hi_ready, l + 1)
                    nc.vector.tensor_tensor(yT_lo[:, 0].rearrange("p c t -> p (c t)"),
                                            ps[:, 2:4, :].rearrange("p b n -> p (b n)"),
                                            yT_hi[:, 0].rearrange("p c t -> p (c t)").bitcast(F32), ALU.subtract).then_inc(att_lo_ready, 1)

                def merge(r, o):
                    t, half = o // 2, o % 2
                    if o < 3:
                        dve.wait_ge(br_done, 9 * l + 3 * r + o + 1)
                    else:
                        pe_has(l, U_BR + 2 * r + 1)
                    g = gates[:, 2 * (2 - r) + half, t, :]
                    dst = merged[:, t, 512 * half:512 * half + 512]
                    first = dst if r == 0 else mtmp[:, o % 2, :]
                    nc.vector.scalar_tensor_tensor(out=first, in0=g, scalar=1.0, in1=ps[:, 4 + o, :],
                                                   op0=ALU.add, op1=ALU.mult).then_inc(br_evac, 1)
                    if r:
                        dve.wait_ge(br_evac, 12 * l + 4 * r + o + 1)
                        ins = nc.vector.tensor_tensor(dst, dst, mtmp[:, o % 2, :], ALU.add)
                        if r == 2:
                            ins.then_inc(merged_ready, 1)
                        else:
                            order(ins)

                work = {3: [parameters, log_sigmoid], 6: [row_scans], 10: [lambda: conv([0, 1])], 11: [lambda: conv([2, 3])],
                        12: [lambda: conv([4, 5])], 13: [lambda: conv([6, 7])], 19: [ml_rows_turned],
                        20: [lambda: att_max(0), ml_weights], 21: [ml_n_state], 22: [lambda: att_y(0), gm_scale_v],
                        23: [lambda: att_max(1), ml_outputs], 24: [ml_head_norm], 25: [lambda: att_y(1)],
                        26: [lambda: att_max(2), ml_gain], 27: [ml_lo, gm_mix], 28: [lambda: att_y(2), gm_lo], 29: [lambda: att_max(3)],
                        31: [lambda: att_y(3)], 33: [att_yT],
                        32: [lambda o=o: merge(0, o) for o in range(4)],
                        34: [lambda o=o: merge(1, o) for o in range(4)],
                        36: [lambda o=o: merge(2, o) for o in range(4)]}
                for i in range(U_OUT - U_SMALL - 1):
                    if i != 36:
                        split(l, U_SMALL + i + RING)
                    w = U_SMALL + i - U_WI
                    if 0 <= w < 18 and w % 6 in (1, 3):
                        projection(w % 6 // 2, w // 6)
                    for f in work.get(i, []):
                        f()
                for i in range(4):
                    lo_in(4 * l + 2, i, MERGED_BANKS)
                for j in range(U_OUT - 2, U_OUT + 2):
                    split(l, j + RING)
                next_x(l, 3 * l + 2, U_FFN2 - 1)
                for i in range(4):
                    lo_in(4 * l + 3, i)
                for j in range(U_OUT + 2, U_OUT + 4):
                    split(l, j + RING)
                ffn(l, 2 * l + 1, U_FFN2)
                next_x(l, 3 * l + 3, UNITS - 1)
                order.end()
            dve.wait_ge(xhat_ready, 4 * 3 * DEPTH + 4)
            dve.wait_ge(rstd_ready, 2 * 3 * DEPTH + 2)
            nc.vector.tensor_scalar(xhat[:, 1, :], xhat[:, 1, :], rstd[:, 1:2], None, ALU.mult).then_inc(y1_ready, 1)

        @block.tensor
        def _(pe):
            pe.sem_inc(unit_done, RING)

            def mm3(dst, x_hi, x_lo, w_h, w_l, first, last, feature_major=False):
                for i, (a, b) in enumerate(((x_hi, w_h), (x_hi, w_l), (x_lo, w_h))):
                    if feature_major:
                        a, b = b, a
                    ins = nc.tensor.matmul(dst, a, b, start=first and i == 0, stop=last and i == 2, skip_group_check=True)
                return ins

            def begin(layer, j, turn=0):
                pe.wait_ge(lo_ready, UNITS * layer + j + RING * turn + RING + 1)

            def tok_block(layer, j, half, bank, wait_tile, tile0_done, turn=0):
                begin(layer, j, turn)
                slot = j % RING
                for t in range(NT):
                    wait_tile(t)
                    for k in range(4):
                        xk = (slice(None), 4 * half + k, slice(t * P, (t + 1) * P))
                        wk = slice(512 * k, 512 * k + 512)
                        ins = mm3(ps[:, bank + t, :], xT_hi[xk], xT_lo[xk], w_hi[:, slot, wk], w_lo[:, slot, wk],
                                  half == 0 and k == 0, half == 1 and k == 3)
                    if half == 1 and t == 0:
                        ins.then_inc(tile0_done, 1)
                ins.then_inc(unit_done, 1)

            def turn(src, t, q, banks=TURN_BANKS):
                for c in range(4):
                    ins = nc.tensor.transpose(ps[:, banks[t] + q, P * c:P * c + P],
                                              src[:, t, P * (4 * q + c):P * (4 * q + c) + P], ident[:, :])
                ins.then_inc(xT_turned, 1)

            def turn_norm(n, t, q):
                pe.wait_ge(xhat_ready, 4 * n + 2 * t + q + 1)
                turn(xhat, t, q)

            def have_xT(group, i):
                pe.wait_ge(xT_lo_ready, 4 * group + i + 1)

            def ffn(l, call, b, group, n):
                def down_tile(j, t, last):
                    slot = j % RING
                    for half in range(2):
                        for k in range(2):
                            hk = (slice(None), k, slice(t * P, (t + 1) * P))
                            wk = slice(1024 * k + 512 * half, 1024 * k + 512 * half + 512)
                            ins = mm3(ps[:, 2 * t + half, :], hT_hi[last][hk], hT_lo[last][hk], w_hi[:, slot, wk], w_lo[:, slot, wk],
                                      False, bool(last) and k == 1)
                        if last and 2 * t + half < 3:
                            ins.then_inc(acc_done, 1)
                    return ins

                def turn_h(last=0):
                    for k in range(2):
                        for t in range(NT):
                            ins = nc.tensor.transpose(ps[:, 6 + last, 256 * k + P * t:256 * k + P * t + P],
                                                      h[:, t, P * k:P * k + P], ident[:, :])
                    ins.then_inc(hT_turned, 1)

                def block(i):
                    tok_block(l, b + 2, 0, 4, lambda t: pe.wait_ge(h_ready, 2 * NB * call + 2 * i + t - 1), gu0_done, i - 1)
                    turn_h()
                    tok_block(l, b + 3, 1, 4, lambda t: None, gu0_done, i - 1)
                    pe.wait_ge(hT_lo_ready, NB * call + i)
                    begin(l, b + 4, i - 1)
                    down_tile(b + 4, 0, 0)

                def clear_acc():
                    pe.wait_ge(x_ready, 2 * n + 2)
                    for bank in range(4):
                        nc.tensor.matmul(ps[:, bank, :], zeros16[:, 0:P], zeros16[:, :], start=True, stop=True)

                turn_norm(n, 0, 0)
                turn_norm(n, 0, 1)
                clear_acc()
                turn_norm(n, 1, 0)
                turn_norm(n, 1, 1)
                tok_block(l, b, 0, 4, lambda t: have_xT(group, 2 * t), gu0_done)
                tok_block(l, b + 1, 1, 4, lambda t: have_xT(group, 2 * t + 1), gu0_done)
                with pe.Fori(1, NB - 1, 1) as i:
                    block(i)
                    down_tile(b + 4, 1, 0).then_inc(unit_done, 1)
                block(NB - 1)
                pe.wait_ge(h_ready, 2 * NB * call + 2 * NB)
                turn_h(1)
                down_tile(b + 4, 1, 0).then_inc(unit_done, 1)
                pe.wait_ge(hT_lo_ready, NB * call + NB)
                begin(l, b + FFN_UNITS - 1)
                down_tile(b + FFN_UNITS - 1, 0, 1)
                down_tile(b + FFN_UNITS - 1, 1, 1).then_inc(unit_done, 1)

            pe.wait_ge(const_ready, 1)
            with pe.Fori(0, DEPTH, 1) as l:
                ffn(l, 2 * l, 0, 4 * l, 3 * l)
                for t in range(NT):
                    for q in range(2):
                        turn_norm(3 * l + 1, t, q)

                def feature_block(j, half, bank, turns):
                    begin(l, j, turns)
                    slot = j % RING
                    for c in range(4):
                        for k in range(4):
                            kk = 4 * half + k
                            wk = slice(512 * k + P * c, 512 * k + P * c + P)
                            ins = mm3(ps[:, bank + c // 2, 256 * (c % 2):256 * (c % 2) + 256], xT_hi[:, kk, :], xT_lo[:, kk, :],
                                      w_hi[:, slot, wk], w_lo[:, slot, wk], half == 0 and k == 0 and c % 2 == 0,
                                      half == 1 and k == 3, feature_major=True)
                    ins.then_inc(unit_done, 1)

                for half in range(2):
                    j = U_SMALL + half
                    have_xT(4 * l + 1, 2 + half)
                    begin(l, j)
                    for k in range(4):
                        wk = slice(SMALL * k, SMALL * k + SMALL)
                        ins = mm3(ps[0:SMALL, 4, 0:S], xT_hi[:, 4 * half + k, :], xT_lo[:, 4 * half + k, :],
                                  w_hi[:, j % RING, wk], w_lo[:, j % RING, wk], half == 0 and k == 0, half == 1 and k == 3,
                                  feature_major=True)
                    ins.then_inc(unit_done, 1)

                pe.wait_ge(par_loaded, 16 * 8 * (l + 1))
                for g in range(4):
                    nc.tensor.transpose(ps[:, 6, P * g:P * g + P], spat_in[:, g, :], ident[:, :])
                nc.tensor.transpose(ps[:, 7, 0:PROWS], prow, ident[0:PROWS, 0:PROWS]).then_inc(par_turned, 1)
                pe.wait_ge(diag_ready, l + 1)
                pe.wait_ge(ones_ready, 1)
                nc.tensor.matmul(ps[:, 5, 0:S], ones[:, :], diag.rearrange("p t n -> p (t n)"), start=True, stop=True).then_inc(rstd_row_done, 1)

                with pe.Fori(0, 3, 1) as g:
                    for c in range(4):
                        if c % 2 == 0:
                            pe.wait_ge(feat_evac, 6 * l + 2 * g + c // 2 + 1)
                        feature_block(U_WI + c, c % 2, c - c % 2, 2 * g)
                    pe.wait_ge(tok_evac, 3 * l + g + 1)
                    pe.wait_ge(z_ready, l + 1)
                    pe.wait_ge(rstd_row_ready, l + 1)
                    tok_block(l, U_WI + 4, 0, 4, lambda t: None, gate0_done, 2 * g)
                    begin(l, U_WI + 5, 2 * g)
                    slot = (U_WI + 5) % RING
                    for t in range(NT):
                        for k in range(4):
                            xk = (slice(None), 4 + k, slice(t * P, (t + 1) * P))
                            wk = slice(512 * k, 512 * k + 512)
                            ins = mm3(ps[:, 4 + t, :], xT_hi[xk], xT_lo[xk], w_hi[:, slot, wk], w_lo[:, slot, wk], False, k == 3)
                    ins.then_inc(unit_done, 1)

                mm = nc.tensor.matmul

                def spatial():
                    pe.wait_ge(wsT_ready, l + 1)
                    pe.wait_ge(vhat_ready, l + 1)
                    for g4 in range(4):
                        for c in range(2):
                            ins = mm(ps[:, 6 + g4 // 2, 256 * (g4 % 2) + P * c:256 * (g4 % 2) + P * c + P],
                                     gm_v[:, c, P * g4:P * g4 + P],
                                     wsT[:, g4, :], start=True, stop=True)
                    ins.then_inc(spatial_done, 1)

                def decay():
                    pe.wait_ge(rows_ready, l + 1)
                    pe.wait_ge(masks_ready, 1)
                    pe.wait_ge(wsT_copied, l + 1)
                    pe.wait_ge(feat_evac, 6 * l + 8)
                    for c in range(2):
                        bank = ps[:, 6 + c, :]
                        mm(bank, g_parts[:, P * c:P * c + P], head_sel[:, 0:MH, :].rearrange("p h t -> p (h t)"),
                           start=True, stop=False, skip_group_check=True)
                        for hd in range(MH):
                            mm(ps[:, 6 + c, P * hd:P * hd + P], head_sel[:, hd, :], m_parts[:, P * c:P * c + P],
                               start=False, stop=False, skip_group_check=True)
                            ins = mm(ps[:, 6 + c, P * hd:P * hd + P], ident16[:, :], mask_k[:, :],
                                     start=False, stop=True, skip_group_check=True)
                    ins.then_inc(decay_done, 1)
                    pe.wait_ge(rexp_ready, l + 1)
                    for k in range(4):
                        ins = mm(ps[:, 0, MH * k:MH * k + MH], r_row[0:MH, P * k:P * k + P], ident[0:MH, 0:MH], start=True, stop=True)
                    ins.then_inc(rT_done, 1)

                def key_query():
                    pe.wait_ge(mlqk_ready, l + 1)
                    pe.wait_ge(rT_ready, l + 1)
                    pe.wait_ge(w_intra_ready, l + 1)
                    for hd in range(MH):
                        ins = nc.tensor.transpose(ps[:, 1, P * hd:P * hd + P], mlqk[:, MH + hd, 0:P], ident[:, :])
                    ins.then_inc(k_turned, 1)
                    for c, bank in ((0, 0), (1, 6)):
                        for hd in range(MH):
                            ins = mm(ps[:, bank, P * hd:P * hd + P], mlqk[:, MH + hd, P * c:P * c + P],
                                     mlqk[:, hd, P * c:P * c + P], start=True, stop=True)
                    ins.then_inc(kq_done, 1)

                def state_intra():
                    pe.wait_ge(k_tok_ready, l + 1)
                    pe.wait_ge(v_w_ready, l + 1)
                    for hd in range(MH):
                        sl = slice(P * hd, P * hd + P)
                        mm(ps[:, 1, sl], k_tok[:, sl], v_w[:, sl], start=True, stop=True)
                        ins = mm(ps[:, 7, hd:hd + 1], k_tok[:, sl], tok16[:, 3, hd:hd + 1], start=True, stop=True)
                    ins.then_inc(state_done, 1)
                    pe.wait_ge(qk_ready, l + 1)
                    for c, bank in ((0, 0), (1, 6)):
                        for hd in range(MH):
                            sl = slice(P * hd, P * hd + P)
                            mm(ps[:, bank, sl], w_intra[:, c, sl], ml_v[:, c, sl], start=True, stop=True)

                def denominators():
                    pe.wait_ge(n_state_ready, l + 1)
                    for c in range(2):
                        for hd in range(MH):
                            mm(ps[:, 7, 8 + 4 * c + hd:9 + 4 * c + hd], w_intra[:, c, P * hd:P * hd + P], ones[:, 0:1],
                               start=True, stop=True)

                def inter():
                    pe.wait_ge(c_state_ready, l + 1)
                    for hd in range(MH):
                        mm(ps[:, 1, P * hd:P * hd + P], mlqk[:, hd, P:S], c_state[:, P * hd:P * hd + P], start=True, stop=True)
                        ins = mm(ps[:, 7, 16 + hd:17 + hd], mlqk[:, hd, P:S], n_state[:, hd:hd + 1], start=True, stop=True)
                    ins.then_inc(inter_done, 1)

                def turn_heads():
                    pe.wait_ge(hn_ready, l + 1)
                    for hd in range(MH):
                        for c in range(2):
                            ins = nc.tensor.transpose(ps[:, hd // 2, 256 * (hd % 2) + P * c:256 * (hd % 2) + P * c + P],
                                                      hm[:, c, P * hd:P * hd + P], ident[:, :])
                    ins.then_inc(ml_turned, 1)

                def score(p):
                    if p == 0:
                        pe.wait_ge(negc_ready, l + 1)
                    if p:
                        pe.wait_ge(y_tok_ready, 4 * l + p)
                    for e in range(2):
                        for t in range(NT):
                            dst = ps[:, 2 + e, 0:256] if t else ps[:, 2 + e, 256:384]
                            keys = P * (t + 1)
                            hp = slice(DH * e, DH * e + DH)
                            mm(dst, qT[hp, p, P * t:P * t + P], kT[hp, p, 0:keys], start=True, stop=False, skip_group_check=True)
                            mm(dst, head_sel[:, 2 * p + e, :], c_parts[:, 0:keys], start=False, stop=False, skip_group_check=True)
                            ins = mm(dst[:, keys - P:keys], ident16[:, :], mask_q[:, :], start=False, stop=True, skip_group_check=True)
                    ins.then_inc(score_done, 1)

                def turn_p(p):
                    pe.wait_ge(prob_ready, 16 * l + 4 * p + 4)
                    for e in range(2):
                        for i in range(3):
                            ins = nc.tensor.transpose(ps[:, 2 + e, P * i:P * i + P], prob[:, 512 * e + P * i:512 * e + P * i + P], ident[:, :])
                    ins.then_inc(p_turned, 1)

                def pv(p):
                    pe.wait_ge(probT_ready, 4 * l + p + 1)
                    for e in range(2):
                        hd = 2 * p + e
                        v = lambda c: att_v[:, c, DH * hd:DH * hd + DH]
                        pt = lambda i: probT[:, 512 * e + P * i:512 * e + P * i + P]
                        mm(ps[:, 2 + e, 384:384 + DH], pt(2), v(0), start=True, stop=True)
                        mm(ps[:, 2 + e, 384 + DH:512], pt(0), v(0), start=True, stop=False)
                        ins = mm(ps[:, 2 + e, 384 + DH:512], pt(1), v(1), start=False, stop=True)
                    ins.then_inc(pv_done, 1)

                def turn_y():
                    pe.wait_ge(y_tok_ready, 4 * l + 4)
                    for c in range(4):
                        for t in range(NT):
                            ins = nc.tensor.transpose(ps[:, 2 + c // 2, 256 * (c % 2) + P * t:256 * (c % 2) + P * t + P],
                                                      y_tok[:, t, P * c:P * c + P], ident[:, :])
                    ins.then_inc(y_turned, 1)

                work = {20: [lambda: score(0), key_query], 21: [lambda: turn_p(0), state_intra],
                        22: [lambda: pv(0), denominators], 23: [lambda: score(1), inter], 24: [lambda: turn_p(1)],
                        25: [lambda: pv(1)], 26: [lambda: score(2), turn_heads, spatial], 27: [lambda: turn_p(2)],
                        28: [lambda: pv(2)],
                        29: [lambda: score(3)], 30: [lambda: turn_p(3)], 31: [lambda: pv(3)], 33: [turn_y]}
                decay()
                for b in range(NGATE):
                    for half in range(2):
                        def wait_tile(t):
                            if half == 0 and b == 0:
                                if t == 0:
                                    pe.wait_ge(tok_evac, 3 * l + 4)
                            elif half == 0:
                                pe.wait_ge(gate_evac, 12 * l + 2 * (b - 1) + t + 1)
                        tok_block(l, U_GATE + 2 * b + half, half, 4, wait_tile, gate0_done)
                        for f in work.get(U_GATE + 2 * b + half - U_SMALL, []):
                            f()

                for r, ready in enumerate((gm_lo_ready, ml_lo_ready, att_lo_ready)):
                    pe.wait_ge(ready, l + 1)
                    if r == 0:
                        pe.wait_ge(gate_evac, 12 * (l + 1))
                        pe.wait_ge(ml_y_ready, l + 1)
                    for a in range(2):
                        j = U_BR + 2 * r + a
                        begin(l, j)
                        for o in range(4):
                            t, half = o // 2, o % 2
                            if r and a == 0:
                                pe.wait_ge(br_evac, 12 * l + 4 * (r - 1) + o + 1)
                            for k in range(2):
                                yk = (slice(None), 2 - r, 2 * a + k, slice(t * P, (t + 1) * P))
                                wk = slice(1024 * k + 512 * half, 1024 * k + 512 * half + 512)
                                ins = mm3(ps[:, 4 + o, :], yT_hi[yk], yT_lo[yk], w_hi[:, j % RING, wk], w_lo[:, j % RING, wk],
                                          a == 0 and k == 0, a == 1 and k == 1)
                            if a == 1 and o < 3:
                                ins.then_inc(br_done, 1)
                        ins.then_inc(unit_done, 1)
                        for f in work.get(j - U_SMALL, []):
                            f()

                for t in range(NT):
                    for q in range(2):
                        pe.wait_ge(merged_ready, 4 * l + 2 * t + q + 1)
                        turn(merged, t, q, MERGED_BANKS)
                for a in range(4):
                    j = U_OUT + a
                    begin(l, j)
                    for t in range(NT):
                        have_xT(4 * l + 2, 2 * t + (a // 2))
                        for half in range(2):
                            for k in range(2):
                                xk = (slice(None), 2 * a + k, slice(t * P, (t + 1) * P))
                                wk = slice(1024 * k + 512 * half, 1024 * k + 512 * half + 512)
                                ins = mm3(ps[:, 2 * t + half, :], xT_hi[xk], xT_lo[xk], w_hi[:, j % RING, wk], w_lo[:, j % RING, wk],
                                          a == 0 and k == 0, a == 3 and k == 1)
                            if a == 3 and 2 * t + half < 3:
                                ins.then_inc(acc_done, 1)
                    ins.then_inc(unit_done, 1)
                ffn(l, 2 * l + 1, U_FFN2, 4 * l + 3, 3 * l + 2)


_INS = ['x', 'norm_ffn1', 'ffn1_gate', 'ffn1_up', 'ffn1_down', 'norm_mix', 'w_in', 'b_f_att', 'b_i_ml', 'b_f_ml',
        'conv_ml', 'norm_ml_head', 'norm_gmlp', 'w_spatial', 'b_spatial', 'w_br_att', 'w_br_ml', 'w_br_gmlp',
        'w_out', 'norm_ffn2', 'ffn2_gate', 'ffn2_up', 'ffn2_down', 'norm_final']


def kernel(**inputs):
    import numpy as _np
    import concourse.bacc as _bacc
    from concourse import mybir as _mybir
    from concourse.bass_utils import run_bass_kernel_spmd as _run

    nc = _bacc.Bacc("TRN2", target_bir_lowering=False, num_devices=1, dynamic_dma_scratch_size=1024)
    arrays, args = {}, []
    for name in _INS:
        a = _np.ascontiguousarray(inputs[name])
        arrays[f"in_{name}_dram"] = a
        args.append(nc.dram_tensor(f"in_{name}_dram", a.shape, _mybir.dt.from_np(a.dtype), kind="ExternalInput").ap())
    shape = inputs["x"].shape
    args.append(nc.dram_tensor("out_0_dram", shape, _mybir.dt.float32, kind="ExternalOutput").ap())
    trunk(nc, *args)
    r = _run(nc, [arrays], core_ids=[0])
    return r.results[0]["out_0_dram"]
```
